# Optimizing a Trainium2 kernel written in Bass

```python
import math
import jax
import jax.numpy as jnp
from jax import lax
import numpy as np
import jax, jax.numpy as jnp

D_MODEL = 1024
BATCH = 1
SEQ = 256
DEPTH = 2

D_MIX = D_MODEL
HEAD_DIM = 64
RWKV_WIDTH = D_MIX // 2
RWKV_HEADS = RWKV_WIDTH // HEAD_DIM
MOBA_WIDTH = D_MIX - RWKV_WIDTH
MOBA_HEADS = MOBA_WIDTH // HEAD_DIM
DECAY_LORA = 64
ICLR_LORA = 64
GATE_LORA = 128
RWKV_PROJ = 3 * RWKV_WIDTH + DECAY_LORA + ICLR_LORA + GATE_LORA
MOBA_PROJ = 3 * MOBA_WIDTH
D_PROJ = RWKV_PROJ + MOBA_PROJ
LNX_EPS = 64e-5
MOBA_BLOCK = 256
MOBA_TOPK = 3
MOBA_Q_CHUNK = 16
REL_BUCKETS = 32
REL_MAX_DISTANCE = 1024
MEM_LEN = 256
XATTN_HEADS = 4
XATTN_HEAD_DIM = D_MODEL // XATTN_HEADS
D_FF = ((8 * D_MODEL // 3 + 127) // 128) * 128
FFN_RES_WEIGHT = 0.5
NORM_EPS = 1e-6


def rms_norm(x, g):
    xf = x.astype(jnp.float32)
    y = xf * lax.rsqrt(jnp.mean(xf * xf, axis=-1, keepdims=True) + NORM_EPS)
    return (y * g.astype(jnp.float32)).astype(x.dtype)

def swiglu_ffn(h, w_in, w_out):
    gate, up = jnp.split(h @ w_in, 2, axis=-1)
    return (jax.nn.silu(gate) * up) @ w_out

def token_shift(z):
    return jnp.pad(z, ((0, 0), (1, 0), (0, 0)))[:, :-1]

def rel_bucket(dist):
    n = jnp.maximum(dist, 0)
    max_exact = REL_BUCKETS // 2
    nf = jnp.maximum(n, 1).astype(jnp.float32)
    large = max_exact + (jnp.log(nf / max_exact) / math.log(REL_MAX_DISTANCE / max_exact)
                         * (REL_BUCKETS - max_exact)).astype(jnp.int32)
    large = jnp.minimum(large, REL_BUCKETS - 1)
    return jnp.where(n < max_exact, n, large)

def rwkv7_time_mix(p, mu, w0, w_up, a0, a_up, g_up, k_k, k_a, r_k, ln_g, ln_b):
    B, S, _ = p.shape
    H, Dh, W = RWKV_HEADS, HEAD_DIM, RWKV_WIDTH
    dt = p.dtype
    f32 = jnp.float32
    p = p + (token_shift(p) - p) * mu
    r, k, v, w_lo, a_lo, g_lo = jnp.split(
        p, [W, 2 * W, 3 * W, 3 * W + DECAY_LORA, 3 * W + DECAY_LORA + ICLR_LORA], axis=-1)
    w_log = -jax.nn.softplus(-(w0 + jnp.tanh(w_lo) @ w_up).astype(f32)) - 0.5
    decay = jnp.exp(-jnp.exp(w_log))
    a = jax.nn.sigmoid(a0 + a_lo @ a_up)
    g = jax.nn.sigmoid(g_lo) @ g_up
    kk = k * k_k
    k = k * (1 + (a - 1) * k_a)
    heads = lambda z: z.reshape(B, S, H, Dh).astype(f32)
    r, k, v, a, decay, kk = (heads(z) for z in (r, k, v, a, decay, kk))
    kk = kk / jnp.maximum(jnp.sqrt(jnp.sum(kk * kk, axis=-1, keepdims=True)), 1e-12)
    b = kk * a

    def step(state, inp):
        r_t, w_t, k_t, v_t, kk_t, b_t = inp
        sa = jnp.einsum('bhij,bhj->bhi', state, -kk_t)
        state = (state * w_t[:, :, None, :] + sa[..., None] * b_t[:, :, None, :]
                 + v_t[..., None] * k_t[:, :, None, :])
        return state, jnp.einsum('bhij,bhj->bhi', state, r_t)

    tm = lambda z: jnp.swapaxes(z, 0, 1)
    state0 = jnp.zeros((B, H, Dh, Dh), f32)
    _, y = lax.scan(step, state0, tuple(tm(z) for z in (r, decay, k, v, kk, b)))
    y = tm(y)
    mean = jnp.mean(y, axis=-1, keepdims=True)
    var = jnp.mean(jnp.square(y - mean), axis=-1, keepdims=True)
    y = ((y - mean) * lax.rsqrt(var + LNX_EPS)).reshape(B, S, W) * ln_g + ln_b
    bonus = jnp.sum(r * k * r_k, axis=-1, keepdims=True) * v
    y = y + bonus.reshape(B, S, W)
    return (y * g).astype(dt)

def moba_attention(q, k, v, rel_bias):
    B, S, _ = q.shape
    H, Dh, BLK, QC = MOBA_HEADS, HEAD_DIM, MOBA_BLOCK, MOBA_Q_CHUNK
    f32 = jnp.float32
    nb = -(-S // BLK)
    pad = nb * BLK - S
    to_heads = lambda z: z.reshape(B, S, H, Dh).transpose(0, 2, 1, 3)
    q = to_heads(q) * (Dh ** -0.5)
    k = jnp.pad(to_heads(k), ((0, 0), (0, 0), (0, pad), (0, 0)))
    v = jnp.pad(to_heads(v), ((0, 0), (0, 0), (0, pad), (0, 0)))
    kb = k.reshape(B, H, nb, BLK, Dh)
    vb = v.reshape(B, H, nb, BLK, Dh)
    k_mean = jnp.mean(kb.astype(f32), axis=3).astype(q.dtype)
    topk = min(MOBA_TOPK, nb)
    n_chunks = S // QC
    qc = q.reshape(B, H, n_chunks, QC, Dh).transpose(2, 0, 1, 3, 4)
    b_ix = jnp.arange(B)[:, None, None, None]
    h_ix = jnp.arange(H)[None, :, None, None]
    blk_ar = jnp.arange(BLK)

    def chunk_fn(args):
        q_c, c = args
        q_start = c * QC
        q_pos = q_start + jnp.arange(QC)
        q_blk = q_start // BLK
        gate = jnp.einsum('bhqd,bhnd->bhqn', q_c, k_mean)
        gate = jnp.where(jnp.arange(nb) < q_blk, gate, -jnp.inf)
        _, idx = lax.top_k(gate, topk)
        valid = idx < q_blk
        k_sel = kb[b_ix, h_ix, idx]
        v_sel = vb[b_ix, h_ix, idx]
        k_pos_sel = idx[..., None] * BLK + blk_ar
        bias_sel = rel_bias[h_ix[..., None], rel_bucket(q_pos[None, None, :, None, None] - k_pos_sel)]
        s_sel = jnp.einsum('bhqd,bhqtkd->bhqtk', q_c, k_sel).astype(f32) + bias_sel.astype(f32)
        s_sel = jnp.where(valid[..., None], s_sel, -jnp.inf)
        k_own = lax.dynamic_index_in_dim(kb, q_blk, axis=2, keepdims=False)
        v_own = lax.dynamic_index_in_dim(vb, q_blk, axis=2, keepdims=False)
        own_pos = q_blk * BLK + blk_ar
        bias_own = rel_bias[:, rel_bucket(q_pos[:, None] - own_pos[None, :])]
        s_own = jnp.einsum('bhqd,bhkd->bhqk', q_c, k_own).astype(f32) + bias_own.astype(f32)[None]
        s_own = jnp.where(own_pos[None, :] <= q_pos[:, None], s_own, -jnp.inf)
        logits = jnp.concatenate([s_sel.reshape(B, H, QC, topk * BLK), s_own], axis=-1)
        probs = jax.nn.softmax(logits, axis=-1).astype(v.dtype)
        p_sel = probs[..., :topk * BLK].reshape(B, H, QC, topk, BLK)
        p_own = probs[..., topk * BLK:]
        return (jnp.einsum('bhqtk,bhqtkd->bhqd', p_sel, v_sel)
                + jnp.einsum('bhqk,bhkd->bhqd', p_own, v_own))

    out = lax.map(chunk_fn, (qc, jnp.arange(n_chunks)))
    return out.transpose(1, 0, 3, 2, 4).reshape(B, S, H * Dh)

def memory_cross_attention(h, mem_n, w_q, w_kv, w_o):
    B, S, D = h.shape
    M = mem_n.shape[1]
    q = (h @ w_q).reshape(B, S, XATTN_HEADS, XATTN_HEAD_DIM)
    k, v = jnp.split(mem_n @ w_kv, 2, axis=-1)
    k = k.reshape(B, M, XATTN_HEADS, XATTN_HEAD_DIM)
    v = v.reshape(B, M, XATTN_HEADS, XATTN_HEAD_DIM)
    logits = jnp.einsum('bshd,bmhd->bhsm', q, k).astype(jnp.float32) * (XATTN_HEAD_DIM ** -0.5)
    probs = jax.nn.softmax(logits, axis=-1).astype(v.dtype)
    o = jnp.einsum('bhsm,bmhd->bshd', probs, v).reshape(B, S, D)
    return o @ w_o

def first_inputs(seed: int = 0) -> dict:
    key = jax.random.key(seed)
    ks = iter(jax.random.split(key, 40))
    f32 = jnp.float32

    def nrm(shape, scale):
        return scale * jax.random.normal(next(ks), shape, f32)

    def dense(fan_in, fan_out):
        return nrm((DEPTH, fan_in, fan_out), fan_in ** -0.5)

    def gain(n):
        return 1.0 + nrm((DEPTH, n), 0.02)

    W = RWKV_WIDTH
    return {
        "x": nrm((BATCH, SEQ, D_MODEL), 1.0),
        "mem": nrm((BATCH, MEM_LEN, D_MODEL), 1.0),
        "rel_bias": nrm((MOBA_HEADS, REL_BUCKETS), 0.5),
        "final_norm_g": 1.0 + nrm((D_MODEL,), 0.02),
        "ffn1_norm_g": gain(D_MODEL),
        "ffn1_w_in": dense(D_MODEL, 2 * D_FF),
        "ffn1_w_out": dense(D_FF, D_MODEL),
        "mix_norm_g": gain(D_MODEL),
        "w_mix_in": dense(D_MODEL, D_PROJ),
        "w_mix_out": dense(D_MIX, D_MODEL),
        "rwkv_mu": jax.random.uniform(next(ks), (DEPTH, RWKV_PROJ), f32),
        "rwkv_w0": jnp.linspace(-6.0, -1.0, W, dtype=f32)[None, :] + nrm((DEPTH, W), 0.1),
        "rwkv_w_up": nrm((DEPTH, DECAY_LORA, W), 0.5 * DECAY_LORA ** -0.5),
        "rwkv_a0": nrm((DEPTH, W), 0.1),
        "rwkv_a_up": dense(ICLR_LORA, W),
        "rwkv_g_up": dense(GATE_LORA, W),
        "rwkv_k_k": 0.85 + nrm((DEPTH, W), 0.02),
        "rwkv_k_a": 1.0 + nrm((DEPTH, W), 0.02),
        "rwkv_r_k": nrm((DEPTH, RWKV_HEADS, HEAD_DIM), 0.1),
        "rwkv_ln_g": gain(W),
        "rwkv_ln_b": nrm((DEPTH, W), 0.02),
        "xattn_norm_g": gain(D_MODEL),
        "mem_norm_g": gain(D_MODEL),
        "xattn_w_q": dense(D_MODEL, D_MODEL),
        "xattn_w_kv": dense(D_MODEL, 2 * D_MODEL),
        "xattn_w_o": dense(D_MODEL, D_MODEL),
        "ffn2_norm_g": gain(D_MODEL),
        "ffn2_w_in": dense(D_MODEL, 2 * D_FF),
        "ffn2_w_out": dense(D_FF, D_MODEL),
    }

def first_block(x, mem, rel_bias, final_norm_g, ffn1_norm_g, ffn1_w_in, ffn1_w_out, mix_norm_g,
              w_mix_in, w_mix_out, rwkv_mu, rwkv_w0, rwkv_w_up, rwkv_a0, rwkv_a_up, rwkv_g_up,
              rwkv_k_k, rwkv_k_a, rwkv_r_k, rwkv_ln_g, rwkv_ln_b, xattn_norm_g, mem_norm_g,
              xattn_w_q, xattn_w_kv, xattn_w_o, ffn2_norm_g, ffn2_w_in, ffn2_w_out):
    for l in range(DEPTH):
        x = x + FFN_RES_WEIGHT * swiglu_ffn(rms_norm(x, ffn1_norm_g[l]), ffn1_w_in[l], ffn1_w_out[l])
        proj = rms_norm(x, mix_norm_g[l]) @ w_mix_in[l]
        p_rwkv = proj[..., :RWKV_PROJ]
        q_m, k_m, v_m = jnp.split(proj[..., RWKV_PROJ:], 3, axis=-1)
        y_rwkv = rwkv7_time_mix(p_rwkv, rwkv_mu[l], rwkv_w0[l], rwkv_w_up[l], rwkv_a0[l],
                                rwkv_a_up[l], rwkv_g_up[l], rwkv_k_k[l], rwkv_k_a[l], rwkv_r_k[l],
                                rwkv_ln_g[l], rwkv_ln_b[l])
        y_moba = moba_attention(q_m, k_m, v_m, rel_bias)
        x = x + jnp.concatenate([y_rwkv, y_moba], axis=-1) @ w_mix_out[l]
        x = x + memory_cross_attention(rms_norm(x, xattn_norm_g[l]), rms_norm(mem, mem_norm_g[l]),
                                       xattn_w_q[l], xattn_w_kv[l], xattn_w_o[l])
        x = x + FFN_RES_WEIGHT * swiglu_ffn(rms_norm(x, ffn2_norm_g[l]), ffn2_w_in[l], ffn2_w_out[l])
    return rms_norm(x, final_norm_g)


GRID_W = 64
CTX_LEN = 256
Q_BLOCK = 128
ROPE_THETA = 10000.0

GQA_HEADS = 6
GQA_KV_HEADS = 2
GQA_GROUP = GQA_HEADS // GQA_KV_HEADS
MLA_HEADS = 6
MLA_NOPE = 64
MLA_ROPE = 32
MLA_QK = MLA_NOPE + MLA_ROPE
MLA_V = 64
MLA_Q_RANK = 256
MLA_KV_RANK = 128
POOL_WINDOWS = (2, 4, 8, 16)
POOL_GROUPS = len(POOL_WINDOWS)
POOL_GROUP_DIM = 64
POOL_WIDTH = POOL_GROUPS * POOL_GROUP_DIM

MIX_WIDTH = GQA_HEADS * HEAD_DIM + MLA_HEADS * MLA_V + POOL_WIDTH
IN_SIZES = (GQA_HEADS * HEAD_DIM, GQA_KV_HEADS * HEAD_DIM, GQA_KV_HEADS * HEAD_DIM,
            MLA_Q_RANK, MLA_KV_RANK, MLA_ROPE, POOL_WIDTH)
IN_WIDTH = sum(IN_SIZES)
D_FF_2 = 4 * D_MODEL
N_MOD = 6


def rms_norm_2(x, g):
    xf = x.astype(jnp.float32)
    y = xf * lax.rsqrt(jnp.mean(xf * xf, axis=-1, keepdims=True) + NORM_EPS)
    return (y * g.astype(jnp.float32)).astype(x.dtype)

def modulate(h, shift, scale):
    return h * (1.0 + scale) + shift

def axial_rope_tables(length, rot_dim):
    rows = length // GRID_W
    row = jnp.repeat(jnp.arange(rows, dtype=jnp.float32), GRID_W)
    col = jnp.tile(jnp.arange(GRID_W, dtype=jnp.float32), rows)
    n = rot_dim // 4
    inv = ROPE_THETA ** (-jnp.arange(n, dtype=jnp.float32) / n)
    ang = jnp.concatenate([row[:, None] * inv, col[:, None] * inv], axis=-1)
    return jnp.cos(ang)[:, None, :], jnp.sin(ang)[:, None, :]

def apply_rope(x, cos, sin):
    half = x.shape[-1] // 2
    xf = x.astype(jnp.float32)
    x1, x2 = xf[..., :half], xf[..., half:]
    return jnp.concatenate([x1 * cos - x2 * sin, x1 * sin + x2 * cos], axis=-1).astype(x.dtype)

def attention(q, k, v, scale):
    b, hk, g, lq, dk = q.shape
    nb = lq // Q_BLOCK
    qb = jnp.moveaxis(q.reshape(b, hk, g, nb, Q_BLOCK, dk), 3, 0)

    def one_block(qi):
        s = jnp.einsum('bhgqd,bhkd->bhgqk', qi, k, preferred_element_type=jnp.float32) * scale
        p = jax.nn.softmax(s, axis=-1)
        return jnp.einsum('bhgqk,bhkd->bhgqd', p.astype(v.dtype), v)

    ob = lax.map(one_block, qb)
    return jnp.moveaxis(ob, 0, 3).reshape(b, hk, g, lq, v.shape[-1])

def merge_heads(o):
    b, hk, g, l, d = o.shape
    return o.transpose(0, 3, 1, 2, 4).reshape(b, l, hk * g * d)

def mixer_inputs(h, w_in, g_q_gqa, g_k_gqa, g_cq, g_ckv, w_uq, w_ukv, g_q_mla, g_k_mla, rope):
    b, l, _ = h.shape
    u = h @ w_in
    offs = np.cumsum(IN_SIZES)[:-1].tolist()
    u_q, u_k, u_v, u_cq, u_ckv, u_kr, pool_in = jnp.split(u, offs, axis=-1)
    qg = rms_norm_2(u_q.reshape(b, l, GQA_HEADS, HEAD_DIM), g_q_gqa)
    kg = rms_norm_2(u_k.reshape(b, l, GQA_KV_HEADS, HEAD_DIM), g_k_gqa)
    vg = u_v.reshape(b, l, GQA_KV_HEADS, HEAD_DIM)
    qm = (rms_norm_2(u_cq, g_cq) @ w_uq).reshape(b, l, MLA_HEADS, MLA_QK)
    kv = (rms_norm_2(u_ckv, g_ckv) @ w_ukv).reshape(b, l, MLA_HEADS, MLA_NOPE + MLA_V)
    k_rope = jnp.broadcast_to(u_kr[:, :, None, :], (b, l, MLA_HEADS, MLA_ROPE))
    km = jnp.concatenate([kv[..., :MLA_NOPE], k_rope], axis=-1)
    vm = kv[..., MLA_NOPE:]
    qm = rms_norm_2(qm, g_q_mla)
    km = rms_norm_2(km, g_k_mla)
    if rope is not None:
        cos_g, sin_g, cos_m, sin_m = rope
        qg = apply_rope(qg, cos_g, sin_g)
        kg = apply_rope(kg, cos_g, sin_g)
        qm = jnp.concatenate([qm[..., :MLA_NOPE], apply_rope(qm[..., MLA_NOPE:], cos_m, sin_m)], axis=-1)
        km = jnp.concatenate([km[..., :MLA_NOPE], apply_rope(km[..., MLA_NOPE:], cos_m, sin_m)], axis=-1)
    qg = qg.reshape(b, l, GQA_KV_HEADS, GQA_GROUP, HEAD_DIM).transpose(0, 2, 3, 1, 4)
    kg = kg.transpose(0, 2, 1, 3)
    vg = vg.transpose(0, 2, 1, 3)
    qm = qm.transpose(0, 2, 1, 3)[:, :, None]
    km = km.transpose(0, 2, 1, 3)
    vm = vm.transpose(0, 2, 1, 3)
    return qg, kg, vg, qm, km, vm, pool_in

def multiscale_pool(u, w_pool, ls_pool):
    b, l, _ = u.shape
    uf = u.astype(jnp.float32)
    cs = jnp.concatenate([jnp.zeros((b, 1, POOL_WIDTH), jnp.float32), jnp.cumsum(uf, axis=1)], axis=1)
    t = jnp.arange(l)
    outs = []
    for gi, w in enumerate(POOL_WINDOWS):
        lo = jnp.maximum(t - w // 2, 0)
        hi = jnp.minimum(t + w // 2, l)
        csg = cs[..., gi * POOL_GROUP_DIM:(gi + 1) * POOL_GROUP_DIM]
        s = jnp.take(csg, hi, axis=1) - jnp.take(csg, lo, axis=1)
        mean = s / (hi - lo).astype(jnp.float32)[None, :, None]
        outs.append(mean - uf[..., gi * POOL_GROUP_DIM:(gi + 1) * POOL_GROUP_DIM])
    y = jnp.stack(outs, axis=2).astype(u.dtype)
    y = jnp.einsum('blgc,gcd->blgd', y, w_pool).reshape(b, l, POOL_WIDTH)
    return y * ls_pool

def token_mix(qg, kg, vg, qm, km, vm, pool_in, w_pool, ls_pool, w_out):
    og = attention(qg, kg, vg, HEAD_DIM ** -0.5)
    om = attention(qm, km, vm, MLA_QK ** -0.5)
    op = multiscale_pool(pool_in, w_pool, ls_pool)
    return jnp.concatenate([merge_heads(og), merge_heads(om), op], axis=-1) @ w_out

def sq_relu_mlp(h, w1, w2):
    return jnp.square(jax.nn.relu(h @ w1)) @ w2

def second_inputs(seed: int = 0) -> dict:
    key = jax.random.key(seed)
    ks = jax.random.split(key, 24)
    f32 = jnp.float32

    def dense(k, shape, fan_in, s=1.0):
        return jax.random.normal(k, shape, f32) * (s * fan_in ** -0.5)

    def gain(k, shape):
        return 1.0 + 0.1 * jax.random.normal(k, shape, f32)

    return {
        "x": jax.random.normal(ks[0], (BATCH, SEQ, D_MODEL), f32),
        "c": jax.random.normal(ks[1], (BATCH, D_MODEL), f32),
        "ctx": jax.random.normal(ks[2], (BATCH, CTX_LEN, D_MODEL), f32),
        "c_ctx": jax.random.normal(ks[3], (D_MODEL,), f32),
        "w_mod": dense(ks[4], (DEPTH, D_MODEL, N_MOD * D_MODEL), D_MODEL, 0.5),
        "b_mod": 0.02 * jax.random.normal(ks[5], (DEPTH, N_MOD * D_MODEL), f32),
        "g_norm1": gain(ks[6], (DEPTH, D_MODEL)),
        "g_norm2": gain(ks[7], (DEPTH, D_MODEL)),
        "w_in": dense(ks[8], (DEPTH, D_MODEL, IN_WIDTH), D_MODEL),
        "g_q_gqa": gain(ks[9], (DEPTH, HEAD_DIM)),
        "g_k_gqa": gain(ks[10], (DEPTH, HEAD_DIM)),
        "g_cq": gain(ks[11], (DEPTH, MLA_Q_RANK)),
        "g_ckv": gain(ks[12], (DEPTH, MLA_KV_RANK)),
        "w_uq": dense(ks[13], (DEPTH, MLA_Q_RANK, MLA_HEADS * MLA_QK), MLA_Q_RANK),
        "w_ukv": dense(ks[14], (DEPTH, MLA_KV_RANK, MLA_HEADS * (MLA_NOPE + MLA_V)), MLA_KV_RANK),
        "g_q_mla": gain(ks[15], (DEPTH, MLA_QK)),
        "g_k_mla": gain(ks[16], (DEPTH, MLA_QK)),
        "w_pool": dense(ks[17], (DEPTH, POOL_GROUPS, POOL_GROUP_DIM, POOL_GROUP_DIM), POOL_GROUP_DIM),
        "ls_pool": gain(ks[18], (DEPTH, POOL_WIDTH)),
        "w_out": dense(ks[19], (DEPTH, MIX_WIDTH, D_MODEL), MIX_WIDTH),
        "w_mlp1": dense(ks[20], (DEPTH, D_MODEL, D_FF_2), D_MODEL),
        "w_mlp2": dense(ks[21], (DEPTH, D_FF_2, D_MODEL), D_FF_2),
    }

def second_block(x, c, ctx, c_ctx, w_mod, b_mod, g_norm1, g_norm2, w_in, g_q_gqa, g_k_gqa, g_cq, g_ckv,
              w_uq, w_ukv, g_q_mla, g_k_mla, w_pool, ls_pool, w_out, w_mlp1, w_mlp2):
    length = x.shape[1]
    cos_g, sin_g = axial_rope_tables(length, HEAD_DIM)
    cos_m, sin_m = axial_rope_tables(length, MLA_ROPE)
    rope = (cos_g.astype(x.dtype), sin_g.astype(x.dtype), cos_m.astype(x.dtype), sin_m.astype(x.dtype))
    x_lat, x_ctx = x, ctx
    for i in range(DEPTH):
        last = i == DEPTH - 1
        mod_lat = (jax.nn.silu(c) @ w_mod[i] + b_mod[i])[:, None, :]
        mod_ctx = (jax.nn.silu(c_ctx) @ w_mod[i] + b_mod[i])[None, None, :]
        sh1, sc1, gt1, sh2, sc2, gt2 = jnp.split(mod_lat, N_MOD, axis=-1)
        csh1, csc1, cgt1, csh2, csc2, cgt2 = jnp.split(mod_ctx, N_MOD, axis=-1)
        layer_w = (w_in[i], g_q_gqa[i], g_k_gqa[i], g_cq[i], g_ckv[i], w_uq[i], w_ukv[i], g_q_mla[i], g_k_mla[i])
        hc = modulate(rms_norm_2(x_ctx, g_norm1[i]), csh1, csc1)
        qg_c, kg_c, vg_c, qm_c, km_c, vm_c, pool_c = mixer_inputs(hc, *layer_w, None)
        h = modulate(rms_norm_2(x_lat, g_norm1[i]), sh1, sc1)
        qg, kg, vg, qm, km, vm, pool_l = mixer_inputs(h, *layer_w, rope)
        mix = token_mix(qg, jnp.concatenate([kg_c, kg], axis=2), jnp.concatenate([vg_c, vg], axis=2),
                        qm, jnp.concatenate([km_c, km], axis=2), jnp.concatenate([vm_c, vm], axis=2),
                        pool_l, w_pool[i], ls_pool[i], w_out[i])
        x_lat = x_lat + gt1 * mix
        x_lat = x_lat + gt2 * sq_relu_mlp(modulate(rms_norm_2(x_lat, g_norm2[i]), sh2, sc2), w_mlp1[i], w_mlp2[i])
        if not last:
            mix_c = token_mix(qg_c, kg_c, vg_c, qm_c, km_c, vm_c, pool_c, w_pool[i], ls_pool[i], w_out[i])
            x_ctx = x_ctx + cgt1 * mix_c
            x_ctx = x_ctx + cgt2 * sq_relu_mlp(modulate(rms_norm_2(x_ctx, g_norm2[i]), csh2, csc2),
                                               w_mlp1[i], w_mlp2[i])
    return x_lat


def setup_inputs(seed=0):
    out = dict(first_inputs(seed))
    for name, value in second_inputs(seed + 1).items():
        if name != "x":
            out[name + "_2"] = value
    return out


def reference(
    x, mem, rel_bias, final_norm_g, ffn1_norm_g, ffn1_w_in, ffn1_w_out, mix_norm_g, w_mix_in,
    w_mix_out, rwkv_mu, rwkv_w0, rwkv_w_up, rwkv_a0, rwkv_a_up, rwkv_g_up, rwkv_k_k, rwkv_k_a,
    rwkv_r_k, rwkv_ln_g, rwkv_ln_b, xattn_norm_g, mem_norm_g, xattn_w_q, xattn_w_kv, xattn_w_o,
    ffn2_norm_g, ffn2_w_in, ffn2_w_out, c_2, ctx_2, c_ctx_2, w_mod_2, b_mod_2, g_norm1_2,
    g_norm2_2, w_in_2, g_q_gqa_2, g_k_gqa_2, g_cq_2, g_ckv_2, w_uq_2, w_ukv_2, g_q_mla_2,
    g_k_mla_2, w_pool_2, ls_pool_2, w_out_2, w_mlp1_2, w_mlp2_2,
):
    x = first_block(
        x, mem, rel_bias, final_norm_g, ffn1_norm_g, ffn1_w_in, ffn1_w_out, mix_norm_g,
        w_mix_in, w_mix_out, rwkv_mu, rwkv_w0, rwkv_w_up, rwkv_a0, rwkv_a_up, rwkv_g_up,
        rwkv_k_k, rwkv_k_a, rwkv_r_k, rwkv_ln_g, rwkv_ln_b, xattn_norm_g, mem_norm_g, xattn_w_q,
        xattn_w_kv, xattn_w_o, ffn2_norm_g, ffn2_w_in, ffn2_w_out,
    )
    return second_block(
        x, c_2, ctx_2, c_ctx_2, w_mod_2, b_mod_2, g_norm1_2, g_norm2_2, w_in_2, g_q_gqa_2,
        g_k_gqa_2, g_cq_2, g_ckv_2, w_uq_2, w_ukv_2, g_q_mla_2, g_k_mla_2, w_pool_2, ls_pool_2,
        w_out_2, w_mlp1_2, w_mlp2_2,
    )


_drawn_inputs = setup_inputs


def setup_inputs(seed=0):
    import zlib

    import numpy as np

    out = dict(_drawn_inputs(seed))
    spreads = {}
    factors = {'final_norm_g': 2.94,
     'ffn1_norm_g': 3.904,
     'rwkv_w_up': 2.903,
     'rwkv_k_k': 7.817,
     'rwkv_k_a': 4.856,
     'rwkv_ln_g': 5.445,
     'rwkv_ln_b': 5.088,
     'xattn_norm_g': 8.0,
     'mem_norm_g': 8.0,
     'ffn2_norm_g': 5.203,
     'ctx_2': 2.995,
     'g_norm1_2': 2.902,
     'g_q_gqa_2': 8.0,
     'g_k_gqa_2': 8.0,
     'g_cq_2': 8.0,
     'g_ckv_2': 7.39,
     'g_q_mla_2': 8.0,
     'g_k_mla_2': 8.0,
     'ls_pool_2': 3.016}
    for name, (base, spread) in spreads.items():
        noise = np.random.default_rng([zlib.crc32(name.encode()), seed]).standard_normal(out[name].shape)
        drawn = base * np.exp(spread * noise) if base else spread * noise
        out[name] = jnp.asarray(drawn.astype(out[name].dtype))
    for name, factor in factors.items():
        out[name] = (out[name] * factor).astype(out[name].dtype)
    return out
```

```python
from contextlib import ExitStack

import numpy as np

import concourse.bass as bass
from concourse import mybir

ALU = mybir.AluOpType
ACT = mybir.ActivationFunctionType
F32 = mybir.dt.float32
AX_X = mybir.AxisListType.X

P = 128
T = 256
D = 1024
KD = D // P
DEPTH = 2
EPS = 1e-6

RING = 6
SLOT = 2048
BLK = 256

HD = 64
RW = 512
NPAIR = RW // P
NH = RW // HD
D_FF = 2816
FFN_STEPS = D_FF // BLK
CH = 64
SUB = 16
LNX_EPS = 64e-5
DECAY = float(np.exp(-0.5))
XH = 4
XD = D // XH

MIX_TILES = 13
MIX_ORDER = [6, 2, 3, 4, 5, 0, 1, 7, 8, 9, 10, 11, 12]
KV_TILES, LIN_TILES = 2 * D // BLK, D // BLK


def first_schedule():
    s = [(kind, i) for i in range(FFN_STEPS) for kind in ("ffn1_gate", "ffn1_up", "ffn1_down")]
    s += [("mix_in", j) for j in MIX_ORDER]
    s += [("kv", j) for j in range(KV_TILES)]
    s += [("mix_out", j) for j in range(LIN_TILES)]
    s += [("xq", j) for j in range(LIN_TILES)]
    s += [("xo", j) for j in range(LIN_TILES)]
    s += [(kind, i) for i in range(FFN_STEPS) for kind in ("ffn2_gate", "ffn2_up", "ffn2_down")]
    return s


FIRST = first_schedule()
FIRST_AT = {name: i for i, name in enumerate(FIRST)}
FIRST_USES = [len(range(s, len(FIRST), RING)) for s in range(RING)]

PARAMS = [("ffn1_norm_g", KD), ("mix_norm_g", KD), ("xattn_norm_g", KD), ("mem_norm_g", KD),
          ("ffn2_norm_g", KD), ("rwkv_mu", 14), ("rwkv_w0", NPAIR), ("rwkv_a0", NPAIR),
          ("rwkv_k_k", NPAIR), ("rwkv_k_a", NPAIR), ("rwkv_r_k", NPAIR), ("rwkv_ln_g", NPAIR),
          ("rwkv_ln_b", NPAIR)]
PARAM_AT = {}
NPAR = 0
for _name, _n in PARAMS:
    PARAM_AT[_name] = NPAR
    NPAR += _n


def constants():
    i = np.arange(P)
    r, c = i[:, None], i[None, :]
    f = lambda m: m.astype(np.float32)
    upper = (r < c) & (r // CH == c // CH)
    blocks = {
        "ident": f(r == c),
        "ones": np.ones((P, P), np.float32),
        "head_ones": f(r // HD == c // HD),
        "flip": f(r + c == P - 1),
        "upper": f(upper),
        "upper_incl": f((r <= c) & (r // CH == c // CH)),
        "upper_sub": f((r < c) & (r // SUB == c // SUB)),
        "lower_sub": f((r > c) & (r // SUB == c // SUB)),
        "lower_off": f((r > c) & (r // CH == c // CH) & (r // SUB != c // SUB)),
    }
    blocks["carry"] = np.tile(f(np.arange(T) % CH != 0), (P, 1))
    return blocks


def rel_bucket_onehot():
    n = np.maximum((T - 1) - np.arange(2 * T), 0)
    buckets, exact, top = 32, 16, 1024
    nf = np.maximum(n, 1).astype(np.float32)
    large = exact + (np.log(nf / np.float32(exact)) / np.float32(np.log(top / exact))
                     * (buckets - exact)).astype(np.int32)
    b = np.where(n < exact, n, np.minimum(large, buckets - 1))
    b = np.where(np.arange(2 * T) > T - 1, buckets, b)
    return (np.arange(buckets + 1)[:, None] == b[None, :]).astype(np.float32)


class Signal:

    def __init__(self, ctx, nc, name, per_layer=0, start=0):
        self.sem = ctx.enter_context(nc.semaphore(name))
        self.name, self.per_layer, self.start, self.n, self.layer0 = name, per_layer, start, 0, 0

    def up(self):
        self.n += 1
        return self.sem, 1

    def at(self, l, n):
        return self.sem, l * self.per_layer + (n + self.start)

    def now(self, l):
        return self.at(l, self.n)

SILU = ACT.Silu
F32R = mybir.dt.float32r
FFN_TILES = 3 * FFN_STEPS
H_READY = (0, 13, 22, 31)
SEQ_PE = 7
SOLVE_PE, SOLVE_DVE = 38, 45
PAIR_FREE = ((2, 3), (4, 5), (7, 9))
DVE_CUM, DVE_KK, DVE_RKK, DVE_FEATURES, DVE_YC, DVE_LN = 5, 9, 24, 29, 31, 39
ACT_KK_SQ, ACT_KK_STD, ACT_LN_SQ, ACT_LN_STD = 4, 6, 7, 9
SOLVER_NEEDS = {"square": (10, 11), "fourth": (18, 20), "eighth": (23, 26), "d3": (28, 30),
                "apply": (31, 32), "turn_n": (33, 34), "y1": (35, 36), "y2": (37, 38), "y3": (39, 40),
                "turn_e": 44}


def SOLVER_GROUPS(lo, up, du, rhs):
    z = lambda s: rhs[:, s, 0:P]
    out = []
    for e in range(2):
        out += [("square", e, 6 + e, up, lo, P, False), ("square", e, 2 + e, lo, up, P, False)]
    for e in range(2):
        out += [("fourth", e, 4 + e, up, lo, P, False), ("fourth", e, 6 + e, lo, up, P, False),
                ("fourth", e, 2 + e, lo, du, P, False)]
    for e in range(2):
        out += [("eighth", e, 4 + e, up, lo, P, False), ("eighth", e, 6 + e, lo, du, P, False)]
    out += [("d3", e, 2 + e, lo, du, P, False) for e in range(2)]
    out += [("apply", e, 4 + 2 * e, du, lambda s: rhs[:, s, :], 2 * P, False) for e in range(2)]
    out += [("turn_n", e, e, lambda s: rhs[:, s, P:2 * P], None, P, True) for e in range(2)]
    out += [("y1", e, 2 + e, up, z, P, False) for e in range(2)]
    out += [("y2", e, e, up, du, P, False) for e in range(2)]
    out += [("y3", e, 2 + e, up, du, P, False) for e in range(2)]
    return out


N_MOD = 6
MODS = N_MOD * KD
FIRST_RISES = {
    "par_ready": 1, "x_ready": 16, "sq_ready": 16, "ss_done": 4, "std_ready": 4, "h_ready": 44,
    "w_high_ready": 66, "w_low_ready": 66, "acc_zero": 2, "silu_done": 22, "act_ready": 66,
    "mix_evac": 13, "mixed": 22, "lora_act": 2, "lora_done": 3, "gates": 10, "dve_step": 39,
    "act_step": 9, "hs_done": 4, "tok_done": 8, "tok_act": 6, "sol_done": 76, "sol_step": 90,
    "seq_done": 14, "seq_step": 17, "y_out": 4, "sc_done": 12, "sm_max": 36, "sm_norm": 36,
    "sm_act": 24, "pt_done": 12, "pt_ready": 12, "av_done": 12, "av_out": 8, "memh_ready": 8,
    "kv_evac": 8, "xq_evac": 4
}
N_MOD = 6
MODS = N_MOD * KD
BIG_NEGATIVE = -1e30
N_INPUTS = 3 + len(PARAMS) + 3


def program(nc, a, out):
    with ExitStack() as ctx:
        store = {}
        sb = lambda n, s: ctx.enter_context(nc.sbuf_tensor(n, s, F32))
        store["x"] = sb("x_sb", [P, KD, T])
        store["par"] = sb("par", [P, DEPTH, NPAR])
        store["final_g"] = sb("final_g", [P, 3 * KD])[:, :]
        consts = sb("consts_sb", [P, sum(c.shape[1] for c in constants().values())])
        cst, at = {"all": consts[:, :]}, 0
        for name, c in constants().items():
            cst[name] = consts[:, at:at + c.shape[1]]
            at += c.shape[1]
        store["cst"] = cst
        store["eps"] = sb("eps", [P, 2])
        store["ps"] = ctx.enter_context(nc.psum_tensor("ps", [P, 8, 512], F32))
        store["w_loaded"] = [Signal(ctx, nc, f"w_loaded{s}") for s in range(RING)]
        store["w_used"] = [Signal(ctx, nc, f"w_used{s}") for s in range(RING)]
        scratch = {"bias": nc.dram_tensor("bias_scratch", (NH, 2 * T), F32).ap(),
                   "mod": nc.dram_tensor("mod_scratch", (DEPTH, P, 2, MODS * P), F32).ap()}
        with ExitStack() as first:
            signals = build_first(nc, first, a, scratch, store)
        with ExitStack() as second:
            signals += build_second(nc, second, a, scratch, store, out)
        for signal in signals:
            rises = signal.layer0 if signal.name in SECOND_RISES else signal.n
            table = SECOND_RISES if signal.name in SECOND_RISES else FIRST_RISES
            assert table.get(signal.name, 0) == rises, signal.name
        return signals


def build_first(nc, ctx, a, scratch, store):
    x_sb, par, cst, eps = store["x"], store["par"], store["cst"], store["eps"]
    PER = FIRST_RISES

    def sb(name, shape):
        return ctx.enter_context(nc.sbuf_tensor(name, shape, F32))

    def sig(name, start=0):
        s = Signal(ctx, nc, name, PER.get(name, 0), start)
        signals.append(s)
        return s

    signals = []
    with ExitStack() as under:
        part = lambda name, shape: under.enter_context(nc.sbuf_tensor(name, shape, F32R))
        w_low = part("w_low", [P, RING, SLOT])
        h_high = part("h_high", [P, KD, T])
        act_high = part("act_high", [P, 2, 512])
        w_high = [part(f"w_high{i}", [P, SLOT])[:, :] for i in range(2)]
        h_low = part("h_low", [P, KD, T])
        act_low = part("act_low", [P, 2, 512])
    ring = sb("ring", [P, RING, SLOT])
    h_sb = sb("h_sb", [P, KD, T])
    probT = sb("probT", [P, 2, 512])
    rk = sb("rk", [P, 2 * NPAIR, T])
    va = sb("va", [P, 2 * NPAIR, T])
    kt = sb("kt", [P, 2 * NPAIR, T])
    e1 = sb("e1", [P, NPAIR, T])
    h_whole = kt
    act_whole = e1[:, :, :].rearrange("p (b a) t -> p b (a t)", b=2)
    mem_sb = sb("mem_sb", [P, KD, T])
    prob = sb("prob", [P, 2, 512])
    hank = sb("hank", [P, NH, T])
    raw_buf = sb("raw_buf", [P, 2 * 2 * (T + 1)])
    dif = sb("dif", [P, 2, T])
    low = sb("low", [P, 2, T])
    sgt = sb("sgt", [P, NPAIR, T])
    cum = sb("cum", [P, NPAIR, T])
    gat = sb("gat", [P, NPAIR, T])
    e2 = sb("e2", [P, NPAIR, T])
    e3 = sb("e3", [P, NPAIR, T])
    cat = sb("cat", [P, KD, T])
    b_tok, k_tok, v_tok = (sb(n, [P, RW]) for n in ("b_tok", "k_tok", "v_tok"))
    ecol = sb("ecol", [P, RW])
    fcol = sb("fcol", [P, RW])
    state = sb("state", [P, NPAIR, HD])
    pend = sb("pend", [P, NPAIR, T // CH])
    mq, mk = sb("mq", [P, NPAIR, T]), sb("mk", [P, NPAIR, T])
    mv = sb("mv", [P, 2, RW])
    lw = sb("lw", [P, 2 * RW])
    std = sb("std", [P, T])
    smx, ssum = sb("smx", [P, 2, 2]), sb("ssum", [P, 2, 2])

    r_t, k_t, v_t, a_t = rk[:, 0:NPAIR], rk[:, NPAIR:], va[:, 0:NPAIR], va[:, NPAIR:]
    kk_t, tmp = kt[:, 0:NPAIR], kt[:, NPAIR:]
    raw = raw_buf[:, :].rearrange("p (b m t) -> p b m t", b=2, m=2)
    mats = lambda ap: ap.rearrange("p a (b t) -> p (a b) t", b=2)
    m_up, l_lo, l_up = mats(sgt[:, :, :]), mats(kk_t), mats(tmp)
    nb_up, nk_up = mats(e2[:, :, :]), mats(e1[:, :, :])
    d_up = raw_buf[:, 0:2 * RW].rearrange("p (s t) -> p s t", s=NH)
    rhs = h_sb[:, :, :]
    e_row, u_tok = low[:, :, :].rearrange("p a (b t) -> p (a b) t", b=2), dif[:, :, :].rearrange("p a t -> p (a t)")
    xq, xk = rk[:, :, :], va[:, :, :]
    xv = kt[:, :, :].rearrange("p (h a) t -> p h (a t)", h=2)
    ps = [store["ps"][:, i, :] for i in range(8)]
    psum = store["ps"]

    ident, ones, head_ones = cst["ident"], cst["ones"], cst["head_ones"]

    def pcol(name, i=0):
        c = PARAM_AT[name] + i
        return par_cur[:, c:c + 1]

    par_cur = sb("par_cur", [P, NPAR])
    cond = sb("cond", [P, 2 * KD])
    wmod = sb("wmod", [P, KD, BLK])
    prod = sb("prod", [P, KD, BLK])
    mod_acc = sb("mod_acc", [P, 2, BLK])
    junk = sb("junk", [P, 3 + RING])

    w_loaded, w_used = store["w_loaded"], store["w_used"]
    w_dram = a

    def slot(n):
        return ring[:, n % RING, :]

    def at_tile(n, l):
        return l * FIRST_USES[n % RING] + n // RING

    def freed(n, l):
        return at_tile(n, l) + 1

    class FfnTiles:

        def __init__(self, l, f):
            self.l, self.f, self.n0 = l, f, FIRST_AT[(f"ffn{f + 1}_gate", 0)]

        def slot(self, r, b):
            return (self.n0 + 3 * b + r) % RING

        def loaded(self, r, b, use):
            s = self.slot(r, b)
            return w_loaded[s].sem, (self.l * FIRST_USES[s] + self.n0 // RING + use + 1) * 16

        def used(self, r, b, use):
            s = self.slot(r, b)
            return w_used[s].sem, self.l * FIRST_USES[s] + (self.n0 // RING + 2) + use

        def split(self, t, signal):
            return signal.at(self.l, t + (FFN_TILES * self.f + 1))

        def act(self, i, part=3):
            return act_ready.at(self.l, 3 * i + (3 * FFN_STEPS * self.f + part))

    lora_loaded = sig("lora_loaded")
    par_ready = sig("par_ready")
    x_ready = sig("x_ready", 1)
    sq_ready = sig("sq_ready")
    ss_done = sig("ss_done")
    std_ready = sig("std_ready")
    h_ready = sig("h_ready")
    w_high_ready = sig("w_high_ready")
    w_low_ready = sig("w_low_ready")
    acc_zero = sig("acc_zero")
    silu_done = sig("silu_done")
    act_ready = sig("act_ready")
    mix_evac = sig("mix_evac")
    mixed = sig("mixed")
    lora_act = sig("lora_act")
    lora_done = sig("lora_done", 1)
    gates = sig("gates")
    dve_step = sig("dve_step")
    act_step = sig("act_step")
    hs_done = sig("hs_done")
    tok_done = sig("tok_done")
    tok_act = sig("tok_act")
    sol_done = sig("sol_done")
    sol_step = sig("sol_step")
    seq_done = sig("seq_done")
    seq_step = sig("seq_step")
    y_out = sig("y_out")
    sc_done = sig("sc_done")
    sm_max = sig("sm_max")
    sm_norm = sig("sm_norm")
    sm_act = sig("sm_act")
    pt_done = sig("pt_done")
    pt_ready = sig("pt_ready")
    av_done = sig("av_done")
    av_out = sig("av_out")
    memh_ready = sig("memh_ready")
    kv_evac = sig("kv_evac")
    wmod_loaded = sig("wmod_loaded")
    mod_stored = sig("mod_stored")
    mod_step = sig("mod_step")
    started = sig("started")
    xq_evac = sig("xq_evac")

    def wait_apart(engine, semaphore, value):
        engine.compute_val(value)
        engine.wait_ge(started.sem, 1)
        engine.wait_ge(semaphore, value)

    def sync_program(sp):
        def load(l, n, source, shape=None):
            s, free = n % RING, freed(n, l)
            wait_apart(sp, w_used[s].sem, free)
            dst = slot(n) if shape is None else slot(n).rearrange(*shape[0], **shape[1])
            sp.dma_start(dst, source).then_inc(w_loaded[s].sem, 16)

        cols = (("p (k n) -> p k n",), {"k": KD})
        rows = (("p (r n) -> p r n",), {"r": 2})

        def column_tile(w, l, c):
            return w[bass.ds(l, 1), :, bass.ds(c, BLK)].rearrange("o (k p) n -> p (o k) n", p=P)

        def row_tile(w, l, r):
            return w[bass.ds(l, 1), bass.ds(r, BLK), :].rearrange("o (k p) n -> p (o k) n", p=P)

        def ffn(l, f):
            w_in, w_out, tiles = w_dram[f"ffn{f + 1}_w_in"], w_dram[f"ffn{f + 1}_w_out"], FfnTiles(l, f)

            def step(i, b, use):
                for r, src in ((0, column_tile(w_in, l, i * BLK)),
                               (1, column_tile(w_in, l, i * BLK + D_FF)),
                               (2, row_tile(w_out, l, i * BLK))):
                    s = tiles.slot(r, b)
                    sp.wait_ge(*tiles.used(r, b, use - 1))
                    dst = ring[:, s, :].rearrange("p (k n) -> p k n", k=KD if r < 2 else 2)
                    sp.dma_start(dst, src).then_inc(w_loaded[s].sem, 16)

            with sp.Fori(0, FFN_STEPS // 2) as j:
                step(j * 2, 0, j)
                step(j * 2 + 1, 1, j)
            step(FFN_STEPS - 1, 0, FFN_STEPS // 2)

        with sp.Fori(0, DEPTH) as l:
            ffn(l, 0)
            for kind, w in (("mix_in", "w_mix_in"), ("kv", "xattn_w_kv"), ("mix_out", "w_mix_out"),
                            ("xq", "xattn_w_q"), ("xo", "xattn_w_o")):
                for name in [n for n in FIRST if n[0] == kind]:
                    load(l, FIRST_AT[name], column_tile(w_dram[w], l, name[1] * BLK), cols)
            ffn(l, 1)

    def tensor_program(pe):
        mm = nc.tensor.matmul

        def norm(l, n):
            squares = cat if n == 3 else h_sb
            for k in range(KD):
                if k % 2 == 0:
                    pe.wait_ge(*sq_ready.at(l, 4 * n + k // 2 + 1))
                last = mm(ps[4][:, 0:T], ones, squares[:, k, :], start=(k == 0), stop=(k == KD - 1))
            last.then_inc(*ss_done.up())

        def normed(l, n):
            def before(k):
                if n in (0, 3):
                    if k % 4 == 0:
                        pe.wait_ge(*h_ready.at(l, H_READY[n] + 1 + 6 * (k // 4 + 1)))
                else:
                    pe.wait_ge(*h_ready.at(l, H_READY[n] + 2 + k))
            return before

        def split_mm(dst, w_hi, w_lo, x_hi, x_lo, start, stop, **more):
            mm(dst, w_hi, x_hi, start=start, stop=False, **more)
            mm(dst, w_hi, x_lo, start=False, stop=False, **more)
            return mm(dst, w_lo, x_hi, start=False, stop=stop, **more)

        def ffn(l, f):
            tiles = FfnTiles(l, f)

            def parts(r, b, t, parity):
                pe.wait_ge(*tiles.split(t, w_low_ready))
                shape = {"k": KD if r < 2 else 2}
                return [ap.rearrange("p (k n) -> p k n", **shape)
                        for ap in (w_high[parity], w_low[:, tiles.slot(r, b), :])]

            def gate_up(i, b, t, parity, reuse, before=None):
                for r, bank in ((0, 4 + b), (1, 6 + b)):
                    hi, lo = parts(r, b, t + r, (parity + r) % 2)
                    if reuse:
                        pe.wait_ge(*(tiles.act(i - 2, 1) if r else
                                     silu_done.at(l, FFN_STEPS * f + i - 1)))
                    for m in range(2):
                        for k in range(KD):
                            if before and r == 0 and m == 0:
                                before(k)
                            cols = slice(m * P, (m + 1) * P)
                            last = split_mm(ps[bank][:, m * T:(m + 1) * T], hi[:, k, cols], lo[:, k, cols],
                                            h_high[:, k, :], h_low[:, k, :], k == 0, k == KD - 1)
                    last.then_inc(w_used[tiles.slot(r, b)].sem, 1)

            def down(i, b, t, parity):
                hi, lo = parts(2, b, t, parity)
                pe.wait_ge(*tiles.act(i))
                for k in range(2):
                    for m in range(KD):
                        cols, ks = slice(m * P, (m + 1) * P), slice(k * T, (k + 1) * T)
                        last = split_mm(ps[m // 2][:, (m % 2) * T:(m % 2 + 1) * T], hi[:, k, cols],
                                        lo[:, k, cols], act_high[:, b, ks], act_low[:, b, ks], False, False,
                                        skip_group_check=True)
                last.then_inc(w_used[tiles.slot(2, b)].sem, 1)

            gate_up(0, 0, 0, 0, False, normed(l, 3 * f))
            gate_up(1, 1, 2, 0, False)
            pe.wait_ge(*acc_zero.at(l, f + 1))
            down(0, 0, 4, 0)
            gate_up(2, 0, 5, 1, True)
            down(1, 1, 7, 1)
            with pe.Fori(1, FFN_STEPS // 2) as j:
                gate_up(j * 2 + 1, 1, j * 6 + 2, 0, True)
                down(j * 2, 0, j * 6 + 4, 0)
                gate_up(j * 2 + 2, 0, j * 6 + 5, 1, True)
                down(j * 2 + 1, 1, j * 6 + 7, 1)
            down(FFN_STEPS - 1, 0, FFN_TILES - 1, 0)

        def column_tile(l, name, bank, x, token_major=False, before=None):
            n = FIRST_AT[name]
            pe.wait_ge(w_loaded[n % RING].sem, (at_tile(n, l) + 1) * 16)
            w = slot(n).rearrange("p (k n) -> p k n", k=KD)
            for m in range(2):
                for k in range(KD):
                    if before and m == 0:
                        before(k)
                    lhs, right = w[:, k, m * P:(m + 1) * P], x[:, k, :]
                    if token_major:
                        lhs, right = x[:, k, m * P:(m + 1) * P], w[:, k, :]
                    last = mm(ps[bank][:, m * T:(m + 1) * T], lhs, right,
                              start=(k == 0), stop=(k == KD - 1))
            last.then_inc(w_used[n % RING].sem, 1)

        def head_sums(src, banks):
            for m in range(NPAIR):
                last = mm(ps[banks + m // 2][:, (m % 2) * T:(m % 2 + 1) * T], head_ones,
                          src[:, m, :], start=True, stop=True)
            last.then_inc(*hs_done.up())

        def moba(l):
            def scores(h):
                pair, hb, e = h // 2, (h % 2) * HD, h % 2
                if h >= 2:
                    pe.wait_ge(*sm_act.at(l, 2 * (h - 1)))
                hi = slice(hb, hb + HD)
                mm(ps[e][:, 0:T], cst["flip"], hank[:, h, :], start=True, stop=False,
                   skip_group_check=True)
                mm(ps[e][:, T:T + P], cst["flip"], hank[:, h, P:T], start=False, stop=False,
                   skip_group_check=True)
                mm(ps[e][:, 0:T], mq[hi, pair, P:T], mk[hi, pair, :], start=False, stop=False,
                   skip_group_check=True)
                mm(ps[e][:, T:T + P], mq[hi, pair, 0:P], mk[hi, pair, 0:P], start=False, stop=True,
                   skip_group_check=True).then_inc(*sc_done.up())

            def turn(h):
                e = h % 2
                pe.wait_ge(*sm_norm.at(l, 3 * (h + 1)))
                if h >= 2:
                    pe.wait_ge(*pt_ready.at(l, h - 1))
                for dst, src in ((P, 0), (2 * P, P), (0, 2 * P)):
                    last = nc.tensor.transpose(ps[2 + e][:, dst:dst + P], prob[:, e, src:src + P], ident)
                last.then_inc(*pt_done.up())

            def out(h):
                pair, hb, e = h // 2, (h % 2) * HD, h % 2
                pe.wait_ge(*pt_ready.at(l, h + 1))
                if pair >= 2 and e == 0:
                    pe.wait_ge(*av_out.at(l, pair - 1))
                dst, cols = ps[6 + pair % 2][hb:hb + HD, 0:T], slice(h * HD, (h + 1) * HD)
                mm(dst, mv[:, 0, cols], probT[:, e, 0:T], start=True, stop=False, skip_group_check=True)
                last = mm(dst[:, P:T], mv[:, 1, cols], probT[:, e, T:T + P], start=False, stop=True,
                          skip_group_check=True)
                last.then_inc(*av_done.up())

            pe.wait_ge(*mix_evac.at(l, MIX_TILES))
            for h in range(NH + 2):
                if h < NH:
                    scores(h)
                if 1 <= h <= NH:
                    turn(h - 1)
                if h >= 2:
                    out(h - 2)

        def solver(l, c):
            ts = slice(c * P, (c + 1) * P)
            s0, d0 = SOLVE_PE * c, SOLVE_DVE * c
            if c:
                pe.wait_ge(*y_out.at(l, 2))
                pe.wait_ge(*seq_step.at(l, 9))
            for q, src in enumerate((e3, a_t, k_t, v_t)):
                for m in range(NPAIR):
                    last = nc.tensor.transpose(ps[q][:, m * P:(m + 1) * P], src[:, m, ts], ident)
                last.then_inc(*tok_done.up())
            for s, (left, right) in enumerate(((k_t, e3), (a_t, e3), (e3, a_t), (a_t, r_t), (k_t, r_t))):
                for e in range(2):
                    if s >= 2:
                        pe.wait_ge(*sol_step.at(l, d0 + PAIR_FREE[s - 2][e]))
                    hi = slice(e * HD, (e + 1) * HD)
                    for m in range(NPAIR):
                        last = mm(ps[4 + 2 * (s % 2) + e][:, m * P:(m + 1) * P], left[hi, m, ts],
                                  right[hi, m, ts], start=True, stop=True)
                    last.then_inc(*sol_done.up())
            pe.wait_ge(*tok_act.at(l, 3 * (c + 1)))
            pe.wait_ge(*sol_step.at(l, d0 + 1 + 2))
            for s in range(NH):
                h = 2 * (s % NPAIR) + s // NPAIR
                last = mm(ps[0][:, s * HD:(s + 1) * HD], m_up[:, s, :], v_tok[:, h * HD:(h + 1) * HD],
                          start=True, stop=True)
            last.then_inc(*sol_done.up())

            def group(bank, e, left, right, cols=P, turned=False):
                for m in range(NPAIR):
                    s = e * NPAIR + m
                    dst = ps[bank + m * cols // 512][:, (m * cols) % 512:(m * cols) % 512 + cols]
                    if turned:
                        last = nc.tensor.transpose(dst, left(s), ident)
                    else:
                        last = mm(dst, left(s), right(s), start=True, stop=True)
                last.then_inc(*sol_done.up())

            lo, up, du = (lambda s: l_lo[:, s, :]), (lambda s: l_up[:, s, :]), (lambda s: d_up[:, s, :])
            for name, e, bank, left, right, cols, turned in SOLVER_GROUPS(lo, up, du, rhs):
                pe.wait_ge(*sol_step.at(l, d0 + SOLVER_NEEDS[name][e]))
                group(bank, e, left, right, cols, turned)
            pe.wait_ge(*sol_step.at(l, d0 + SOLVER_NEEDS["turn_e"]))
            for m in range(NPAIR):
                last = nc.tensor.transpose(ps[4][:, m * P:(m + 1) * P], ecol[:, m * P:(m + 1) * P], ident)
            last.then_inc(*sol_done.up())

        def recurrence(l, c):
            for q in range(2):
                tb, chunk = slice(q * CH, (q + 1) * CH), 2 * c + q
                t0 = c * P + q * CH
                if q == 0:
                    wait_apart(pe, *sol_step.at(l, SOLVE_DVE * (c + 1)))
                wait_apart(pe, *seq_step.at(l, 1 + 4 * chunk))
                for e in range(2):
                    hi = slice(e * HD, (e + 1) * HD)
                    for m in range(NPAIR):
                        last = mm(ps[e][tb, m * HD:(m + 1) * HD], e_row[hi, m, tb], state[hi, m, :],
                                  start=True, stop=True)
                    last.then_inc(*seq_done.up())
                for e in range(2):
                    hi = slice(e * HD, (e + 1) * HD)
                    for m in range(NPAIR):
                        mm(ps[4 + e][hi, m * P + q * CH:m * P + (q + 1) * CH], state[hi, m, :],
                           r_t[hi, m, t0:t0 + CH], start=(q == 0 and m == 0), stop=False,
                           skip_group_check=True)
                wait_apart(pe, *seq_step.at(l, 1 + 4 * chunk + 2))
                for e in range(2):
                    hi = slice(e * HD, (e + 1) * HD)
                    for m in range(NPAIR):
                        h = 2 * m + e
                        hc = slice(h * HD, (h + 1) * HD)
                        dst = ps[2][hi, m * HD:(m + 1) * HD]
                        mm(dst, b_tok[tb, hc], u_tok[tb, hc], start=True, stop=False)
                        last = mm(dst, k_tok[tb, hc], v_tok[tb, hc], start=False, stop=True)
                last.then_inc(*seq_done.up())
            for e in range(2):
                hi = slice(e * HD, (e + 1) * HD)
                for m in range(NPAIR):
                    h, s = 2 * m + e, e * NPAIR + m
                    hc = slice(h * HD, (h + 1) * HD)
                    dst = ps[4 + e][hi, m * P:(m + 1) * P]
                    mm(dst, u_tok[:, hc], nb_up[:, s, :], start=False, stop=False, skip_group_check=True)
                    last = mm(dst, v_tok[:, hc], nk_up[:, s, :], start=False, stop=True,
                              skip_group_check=True)
            last.then_inc(*seq_done.up())

        def cross(l):
            def scores(h):
                e = h % 2
                if h >= 2:
                    pe.wait_ge(*sm_act.at(l, 2 * NH + 2 * (h - 1)))
                for t in range(2):
                    for k in range(2):
                        last = mm(ps[e][:, t * T:(t + 1) * T], xq[:, 2 * h + k, t * P:(t + 1) * P],
                                  xk[:, 2 * h + k, :], start=(k == 0), stop=(k == 1))
                last.then_inc(*sc_done.up())

            def turn(h):
                e = h % 2
                pe.wait_ge(*sm_norm.at(l, 3 * (NH + h + 1)))
                if h >= 2:
                    pe.wait_ge(*pt_ready.at(l, NH + h - 1))
                for t in range(2):
                    for k in range(2):
                        last = nc.tensor.transpose(ps[2 + e][:, k * T + t * P:k * T + (t + 1) * P],
                                                   prob[:, e, t * T + k * P:t * T + (k + 1) * P], ident)
                last.then_inc(*pt_done.up())

            def out(h):
                e = h % 2
                pe.wait_ge(*pt_ready.at(l, NH + h + 1))
                if h >= 2:
                    pe.wait_ge(*av_out.at(l, NPAIR + h - 1))
                for i in range(2):
                    f = (2 * h + i) * P
                    for k in range(2):
                        last = mm(ps[6 + e][:, i * T:(i + 1) * T], xv[:, k, f:f + P],
                                  probT[:, e, k * T:(k + 1) * T], start=(k == 0), stop=(k == 1))
                last.then_inc(*av_done.up())

            pe.wait_ge(*xq_evac.at(l, LIN_TILES))
            for h in range(XH + 2):
                if h < XH:
                    scores(h)
                if 1 <= h <= XH:
                    turn(h - 1)
                if h >= 2:
                    out(h - 2)

        with pe.Fori(0, DEPTH) as l:
            norm(l, 0)
            ffn(l, 0)
            norm(l, 1)
            for n, j in enumerate(MIX_ORDER):
                if n >= 4:
                    pe.wait_ge(*mix_evac.at(l, n - 3))
                column_tile(l, ("mix_in", j), 4 + n % 4, h_sb, token_major=(j >= 11),
                            before=normed(l, 1) if n == 0 else None)
                if n == 2:
                    pe.wait_ge(lora_loaded.sem, l * 48 + 48)
                    pe.wait_ge(*lora_act.at(l, 2))
                    for which, rows in ((0, slice(0, HD)), (1, slice(HD, P))):
                        for m in range(NPAIR):
                            last = mm(ps[2 * which + m // 2][:, (m % 2) * T:(m % 2 + 1) * T],
                                      lw[rows, m * P:(m + 1) * P], low[rows, 0, :],
                                      start=True, stop=True)
                        last.then_inc(*lora_done.up())
                if n == 4:
                    pe.wait_ge(*gates.at(l, 4))
                    for m in range(NPAIR):
                        last = mm(ps[m // 2][:, (m % 2) * T:(m % 2 + 1) * T],
                                  lw[:, RW + m * P:RW + (m + 1) * P], low[:, 1, :],
                                  start=True, stop=True)
                    last.then_inc(*lora_done.up())
                if n == 8:
                    pe.wait_ge(*gates.at(l, 8))
                    pe.wait_ge(*act_step.at(l, ACT_KK_SQ))
                    head_sums(sgt, 2)
                if n == 11:
                    pe.wait_ge(*gates.at(l, 10))
                    pe.wait_ge(*dve_step.at(l, DVE_RKK))
                    head_sums(tmp, 0)
            pe.wait_ge(*dve_step.at(l, DVE_FEATURES))
            moba(l)
            for c in range(2):
                if c == 0:
                    pe.wait_ge(*sm_act.at(l, 2 * NH))
                    pe.wait_ge(*pt_ready.at(l, NH))
                    pe.wait_ge(*av_out.at(l, NPAIR))
                solver(l, c)
                recurrence(l, c)
            pe.wait_ge(*y_out.at(l, 4))
            pe.wait_ge(*memh_ready.at(l, KD))
            for j in range(KV_TILES):
                if j >= 4:
                    pe.wait_ge(*kv_evac.at(l, j - 3))
                column_tile(l, ("kv", j), 4 + j % 4, h_sb, token_major=(j >= 4))
                if j == 0:
                    head_sums(cat, 0)
                if j == 2:
                    pe.wait_ge(*act_step.at(l, ACT_LN_SQ))
                    head_sums(sgt, 2)
            pe.wait_ge(*dve_step.at(l, DVE_LN))
            pe.wait_ge(*kv_evac.at(l, KV_TILES))
            for j in range(LIN_TILES):
                column_tile(l, ("mix_out", j), 4 + j % 4, cat)
            norm(l, 2)
            for j in range(LIN_TILES):
                column_tile(l, ("xq", j), 4 + j % 4, h_sb, before=None if j else normed(l, 2))
            cross(l)
            pe.wait_ge(*av_out.at(l, NPAIR + XH))
            for j in range(LIN_TILES):
                column_tile(l, ("xo", j), 4 + j % 4, h_sb)
            norm(l, 3)
            ffn(l, 1)

    def modulation_program(pool):
        g = nc.gpsimd
        n_tiles = MODS * P // BLK
        MOD_STAGES = 5

        with pool.Fori(0, DEPTH) as l:
            with pool.Fori(0, n_tiles) as t:
                done = l * n_tiles + t
                src = w_dram["w_mod_2"][bass.ds(l, 1), :, bass.ds(t * BLK, BLK)]
                pool.dma_start(wmod[:, :, :], src.rearrange("o (k p) n -> p (o k) n", p=P)
                               ).then_inc(wmod_loaded.sem, 16)
                pool.wait_ge(wmod_loaded.sem, done * 16 + 16)
                for c, dst in enumerate((prod[:, :, :], wmod[:, :, :])):
                    g.tensor_tensor(dst, wmod[:, :, :], cond[:, c * KD:(c + 1) * KD].rearrange(
                        "p (k o) -> p k o", o=1).to_broadcast([P, KD, BLK]), ALU.mult
                        ).then_inc(mod_step.sem, 1)
                    pool.wait_ge(mod_step.sem, done * MOD_STAGES + c + 1)
                for r, half in enumerate((4, 2, 1)):
                    for c, part in enumerate((prod, wmod)):
                        dst = part[:, 0:half, :] if half > 1 else mod_acc[:, c:c + 1, :]
                        last = g.tensor_tensor(dst, part[:, 0:half, :], part[:, half:2 * half, :],
                                               ALU.add)
                    last.then_inc(mod_step.sem, 1)
                    pool.wait_ge(mod_step.sem, done * MOD_STAGES + 3 + r)
                dst = scratch["mod"][bass.ds(l, 1), :, :, bass.ds(t * BLK, BLK)]
                pool.dma_start(dst.rearrange("o p c n -> p (o c) n"), mod_acc[:, :, :]
                               ).then_inc(mod_stored.sem, 16)
                pool.wait_ge(mod_stored.sem, done * 16 + 16)

    def scalar_program(act):
        go = nc.scalar.activation

        def norm(l, n):
            squares = cat if n == 3 else h_sb
            for q in range(4):
                act.wait_ge(*x_ready.at(l, 4 * (n - 1) + q + 1 if n else 0))
                go(squares[:, 2 * q:2 * q + 2, :], x_sb[:, 2 * q:2 * q + 2, :],
                   ACT.Square).then_inc(*sq_ready.up())
            if n in (0, 3):
                w_high_part(FfnTiles(l, n // 3), 0, 0, 0, 0)
            act.wait_ge(*ss_done.at(l, n + 1))
            go(std[:, :], ps[4][:, 0:T], ACT.Sqrt, bias=eps[:, 0:1], scale=1.0 / D).then_inc(*std_ready.up())

        def w_high_part(tiles, r, b, use, parity, before=None):
            act.wait_ge(*tiles.loaded(r, b, use))
            if before:
                act.wait_ge(*tiles.used(*before))
            go(w_high[parity], ring[:, tiles.slot(r, b), :], ACT.Copy).then_inc(w_high_ready.sem, 1)

        def ffn(l, f):
            tiles = FfnTiles(l, f)
            w_high_of = lambda *which: w_high_part(tiles, *which)

            def silu(i, b, use, reuse):
                act.wait_ge(*tiles.used(0, b, use))
                if reuse:
                    act.wait_ge(*tiles.act(i - 2, 1))
                go(prob[:, b, :], ps[4 + b], SILU).then_inc(silu_done.sem, 1)

            w_high_of(1, 0, 0, 1)
            w_high_of(0, 1, 0, 0, (0, 0, 0))
            silu(0, 0, 0, False)
            w_high_of(1, 1, 0, 1, (1, 0, 0))
            w_high_of(2, 0, 0, 0, (0, 1, 0))
            silu(1, 1, 0, False)
            w_high_of(0, 0, 1, 1, (1, 1, 0))
            w_high_of(1, 0, 1, 0, (2, 0, 0))
            w_high_of(2, 1, 0, 1, (0, 0, 1))
            with act.Fori(1, FFN_STEPS // 2) as j:
                silu(j * 2, 0, j, True)
                w_high_of(0, 1, j, 0, (1, 0, j))
                w_high_of(1, 1, j, 1, (2, 1, j - 1))
                w_high_of(2, 0, j, 0, (0, 1, j))
                silu(j * 2 + 1, 1, j, True)
                w_high_of(0, 0, j + 1, 1, (1, 1, j))
                w_high_of(1, 0, j + 1, 0, (2, 0, j))
                w_high_of(2, 1, j, 1, (0, 0, j + 1))
            silu(FFN_STEPS - 1, 0, FFN_STEPS // 2, True)
            w_high_of(2, 0, FFN_STEPS // 2, 0, (1, 0, FFN_STEPS // 2))
            w_high_ready.n += FFN_TILES
            silu_done.n += FFN_STEPS

        def take(l, name, bank, dst, signal, scale=1.0):
            n = FIRST_AT[name]
            act.wait_ge(w_used[n % RING].sem, freed(n, l) + 1)
            go(dst, ps[bank].rearrange("p (m t) -> p m t", m=2), ACT.Copy,
               scale=scale).then_inc(*signal.up())

        def softmax(l, heads, base, scale, widths):
            for h in range(heads + 1):
                if h < heads:
                    e, g = h % 2, base + h
                    act.wait_ge(*sm_max.at(l, 3 * (g + 1)))
                    if h >= 2:
                        act.wait_ge(*pt_done.at(l, g - 1))
                    at = 0
                    for t, w in enumerate(widths):
                        go(prob[:, e, at:at + w], ps[e][:, at:at + w], ACT.Exp, bias=smx[:, e, t:t + 1],
                           scale=scale, accum_out=ssum[:, e, t:t + 1]).then_inc(*sm_act.up())
                        at += w
                if h >= 1:
                    e, g = (h - 1) % 2, base + h - 1
                    act.wait_ge(*pt_done.at(l, g + 1))
                    if h >= 3:
                        act.wait_ge(*av_done.at(l, g - 1))
                    w = sum(widths)
                    go(probT[:, e, 0:w], ps[2 + e][:, 0:w], ACT.Copy).then_inc(*pt_ready.up())

        with act.Fori(0, DEPTH) as l:
            act.wait_ge(*lora_done.at(l, 0))
            for dst, src in ((lw[0:HD, 0:RW], "rwkv_w_up"), (lw[HD:P, 0:RW], "rwkv_a_up"),
                             (lw[:, RW:], "rwkv_g_up")):
                act.dma_start(dst, w_dram[src][bass.ds(l, 1)].rearrange("o k n -> (o k) n")
                              ).then_inc(lora_loaded.sem, 16)
            norm(l, 0)
            ffn(l, 0)
            norm(l, 1)
            for n, j in enumerate(MIX_ORDER):
                if n < 7:
                    act.wait_ge(*mixed.at(l, 1 + 3 * max(n - 1, 0)))
                    take(l, ("mix_in", j), 4 + n % 4, raw[:, n % 2, :, 1:T + 1], mix_evac)
                elif j < 9:
                    take(l, ("mix_in", j), 4 + n % 4, mq[:, 2 * (j - 7):2 * (j - 7) + 2, :], mix_evac,
                         scale=HD ** -0.5)
                elif j < 11:
                    take(l, ("mix_in", j), 4 + n % 4, mk[:, 2 * (j - 9):2 * (j - 9) + 2, :], mix_evac)
                else:
                    take(l, ("mix_in", j), 4 + n % 4, mv[:, :, (j - 11) * BLK:(j - 10) * BLK], mix_evac)
                if n == 1:
                    act.wait_ge(*mixed.at(l, 4))
                    go(low[0:HD, 0, :], low[0:HD, 0, :], ACT.Tanh).then_inc(*lora_act.up())
                    go(low[:, 1, :], low[:, 1, :], ACT.Sigmoid).then_inc(*lora_act.up())
                if n == 3:
                    for dst, bank, bias, which in ((sgt, 0, "rwkv_w0", 1), (a_t, 2, "rwkv_a0", 2)):
                        act.wait_ge(*lora_done.at(l, which))
                        for m in range(NPAIR):
                            go(dst[:, m, :], ps[bank + m // 2][:, (m % 2) * T:(m % 2 + 1) * T],
                               ACT.Sigmoid, bias=pcol(bias, m)).then_inc(*gates.up())
                if n == 5:
                    act.wait_ge(*lora_done.at(l, 3))
                    for i in range(2):
                        go(gat[:, 2 * i:2 * i + 2, :], ps[i].rearrange("p (m t) -> p m t", m=2),
                           ACT.Copy).then_inc(*gates.up())
                    act.wait_ge(*dve_step.at(l, DVE_CUM))
                    go(e1[:, :, :], cum[:, :, :], ACT.Exp, scale=-DECAY).then_inc(*act_step.up())
                    go(e2[:, :, :], cum[:, :, :], ACT.Exp, scale=DECAY).then_inc(*act_step.up())
                    go(e3[:, :, :], e3[:, :, :], ACT.Exp, scale=-DECAY).then_inc(*act_step.up())
                if n == 6:
                    act.wait_ge(*dve_step.at(l, DVE_KK))
                    go(sgt[:, :, :], kk_t, ACT.Square).then_inc(*act_step.up())
                if n == 8:
                    act.wait_ge(*hs_done.at(l, 1))
                    for i in range(2):
                        go(sgt[:, 2 * i:2 * i + 2, :], ps[2 + i].rearrange("p (m t) -> p m t", m=2),
                           ACT.Sqrt).then_inc(*act_step.up())
            softmax(l, NH, 0, 1.0, (T, P))
            for c in range(2):
                for q, dst in enumerate((b_tok, k_tok, v_tok)):
                    act.wait_ge(*tok_done.at(l, 4 * c + q + 2))
                    go(dst[:, :], ps[q + 1], ACT.Copy).then_inc(*tok_act.up())
                act.wait_ge(*seq_done.at(l, SEQ_PE * (c + 1)))
                for e in range(2):
                    hi = slice(e * HD, (e + 1) * HD)
                    go(cat[hi, 0:NPAIR, c * P:(c + 1) * P],
                       ps[4 + e][hi, :].rearrange("p (m t) -> p m t", m=NPAIR),
                       ACT.Copy).then_inc(*y_out.up())
            for k in range(KD):
                go(h_sb[:, k, :], mem_sb[:, k, :], ACT.Copy, scale=pcol("mem_norm_g", k)
                   ).then_inc(*memh_ready.up())
            for j in range(KV_TILES):
                take(l, ("kv", j), 4 + j % 4, xk[:, 2 * j:2 * j + 2, :] if j < 4 else
                     xv[:, :, (j - 4) * BLK:(j - 3) * BLK], kv_evac)
                if j == 1:
                    act.wait_ge(*dve_step.at(l, DVE_YC))
                    go(sgt[:, :, :], cat[:, 0:NPAIR, :], ACT.Square).then_inc(*act_step.up())
                if j == 2:
                    act.wait_ge(*hs_done.at(l, 4))
                    for i in range(2):
                        go(sgt[:, 2 * i:2 * i + 2, :], ps[2 + i].rearrange("p (m t) -> p m t", m=2),
                           ACT.Sqrt, bias=eps[:, 1:2], scale=1.0 / HD).then_inc(*act_step.up())
            norm(l, 2)
            for j in range(LIN_TILES):
                take(l, ("xq", j), 4 + j % 4, xq[:, 2 * j:2 * j + 2, :], xq_evac)
            softmax(l, XH, NH, XD ** -0.5, (T, T))
            norm(l, 3)
            ffn(l, 1)

    def vector_program(dve):
        v = nc.vector

        def residual(l, n, names, scale):
            for q in range(4):
                bank, tile = (q, names[0]) if len(names) == 1 else (4 + q, names[q])
                s = tile % RING
                dve.wait_ge(w_used[s].sem, freed(tile, l) + 1)
                v.scalar_tensor_tensor(x_sb[:, 2 * q:2 * q + 2, :],
                                       ps[bank].rearrange("p (m t) -> p m t", m=2), scale,
                                       x_sb[:, 2 * q:2 * q + 2, :], ALU.mult, ALU.add
                                       ).then_inc(*x_ready.up())

        def norm(l, n, gain):
            if n in (0, 3):
                dve.wait_ge(*x_ready.at(l, 4 * n))
                v.memset(psum[:, 0:4, :], 0.0).then_inc(*acc_zero.up())
                w_low_part(FfnTiles(l, n // 3), 0, 0, 0, 0)
            dve.wait_ge(*std_ready.at(l, n + 1))
            step(l, v.reciprocal(std[:, :], std[:, :]), h_ready)
            if n in (0, 3):
                for half in (slice(0, KD // 2), slice(KD // 2, KD)):
                    for k in range(half.start, half.stop):
                        v.scalar_tensor_tensor(h_whole[:, k, :], x_sb[:, k, :], pcol(gain, k), std[:, :],
                                               ALU.mult, ALU.mult).then_inc(*h_ready.up())
                    dve.wait_ge(*h_ready.now(l))
                    step(l, v.tensor_copy(h_high[:, half, :], h_whole[:, half, :]), h_ready)
                    v.tensor_tensor(h_low[:, half, :], h_whole[:, half, :], h_high[:, half, :], ALU.subtract
                                    ).then_inc(*h_ready.up())
            else:
                for k in range(KD):
                    v.scalar_tensor_tensor(h_sb[:, k, :], x_sb[:, k, :], pcol(gain, k), std[:, :],
                                           ALU.mult, ALU.mult).then_inc(*h_ready.up())

        def w_low_part(tiles, r, b, t, parity):
            slot = tiles.slot(r, b)
            dve.wait_ge(*tiles.split(t, w_high_ready))
            v.tensor_tensor(w_low[:, slot, :], ring[:, slot, :], w_high[parity], ALU.subtract
                            ).then_inc(w_low_ready.sem, 1)

        def ffn(l, f):
            tiles = FfnTiles(l, f)
            w_low_of = lambda *which: w_low_part(tiles, *which)

            def times_up(i, b, use, reuse):
                dve.wait_ge(*silu_done.at(l, i + (FFN_STEPS * f + 1)))
                dve.wait_ge(*tiles.used(1, b, use))
                if reuse:
                    dve.wait_ge(*tiles.used(2, b, use - 1))
                v.tensor_tensor(act_whole[:, b, :], prob[:, b, :], ps[6 + b], ALU.mult
                                ).then_inc(act_ready.sem, 1)
                dve.wait_ge(*tiles.act(i, 1))
                v.tensor_copy(act_high[:, b, :], act_whole[:, b, :]).then_inc(act_ready.sem, 1)
                dve.wait_ge(*tiles.act(i, 2))
                v.tensor_tensor(act_low[:, b, :], act_whole[:, b, :], act_high[:, b, :], ALU.subtract
                                ).then_inc(act_ready.sem, 1)

            w_low_of(1, 0, 1, 1)
            w_low_of(0, 1, 2, 0)
            times_up(0, 0, 0, False)
            w_low_of(1, 1, 3, 1)
            w_low_of(2, 0, 4, 0)
            w_low_of(0, 0, 5, 1)
            times_up(1, 1, 0, False)
            w_low_of(1, 0, 6, 0)
            w_low_of(2, 1, 7, 1)
            with dve.Fori(1, FFN_STEPS // 2) as j:
                w_low_of(0, 1, j * 6 + 2, 0)
                times_up(j * 2, 0, j, True)
                w_low_of(1, 1, j * 6 + 3, 1)
                w_low_of(2, 0, j * 6 + 4, 0)
                w_low_of(0, 0, j * 6 + 5, 1)
                times_up(j * 2 + 1, 1, j, True)
                w_low_of(1, 0, j * 6 + 6, 0)
                w_low_of(2, 1, j * 6 + 7, 1)
            w_low_of(2, 0, FFN_TILES - 1, 0)
            times_up(FFN_STEPS - 1, 0, FFN_STEPS // 2, True)
            w_low_ready.n += FFN_TILES
            act_ready.n += 3 * FFN_STEPS
            residual(l, None, [tiles.n0 + FFN_TILES - 1], 0.5)

        def step(l, instruction, signal=None):
            signal = signal or dve_step
            instruction.then_inc(*signal.up())
            dve.wait_ge(*signal.now(l))

        def shift(l, n, j):
            dst, at = {6: (low, 0), 2: (k_t, 0), 3: (k_t, 2), 4: (v_t, 0), 5: (v_t, 2),
                       0: (r_t, 0), 1: (r_t, 2)}[j]
            dve.wait_ge(*mix_evac.at(l, n + 1))
            b = raw[:, n % 2]
            step(l, v.tensor_tensor(dif[:, :, :], b[:, :, 0:T], b[:, :, 1:T + 1], ALU.subtract), mixed)
            for m in range(2):
                step(l, v.scalar_tensor_tensor(dst[:, at + m, :], dif[:, m, :], pcol("rwkv_mu", 2 * j + m),
                                               b[:, m, 1:T + 1], ALU.mult, ALU.add), mixed)

        def softmax(l, heads, base, scale, widths, evac):
            for h in range(heads + 2):
                if h < heads:
                    e, g = h % 2, base + h
                    dve.wait_ge(*sc_done.at(l, g + 1))
                    at = 0
                    for t, w in enumerate(widths):
                        step(l, v.tensor_reduce(smx[:, e, t:t + 1], ps[e][:, at:at + w], AX_X, ALU.max),
                             sm_max)
                        at += w
                    step(l, v.tensor_scalar(smx[:, e, :], smx[:, e, :], -scale, None, ALU.mult), sm_max)
                if 1 <= h <= heads:
                    e, g = (h - 1) % 2, base + h - 1
                    dve.wait_ge(*sm_act.at(l, 2 * (g + 1)))
                    step(l, v.reciprocal(ssum[:, e, :], ssum[:, e, :]), sm_norm)
                    at = 0
                    for t, w in enumerate(widths):
                        step(l, v.tensor_scalar(prob[:, e, at:at + w], prob[:, e, at:at + w],
                                                ssum[:, e, t:t + 1], None, ALU.mult), sm_norm)
                        at += w
                if h >= 2:
                    evac(h - 2)

        def moba_out(l):
            def evac(h):
                if h % 2:
                    dve.wait_ge(*av_done.at(l, h + 1))
                    step(l, v.tensor_copy(cat[:, NPAIR + h // 2, :], ps[6 + (h // 2) % 2][:, 0:T]), av_out)
            return evac

        def cross_out(l):
            def evac(h):
                dve.wait_ge(*av_done.at(l, NH + h + 1))
                step(l, v.tensor_copy(h_sb[:, 2 * h:2 * h + 2, :],
                                      ps[6 + h % 2].rearrange("p (m t) -> p m t", m=2)), av_out)
            return evac

        def by_slot(ap, e):
            return ap[:, e * NPAIR:(e + 1) * NPAIR, :]

        def bank4(b):
            return ps[b].rearrange("p (s t) -> p s t", s=NPAIR)

        def mask(name):
            return cst[name].rearrange("p (o t) -> p o t", o=1).to_broadcast([P, NPAIR, P])

        def solver(l, c):
            def need(n):
                dve.wait_ge(*sol_done.at(l, SOLVE_PE * c + n))

            def take(n, instruction):
                step(l, instruction(), sol_step)

            def masked(n, dst, e, bank, name):
                need(n)
                step(l, v.tensor_tensor(by_slot(dst, e), bank4(bank), mask(name), ALU.mult), sol_step)

            def copy(n, dst, bank):
                need(n)
                step(l, v.tensor_copy(dst, bank4(bank)), sol_step)

            def add(n, dst, bank, more):
                need(n)
                step(l, v.tensor_tensor(dst, bank4(bank), more, ALU.add), sol_step)

            dve.wait_ge(*tok_done.at(l, 4 * c + 1))
            step(l, v.tensor_copy(rhs[:, :, 0:HD].rearrange("p (e m) d -> p m e d", e=2),
                                  ps[0].rearrange("p (m e d) -> p m e d", m=NPAIR, e=2)), sol_step)
            for e in range(2):
                masked(1 + e, m_up, e, 4 + e, "upper")
            for e in range(2):
                masked(3 + e, l_up, e, 6 + e, "upper_sub")
            for e in range(2):
                masked(5 + e, l_lo, e, 4 + e, "lower_sub")
                masked(5 + e, rhs[:, :, P:2 * P], e, 4 + e, "lower_off")
            for e in range(2):
                masked(7 + e, nb_up, e, 6 + e, "upper_incl")
            for e in range(2):
                masked(9 + e, nk_up, e, 4 + e, "upper_incl")
            need(11)
            step(l, v.tensor_copy(rhs[:, :, HD:P], ps[0].rearrange("p (s d) -> p s d", s=NH)), sol_step)
            for e in range(2):
                step(l, v.tensor_tensor(by_slot(d_up, e), by_slot(l_up, e), mask("ident"), ALU.add),
                     sol_step)
            for e in range(2):
                copy(13 + 2 * e, by_slot(l_lo, e), 6 + e)
                copy(13 + 2 * e, by_slot(l_up, e), 2 + e)
            for e in range(2):
                add(18 + 3 * e, by_slot(d_up, e), 2 + e, by_slot(d_up, e))
                copy(18 + 3 * e, by_slot(l_lo, e), 4 + e)
                copy(18 + 3 * e, by_slot(l_up, e), 6 + e)
            for e in range(2):
                add(23 + 2 * e, by_slot(d_up, e), 6 + e, by_slot(d_up, e))
                copy(23 + 2 * e, by_slot(l_lo, e), 4 + e)
            for e in range(2):
                add(26 + e, by_slot(d_up, e), 2 + e, by_slot(d_up, e))
            for e in range(2):
                need(28 + e)
                step(l, v.tensor_copy(by_slot(rhs, e), psum[:, 4 + 2 * e:6 + 2 * e, :].rearrange(
                    "p b (s t) -> p (b s) t", s=2)), sol_step)
            for e in range(2):
                copy(30 + e, by_slot(l_up, e), 0 + e)
            for e in range(2):
                add(32 + e, by_slot(d_up, e), 2 + e, by_slot(rhs, e)[:, :, 0:P])
            for e in range(2):
                add(34 + e, by_slot(d_up, e), 0 + e, by_slot(rhs, e)[:, :, 0:P])
            for e in range(2):
                need(36 + e)
                for col, dst in ((0, ecol), (HD, fcol)):
                    step(l, v.tensor_tensor(
                        dst[:, :].rearrange("p (m e d) -> p m e d", m=NPAIR, e=2)[:, :, e, :],
                        bank4(2 + e)[:, :, col:col + HD], by_slot(rhs, e)[:, :, col:col + HD], ALU.add),
                        sol_step)
            copy(38, e_row, 4)

        def recurrence(l, c):
            for q in range(2):
                tb, base = slice(q * CH, (q + 1) * CH), SEQ_PE * c + 3 * q
                head = lambda ap, e: ap[tb, :].rearrange("p (m e d) -> p m e d", m=NPAIR, e=2)[:, :, e, :]
                for e in range(2):
                    dve.wait_ge(*seq_done.at(l, base + e + 1))
                    step(l, v.tensor_tensor(head(u_tok, e), ps[e][tb, 0:NPAIR * HD].rearrange(
                        "p (m d) -> p m d", m=NPAIR), head(fcol, e), ALU.add), seq_step)
                dve.wait_ge(*seq_done.at(l, base + 3))
                step(l, v.tensor_tensor(state[:, :, :], ps[2][:, 0:NPAIR * HD].rearrange(
                    "p (m d) -> p m d", m=NPAIR), state[:, :, :], ALU.add), seq_step)
                step(l, v.tensor_tensor(state[:, :, :], state[:, :, :],
                                        pend[:, :, 2 * c + q:2 * c + q + 1].to_broadcast([P, NPAIR, HD]),
                                        ALU.mult), seq_step)

        with dve.Fori(0, DEPTH) as l:
            step(l, v.tensor_copy(par_cur[:, :], par[:, bass.ds(l, 1), :].rearrange("p o n -> p (o n)")),
                 par_ready)
            norm(l, 0, "ffn1_norm_g")
            ffn(l, 0)
            norm(l, 1, "mix_norm_g")
            step(l, v.memset(raw_buf[:, :], 0.0), mixed)
            for n, j in enumerate(MIX_ORDER[:7]):
                shift(l, n, j)
                if n == 3:
                    dve.wait_ge(*gates.at(l, 4))
                    for m in range(NPAIR):
                        step(l, v.tensor_tensor_scan(cum[:, m, :], cst["carry"], sgt[:, m, :], 0.0,
                                                     ALU.mult, ALU.add))
                    step(l, v.tensor_tensor(e3[:, :, :], cum[:, :, :], sgt[:, :, :], ALU.subtract))
                if n == 4:
                    for m in range(NPAIR):
                        step(l, v.tensor_scalar(kk_t[:, m, :], k_t[:, m, :], pcol("rwkv_k_k", m), None,
                                                ALU.mult))
                    dve.wait_ge(*gates.at(l, 8))
                    for m in range(NPAIR):
                        step(l, v.tensor_scalar(tmp[:, m, :], a_t[:, m, :], 1.0, pcol("rwkv_k_a", m),
                                                ALU.subtract, ALU.mult))
                    step(l, v.scalar_tensor_tensor(k_t, tmp, 1.0, k_t, ALU.add, ALU.mult))
            dve.wait_ge(*act_step.at(l, ACT_KK_STD))
            step(l, v.tensor_scalar(sgt[:, :, :], sgt[:, :, :], 1e-12, None, ALU.max))
            step(l, v.reciprocal(sgt[:, :, :], sgt[:, :, :]))
            step(l, v.tensor_tensor(kk_t, kk_t, sgt[:, :, :], ALU.mult))
            step(l, v.tensor_tensor(a_t, kk_t, a_t, ALU.mult))
            step(l, v.tensor_tensor(a_t, a_t, e2[:, :, :], ALU.mult))
            step(l, v.scalar_tensor_tensor(e3[:, :, :], kk_t, -1.0, e3[:, :, :], ALU.mult, ALU.mult))
            for m in range(NPAIR):
                step(l, v.scalar_tensor_tensor(tmp[:, m, :], r_t[:, m, :], pcol("rwkv_r_k", m),
                                               k_t[:, m, :], ALU.mult, ALU.mult))
            step(l, v.tensor_tensor(k_t, k_t, e2[:, :, :], ALU.mult))
            step(l, v.tensor_tensor(r_t, r_t, e1[:, :, :], ALU.mult))
            dve.wait_ge(*hs_done.at(l, 2))
            for i in range(2):
                step(l, v.tensor_tensor(cum[:, 2 * i:2 * i + 2, :], ps[i].rearrange(
                    "p (m t) -> p m t", m=2), v_t[:, 2 * i:2 * i + 2, :], ALU.mult))
            step(l, v.tensor_copy(pend[:, :, :], e1[:, :, CH - 1::CH]))
            step(l, v.memset(state[:, :, :], 0.0), seq_step)
            softmax(l, NH, 0, 1.0, (T, P), moba_out(l))
            for c in range(2):
                solver(l, c)
                recurrence(l, c)
            dve.wait_ge(*y_out.at(l, 4))
            dve.wait_ge(*hs_done.at(l, 3))
            for i in range(2):
                y = cat[:, 2 * i:2 * i + 2, :]
                step(l, v.scalar_tensor_tensor(y, ps[i].rearrange("p (m t) -> p m t", m=2), -1.0 / HD, y,
                                               ALU.mult, ALU.add))
            y = cat[:, 0:NPAIR, :]
            dve.wait_ge(*act_step.at(l, ACT_LN_STD))
            step(l, v.reciprocal(sgt[:, :, :], sgt[:, :, :]))
            step(l, v.tensor_tensor(y, y, sgt[:, :, :], ALU.mult))
            for m in range(NPAIR):
                step(l, v.tensor_scalar(cat[:, m, :], cat[:, m, :], pcol("rwkv_ln_g", m),
                                        pcol("rwkv_ln_b", m), ALU.mult, ALU.add))
            step(l, v.tensor_tensor(y, y, cum[:, :, :], ALU.add))
            step(l, v.tensor_tensor(y, y, gat[:, :, :], ALU.mult))
            residual(l, 1, [FIRST_AT[("mix_out", j)] for j in range(LIN_TILES)], 1.0)
            norm(l, 2, "xattn_norm_g")
            softmax(l, XH, NH, XD ** -0.5, (T, T), cross_out(l))
            residual(l, 2, [FIRST_AT[("xo", j)] for j in range(LIN_TILES)], 1.0)
            norm(l, 3, "ffn2_norm_g")
            ffn(l, 1)


    with nc.Block() as block:
        loaded = Signal(ctx, nc, "inputs_loaded")
        const_loaded = Signal(ctx, nc, "const_loaded")
        relb_loaded = Signal(ctx, nc, "relb_loaded")
        turned = Signal(ctx, nc, "inputs_turned")
        placed = Signal(ctx, nc, "inputs_placed")
        mem_sq = Signal(ctx, nc, "mem_squares")
        mem_norm = Signal(ctx, nc, "mem_normalised")
        bias_row = Signal(ctx, nc, "bias_row")
        bias_stored = Signal(ctx, nc, "bias_stored")
        x_tok = h_sb[:, :, :].rearrange("p (h a) t -> p h (a t)", h=2)
        m_tok = cat[:, :, :].rearrange("p (h a) t -> p h (a t)", h=2)
        p_rows = rk[:, 0:2, :].rearrange("p a t -> p (a t)")
        onehot, relb, rows = va[:, 0:2, :].rearrange("p a t -> p (a t)"), std[0:33, 0:NH], kt[0:NH, 0:2, :].rearrange("p a t -> p (a t)")
        n_loads = 0

        @block.sync
        def _(sp):
            sp.dma_start(cst["all"], w_dram["consts"]).then_inc(const_loaded.sem, 16)
            sp.dma_start(x_tok, w_dram["x"].rearrange("o (h p) n -> p (o h) n", p=P)).then_inc(loaded.sem, 16)
            sp.dma_start(m_tok, w_dram["mem"].rearrange("o (h p) n -> p (o h) n", p=P)).then_inc(loaded.sem, 16)
            sp.dma_start(onehot[0:33, :], w_dram["onehot"]).then_inc(loaded.sem, 16)
            sp.wait_ge(*bias_row.at(0, 1))
            sp.dma_start(scratch["bias"], rows).then_inc(bias_stored.sem, 16)
            sp.wait_ge(bias_stored.sem, 16)
            src = scratch["bias"]
            sp.dma_start(hank[:, :, :], bass.AP(src.tensor, 0, [[1, P], [2 * T, NH], [1, T]])
                         ).then_inc(bias_stored.sem, 16)
            sp.wait_ge(bias_stored.sem, 32)

        @block.gpsimd
        def _(pool):
            for n, signal in enumerate([started, x_ready, lora_done] + w_used):
                nc.gpsimd.memset(junk[:, n:n + 1], 0.0).then_inc(signal.sem, 1)
            nc.gpsimd.memset(std[0:33, 0:NH], BIG_NEGATIVE).then_inc(*mem_norm.up())
            pool.wait_ge(*mem_norm.at(0, 1))
            pool.dma_start(relb[0:32, :], w_dram["rel_bias"].rearrange("h b -> b h"),
                           allow_slow_non_contiguous=True).then_inc(relb_loaded.sem, 16)

        @block.scalar
        def _(act):
            for name, n in PARAMS:
                r = w_dram[name]
                if len(r.shape) == 3:
                    r = r.rearrange("l h d -> l (h d)")
                c = PARAM_AT[name]
                act.dma_start(p_rows[c:c + n, 0:DEPTH * P].rearrange("c (l p) -> c l p", l=DEPTH),
                              r.rearrange("l (c p) -> c l p", p=P)).then_inc(loaded.sem, 16)
            act.dma_start(p_rows[NPAR:NPAR + KD, 0:P],
                          w_dram["final_norm_g"].rearrange("(c p) -> c p", p=P)).then_inc(loaded.sem, 16)
            for n, name in ((1, "c_ctx_2"), (2, "c_2")):
                src = w_dram[name] if len(w_dram[name].shape) == 1 else w_dram[name][0]
                act.dma_start(p_rows[NPAR + n * KD:NPAR + (n + 1) * KD, 0:P],
                              src.rearrange("(c p) -> c p", p=P)).then_inc(loaded.sem, 16)
            act.wait_ge(loaded.sem, 16 * N_INPUTS)
            act.wait_ge(*placed.at(0, 1))
            for h in range(2):
                nc.scalar.activation(probT[:, :, :].rearrange("p a n -> p (a n)"), m_tok[:, h, :],
                                     ACT.Square, accum_out=smx[:, h, 0:1]).then_inc(*mem_sq.up())
                act.wait_ge(*mem_sq.now(0))
            nc.scalar.activation(smx[:, :, 1:2], smx[:, :, 0:1], ACT.Sqrt, bias=eps[:, 0:1],
                                 scale=1.0 / D).then_inc(*mem_sq.up())
            act.wait_ge(*placed.at(0, 7))
            nc.scalar.activation(cond[:, :], store["final_g"][:, KD:3 * KD], SILU).then_inc(*mem_sq.up())

        @block.tensor
        def _(pe):
            pe.wait_ge(const_loaded.sem, 16)
            pe.wait_ge(loaded.sem, 16 * N_INPUTS)
            pe.wait_ge(relb_loaded.sem, 16)
            for l in range(DEPTH):
                nc.tensor.transpose(ps[0][:, l * P:l * P + NPAR], p_rows[0:NPAR, l * P:(l + 1) * P],
                                    ident[0:NPAR, 0:NPAR])
            nc.tensor.matmul(ps[1][0:NH, :], relb, onehot[0:33, :], start=True, stop=True)
            for h in range(2):
                for k in range(KD):
                    b, at = 2 + k // 2, (k % 2) * T + h * P
                    last = nc.tensor.transpose(ps[b][:, at:at + P], x_tok[:, h, k * P:(k + 1) * P], ident)
            last.then_inc(*turned.up())
            pe.wait_ge(*placed.at(0, 6))
            pe.wait_ge(*mem_norm.at(0, 4))
            for h in range(2):
                for k in range(KD):
                    b, at = 2 + k // 2, (k % 2) * T + h * P
                    last = nc.tensor.transpose(ps[b][:, at:at + P], m_tok[:, h, k * P:(k + 1) * P], ident)
            last.then_inc(*turned.up())
            nc.tensor.transpose(ps[0][:, 0:NPAR + 3 * KD], p_rows[0:NPAR + 3 * KD, 0:P],
                                ident[0:NPAR + 3 * KD, 0:NPAR + 3 * KD]).then_inc(*turned.up())

        @block.vector
        def _(dve):
            v = nc.vector
            v.memset(eps[:, 0:1], EPS)
            v.memset(eps[:, 1:2], LNX_EPS).then_inc(*placed.up())
            dve.wait_ge(*turned.at(0, 1))
            v.tensor_copy(par[:, 0:DEPTH, :], ps[0][:, 0:DEPTH * P].rearrange(
                "p (l c) -> p l c", l=DEPTH)[:, :, 0:NPAR]).then_inc(*placed.up())
            v.tensor_copy(rows, ps[1][0:NH, :]).then_inc(*bias_row.up())
            for q in range(4):
                v.tensor_copy(x_sb[:, 2 * q:2 * q + 2, :], ps[2 + q].rearrange("p (m t) -> p m t", m=2)
                              ).then_inc(*placed.up())
            dve.wait_ge(*mem_sq.at(0, 3))
            v.reciprocal(smx[:, :, 1:2], smx[:, :, 1:2]).then_inc(*mem_norm.up())
            dve.wait_ge(*mem_norm.at(0, 2))
            for h in range(2):
                v.tensor_scalar(m_tok[:, h, :], m_tok[:, h, :], smx[:, h, 1:2], None, ALU.mult
                                ).then_inc(*mem_norm.up())
            dve.wait_ge(*turned.at(0, 3))
            v.tensor_copy(store["final_g"], ps[0][:, NPAR:NPAR + 3 * KD]).then_inc(*placed.up())
            for q in range(4):
                v.tensor_copy(mem_sb[:, 2 * q:2 * q + 2, :], ps[2 + q].rearrange("p (m t) -> p m t", m=2)
                              ).then_inc(*placed.up())
            dve.wait_ge(*placed.now(0))
            dve.wait_ge(*mem_sq.at(0, 4))

    block = ctx.enter_context(nc.Block())

    @block.sync
    def _(sp):
        sync_program(sp)

    @block.gpsimd
    def _(pool):
        modulation_program(pool)

    @block.tensor
    def _(pe):
        tensor_program(pe)

    @block.scalar
    def _(act):
        scalar_program(act)

    @block.vector
    def _(dve):
        vector_program(dve)

    return signals


RING2 = 8
CTX, LAT = 0, 1
TT = 2 * T
GQ, KVH = 6, 2
MH, NOPE, ROPE_D = 6, 64, 32
MQK = NOPE + ROPE_D
HID = 4 * D
MLP_STEPS = HID // BLK
WINDOWS = (2, 4, 8, 16)
GRID_W = 64
EDGE = max(WINDOWS) // 2
IN_TILES = [(2, 512, 256), (3, 768, 256), (0, 0, 256), (1, 256, 256), (4, 1024, 32), (5, 1056, 256)]
MOD_THIRDS = 3

PARAMS2 = [("b_mod", MODS), ("g_norm1", KD), ("g_norm2", KD), ("g_cq", 2), ("g_ckv", 1), ("ls_pool", 2)]
PARAM2_AT = {}
NPAR2 = 0
for _name, _n in PARAMS2:
    PARAM2_AT[_name] = NPAR2
    NPAR2 += _n
for _name in ("g_q_gqa", "g_k_gqa", "g_q_mla", "g_k_mla"):
    PARAM2_AT[_name] = NPAR2
    NPAR2 += 1


def second_schedule():
    s = []
    for i in range(DEPTH):
        s += [("mod", i, c, t) for c in range(2) for t in range(MOD_THIRDS)]
        s += [("in", i, j) for j, _, _ in IN_TILES]
        s += [("uq", i), ("ukv", i)]
        s += [("out", i, j) for j in range(LIN_TILES)]
        for c in (CTX, LAT) if i < DEPTH - 1 else (LAT,):
            s += [(kind, i, c, n) for n in range(MLP_STEPS) for kind in ("mlp1", "mlp2")]
    return s


SECOND = second_schedule()
SECOND_AT = {name: n for n, name in enumerate(SECOND)}


def constants2():
    def rope(dim):
        n = dim // 4
        inv = (np.float32(10000.0) ** (-np.arange(n, dtype=np.float32) / np.float32(n))).astype(np.float32)
        row = np.repeat(np.arange(T // GRID_W, dtype=np.float32), GRID_W)
        col = np.tile(np.arange(GRID_W, dtype=np.float32), T // GRID_W)
        ang = np.concatenate([row[:, None] * inv, col[:, None] * inv], axis=-1)
        return np.cos(ang).T.astype(np.float32), np.sin(ang).T.astype(np.float32)

    def rotation(at, half):
        m = np.zeros((P, P), np.float32)
        for a in at:
            for i in range(half):
                m[a + half + i, a + i] = -1.0
                m[a + i, a + half + i] = 1.0
        return m

    cg, sg = rope(HD)
    cm, sm = rope(ROPE_D)
    cos_m, sin_m = np.ones((P, T), np.float32), np.zeros((P, T), np.float32)
    cos_m[NOPE:MQK], sin_m[NOPE:MQK] = np.tile(cm, (2, 1)), np.tile(sm, (2, 1))
    t = np.arange(T)
    count = [np.minimum(t + w // 2, T) - np.maximum(t - w // 2, 0) for w in WINDOWS]
    inv_count = (1.0 / np.array(count)).astype(np.float32)
    pool = np.concatenate([np.repeat(inv_count[2 * a:2 * a + 2], HD, axis=0) for a in range(2)], axis=1)
    return {"cos_g": np.tile(cg, (4, 1)), "sin_g": np.tile(sg, (4, 1)), "cos_m": cos_m, "sin_m": sin_m,
            "rot_g": rotation((0, HD), HD // 2), "rot_m": rotation((NOPE,), ROPE_D // 2),
            "pool": pool}


SECOND_RISES = {
    "second_turned": 2, "second_placed": 15, "mod_ready": 3, "x2_ready": 32, "sq2_ready": 16,
    "ss2_done": 4, "std2_ready": 4, "scaled": 36, "h2_ready": 32, "acc2_zero": 2, "relu_done": 32,
    "act2_ready": 32, "in_evac": 16, "nrm_act": 5, "nrm_sum": 14, "nrm_dve": 14, "rot_done": 13,
    "mla_done": 14, "mla_evac": 16, "pool_dve": 17, "pool_done": 1, "sc2_done": 48, "sm2_max": 96,
    "sm2_norm": 96, "sm2_act": 48, "pt2_done": 48, "pt2_ready": 48, "av2_done": 48, "av2_out": 12,
    "placed_act": 5, "mla_sq": 12, "mla_std": 12, "mla_dve": 60
}


def build_second(nc, ctx, a, scratch, store, out):
    PER = SECOND_RISES
    signals = []

    def sb(name, shape):
        return ctx.enter_context(nc.sbuf_tensor(name, shape, F32))

    def sig(name):
        s = Signal(ctx, nc, name, PER.get(name, 0))
        signals.append(s)
        return s

    eps, psum = store["eps"], store["ps"]
    ps = [psum[:, i, :] for i in range(8)]
    ident, ones, head_ones = (store["cst"][n] for n in ("ident", "ones", "head_ones"))
    w = a
    ring = sb("ring2", [P, RING2, SLOT])
    xs = [sb("xc_sb", [P, KD, T]), store["x"]]
    h = sb("h2_sb", [P, KD, TT])
    n_const = sum(c.shape[1] for c in constants2().values())
    cbuf = sb("consts2_sb", [P, n_const])
    cst, _at = {}, 0
    for name, c in constants2().items():
        cst[name] = cbuf[:, _at:_at + c.shape[1]]
        _at += c.shape[1]
    par = sb("par2", [P, DEPTH, NPAR2])
    mod = sb("mod", [P, 2, MODS])
    scl = sb("scl", [P, 2, 2, KD])
    qk = sb("qk", [P, 4, TT])
    ksw = sb("ksw", [P, TT])
    vg = sb("vg", [P, 4, P])
    cc = sb("cc", [P, 3, TT])
    sqc = sb("sqc", [P, 3, TT])
    sqk = sb("sqk", [P, 4, TT])
    qm, km = sb("qm", [P, MH, TT]), sb("km", [P, MH, TT])
    sqm = sb("sqm", [P, 2, TT])
    vm = sb("vm", [P, 4, MH * HD])
    pin = sb("pin", [P, 2, TT])
    wp = sb("wp", [P, 2, DEPTH, HD])
    std = sb("std2", [P, 2, T])
    prob, probT = sb("prob2", [P, 2, 512]), sb("probT2", [P, 2, 512])
    smx, ssum = sb("smx2", [P, 2]), sb("ssum2", [P, 2])
    csum = sqk[:, :, :].rearrange("p a t -> p (a t)")[:, 0:4 * (T + 2 * EDGE + 1)].rearrange(
        "p (s t) -> p s t", s=4)
    pooled = sqc[:, 0:2, :]
    squares = [b[:, :, :].rearrange("p a (c t) -> p (a c) t", c=2) for b in (sqk, qk)]
    rot = sqc[:, 0:2, :].rearrange("p a t -> p (a t)")

    in_loaded, par_loaded = sig("second_loaded"), sig("param2_loaded")
    turned, placed = sig("second_turned"), sig("second_placed")
    w_loaded = [sig(f"v_loaded{s}") for s in range(RING2)]
    w_used = [sig(f"v_used{s}") for s in range(RING2)]
    mod_ready = sig("mod_ready")
    x_ready, sq_ready, ss_done = sig("x2_ready"), sig("sq2_ready"), sig("ss2_done")
    std_ready, scaled, h_ready = sig("std2_ready"), sig("scaled"), sig("h2_ready")
    acc_zero, relu_done, act_ready = sig("acc2_zero"), sig("relu_done"), sig("act2_ready")
    in_evac = sig("in_evac")
    nrm_act = sig("nrm_act")
    nrm_sum = sig("nrm_sum")
    nrm_dve = sig("nrm_dve")
    rot_done = sig("rot_done")
    mla_done = sig("mla_done")
    mla_evac = sig("mla_evac")
    pool_dve, pool_done = sig("pool_dve"), sig("pool_done")
    sc_done, sm_max, sm_norm, sm_act = sig("sc2_done"), sig("sm2_max"), sig("sm2_norm"), sig("sm2_act")
    pt_done, pt_ready, av_done, av_out = sig("pt2_done"), sig("pt2_ready"), sig("av2_done"), sig("av2_out")
    stored = sig("stored")

    def streams(i):
        return (CTX, LAT) if i < DEPTH - 1 else (LAT,)

    def cols(s, t=0, n=T):
        return slice(s * T + t, s * T + t + n)

    def pcol(i, name, n=0, rows=P):
        c = PARAM2_AT[name] + n
        return par[0:rows, i, c:c + 1]

    def place(name):
        n = SECOND_AT[name]
        return n % RING2, n // RING2

    def units(i):
        return [(s, hd, t) for s in streams(i) for hd in range(GQ + MH) for t in range(2)]

    def layer_ends(i):
        for x in signals:
            if i == 0 and not x.layer0:
                x.layer0 = x.n

    def unit_base(i):
        return len(units(0)) if i else 0

    def sync_program(sp):
        def load(name, view, src):
            s, use = place(name)
            if use:
                sp.wait_ge(w_used[s].sem, use)
            sp.dma_start(view(ring[:, s, :]), src).then_inc(w_loaded[s].sem, 16)

        def k_view(k, n):
            return lambda r: r[:, 0:k * n].rearrange("p (k n) -> p k n", k=k)

        def col_src(m, i, c, n):
            return m[i, :, c:c + n].rearrange("(k p) n -> p k n", p=P)

        for i in range(DEPTH):
            for c in range(2):
                for t in range(MOD_THIRDS):
                    load(("mod", i, c, t), lambda r: r,
                         scratch["mod"][i, :, c, t * SLOT:(t + 1) * SLOT])
            for j, c, n in IN_TILES:
                load(("in", i, j), k_view(KD, n), col_src(w["w_in_2"], i, c, n))
            load(("uq", i), k_view(2, MH * MQK), col_src(w["w_uq_2"], i, 0, MH * MQK))
            load(("ukv", i), lambda r: r[:, 0:MH * P], w["w_ukv_2"][i])
            for j in range(LIN_TILES):
                load(("out", i, j), k_view(KD, BLK), col_src(w["w_out_2"], i, j * BLK, BLK))
            for c in streams(i):
                n0 = SECOND_AT[("mlp1", i, c, 0)]
                with sp.Fori(0, MLP_STEPS // 4) as j:
                    for q in range(4):
                        for r in range(2):
                            n, at = n0 + 2 * q + r, j * (4 * BLK) + q * BLK
                            s = n % RING2
                            sp.wait_ge(w_used[s].sem, j + n // RING2)
                            if r == 0:
                                src = w["w_mlp1_2"][i, :, bass.ds(at, BLK)].rearrange("(k p) n -> p k n", p=P)
                            else:
                                src = w["w_mlp2_2"][i, bass.ds(at, BLK), :].rearrange("(k p) n -> p k n", p=P)
                            sp.dma_start(k_view(KD if r == 0 else 2, BLK if r == 0 else D)(ring[:, s, :]),
                                         src).then_inc(w_loaded[s].sem, 16)

    def tensor_program(pe):
        mm = nc.tensor.matmul

        def loaded(name):
            s, use = place(name)
            pe.wait_ge(w_loaded[s].sem, 16 * (use + 1))
            return ring[:, s, :], w_used[s]

        def norm(i, n, which):
            for s in which:
                for k in range(KD):
                    if k % 2 == 0:
                        pe.wait_ge(*sq_ready.at(i, norm_at(i, n, s) * 4 + k // 2 + 1))
                    last = mm(ps[2 + s][:, 0:T], ones, squares[s][:, k, :], start=(k == 0), stop=(k == KD - 1))
                last.then_inc(*ss_done.up())

        def mlp(i, c):
            n0, base = SECOND_AT[("mlp1", i, c, 0)], MLP_STEPS * streams(i).index(c)

            def up(j, q, step):
                n = n0 + 2 * q
                s = n % RING2
                pe.wait_ge(w_loaded[s].sem, (j + n // RING2 + 1) * 16)
                if not (isinstance(step, int) and step == 0):
                    pe.wait_ge(*relu_done.at(i, step + (base - 1)))
                wt = ring[:, s, :].rearrange("p (k n) -> p k n", k=KD)
                for m in range(2):
                    for k in range(KD):
                        last = mm(ps[4 + q % 2][:, m * T:(m + 1) * T], wt[:, k, m * P:(m + 1) * P],
                                  h[:, k, cols(c)], start=(k == 0), stop=(k == KD - 1))
                last.then_inc(w_used[s].sem, 1)

            def down(j, q, step):
                n = n0 + 2 * q + 1
                s = n % RING2
                pe.wait_ge(w_loaded[s].sem, (j + n // RING2 + 1) * 16)
                pe.wait_ge(*act_ready.at(i, step + (base + 1)))
                wt = ring[:, s, :].rearrange("p (k n) -> p k n", k=2)
                for k in range(2):
                    for m in range(KD):
                        last = mm(ps[m // 2][:, (m % 2) * T:(m % 2 + 1) * T], wt[:, k, m * P:(m + 1) * P],
                                  probT[:, q % 2, k * T:(k + 1) * T], start=False, stop=False,
                                  skip_group_check=True)
                last.then_inc(w_used[s].sem, 1)

            n_groups = MLP_STEPS // 4
            up(0, 0, 0)
            pe.wait_ge(*acc_zero.at(i, streams(i).index(c) + 1))
            with pe.Fori(0, n_groups - 1) as j:
                for q in range(4):
                    up(j + (q + 1) // 4, (q + 1) % 4, j * 4 + (q + 1))
                    down(j, q, j * 4 + q)
            for q in range(4):
                if q < 3:
                    up(n_groups - 1, q + 1, MLP_STEPS - 4 + q + 1)
                down(n_groups - 1, q, MLP_STEPS - 4 + q)

        pe.wait_ge(*placed.at(0, 1))
        pe.wait_ge(in_loaded.sem, 16 * 2)
        pe.wait_ge(par_loaded.sem, 16 * N_PARAM2)
        for i in range(DEPTH):
            nc.tensor.transpose(ps[0][:, i * P:i * P + NPAR2], p_rows2[:, i * P:(i + 1) * P],
                                ident[0:NPAR2, 0:NPAR2])
        for t in range(2):
            for k in range(KD):
                b, at = 2 + k // 2, (k % 2) * T + t * P
                last = nc.tensor.transpose(ps[b][:, at:at + P], c_tok[:, t, k * P:(k + 1) * P], ident)
        last.then_inc(*turned.up())
        pe.wait_ge(*placed.at(0, 6))
        for k in range(KD):
            if k % 2 == 0:
                pe.wait_ge(*placed_act.at(0, k // 2 + 1))
            last = mm(ps[6][:, 0:T], ones, h[:, k, cols(LAT)], start=(k == 0), stop=(k == KD - 1))
        last.then_inc(*turned.up())

        for i in range(DEPTH):
            ub = unit_base(i)
            if i:
                pe.wait_ge(*x_ready.at(i, 0))
            for c in range(2):
                for t in range(MOD_THIRDS):
                    r, used = loaded(("mod", i, c, t))
                    for n in range(SLOT // P):
                        col = c * MODS + t * (SLOT // P) + n
                        last = mm(ps[0][:, col:col + 1], r[:, n * P:(n + 1) * P], ones[:, 0:1],
                                  start=True, stop=True)
                    last.then_inc(used.sem, 1)
            norm(i, 0, (CTX, LAT))
            pe.wait_ge(*h_ready.at(i, 2 * KD))
            for n, (j, _, width) in enumerate(IN_TILES):
                r, used = loaded(("in", i, j))
                wt = r[:, 0:KD * width].rearrange("p (k n) -> p k n", k=KD)
                if n >= 2:
                    pe.wait_ge(*in_evac.at(i, 2 * (n - 1)))
                bank = 4 + 2 * (n % 2)
                if j == 2:
                    for t in range(4):
                        for k in range(KD):
                            mm(ps[bank][:, t * P:(t + 1) * P], h[:, k, t * P:(t + 1) * P], wt[:, k, 0:P],
                               start=(k == 0), stop=(k == KD - 1))
                    for k in range(KD):
                        last = mm(ps[bank + 1], wt[:, k, P:2 * P], h[:, k, :], start=(k == 0), stop=(k == KD - 1))
                elif j == 4:
                    for k in range(KD):
                        last = mm(ps[bank][NOPE:MQK, :], wt[:, k, :], h[:, k, :], start=(k == 0), stop=(k == KD - 1))
                else:
                    for m in range(2):
                        for k in range(KD):
                            last = mm(ps[bank + m], wt[:, k, m * P:(m + 1) * P], h[:, k, :],
                                      start=(k == 0), stop=(k == KD - 1))
                last.then_inc(used.sem, 1)
                if n == 2:
                    pe.wait_ge(*nrm_act.at(i, 1))
                    pe.wait_ge(*mod_ready.at(i, 1))
                    for k in range(2):
                        mm(ps[0], ones, sqc[:, k, :], start=(k == 0), stop=(k == 1))
                    mm(ps[1], ones, sqc[:, 2, :], start=True, stop=True).then_inc(*nrm_sum.up())
            pe.wait_ge(*nrm_act.at(i, NRM_ACT_QK_SQ))
            for m in range(4):
                last = mm(ps[m], head_ones, sqk[:, m, :], start=True, stop=True)
            last.then_inc(*nrm_sum.up())
            pe.wait_ge(*in_evac.at(i, IN_EVACS))
            pe.wait_ge(*nrm_dve.at(i, NRM_DVE_C))
            ruq, used_q = loaded(("uq", i))
            wq = ruq[:, 0:2 * MH * MQK].rearrange("p (k n) -> p k n", k=2)
            rkv, used_kv = loaded(("ukv", i))
            wkv = rkv[:, 0:MH * P].rearrange("p (m n) -> p m n", m=MH)
            for u in range(2 * MH + 2):
                if u < 2 * MH:
                    if u >= 4:
                        pe.wait_ge(*mla_evac.at(i, u - 3))
                    bank = 4 + u % 4
                    if u < MH:
                        for k in range(2):
                            last = mm(ps[bank][0:MQK, :], wq[:, k, u * MQK:(u + 1) * MQK], cc[:, k, :],
                                      start=(k == 0), stop=(k == 1))
                    else:
                        last = mm(ps[bank][0:NOPE, :], wkv[:, u - MH, 0:NOPE], cc[:, 2, :],
                                  start=True, stop=True)
                    last.then_inc(*((used_q.sem, 1) if u == MH - 1 else mla_done.up()))
                if u == 0:
                    pe.wait_ge(*nrm_dve.at(i, NRM_DVE_QK))
                    for m in range(4):
                        last = mm(ps[2 + m // 2][:, (m % 2) * T:(m % 2 + 1) * T], cst["rot_g"],
                                  qk[:, m, cols(LAT)], start=True, stop=True)
                    last.then_inc(*rot_done.up())
                if 1 <= u <= 2 * MH:
                    b = (u - 1) % 2
                    pe.wait_ge(*mla_sq.at(i, u))
                    if u >= 3:
                        pe.wait_ge(*mla_std.at(i, u - 2))
                    mm(ps[b][0:MQK, :], ones[0:MQK, 0:MQK], sqm[0:MQK, b, :], start=True, stop=True
                       ).then_inc(*nrm_sum.up())
                if u >= 2:
                    b = (u - 2) % 2
                    src = (qm if u - 2 < MH else km)[0:MQK, (u - 2) % MH, cols(LAT)]
                    pe.wait_ge(*nrm_dve.at(i, NRM_DVE_ROPE))
                    pe.wait_ge(*mla_dve.at(i, MLA_NORMED(u - 2)))
                    mm(ps[2 + b][0:MQK, 0:T], cst["rot_m"][0:MQK, 0:MQK], src, start=True, stop=True
                       ).then_inc(*rot_done.up())
            for t in range(4):
                pe.wait_ge(*mla_evac.at(i, 2 * MH - 3 + t))
                last = mm(ps[4 + t][:, 0:MH * HD], cc[:, 2, t * P:(t + 1) * P], wkv[:, :, NOPE:P],
                          start=True, stop=True)
                last.then_inc(*((used_kv.sem, 1) if t == 3 else mla_done.up()))
            pe.wait_ge(*pool_dve.at(i, POOL_DVE))
            pe.wait_ge(*mla_dve.at(i, MLA_DVE))
            pe.wait_ge(*nrm_dve.at(i, NRM_DVE))
            for g in range(4):
                hi = slice((g % 2) * HD, (g % 2 + 1) * HD)
                last = mm(ps[g][hi, :], wp[hi, g // 2, i, :], pooled[hi, g // 2, :], start=True, stop=True)
            last.then_inc(*pool_done.up())
            pe.wait_ge(*pool_dve.at(i, POOL_DVE + 4))
            pe.wait_ge(*mla_evac.at(i, 2 * MH + 4))

            us = units(i)

            def scores(n):
                s, hd, t = us[n]
                nk = T if s == CTX else TT
                if n >= 2:
                    pe.wait_ge(*sm_act.at(0, ub + n - 1))
                q = cols(s, t * P, P)
                if hd < GQ:
                    hi = slice((hd % 2) * HD, (hd % 2 + 1) * HD)
                    same = hd % 2 == hd // (GQ // KVH)
                    key = qk[hi, 3, 0:nk] if same else ksw[hi, 0:nk]
                    last = mm(ps[n % 2][:, 0:nk], qk[hi, hd // 2, q], key, start=True, stop=True)
                else:
                    last = mm(ps[n % 2][:, 0:nk], qm[0:MQK, hd - GQ, q], km[0:MQK, hd - GQ, 0:nk],
                              start=True, stop=True)
                last.then_inc(*sc_done.up())

            def turn(n):
                s, hd, t = us[n]
                pe.wait_ge(*sm_norm.at(0, 2 * (ub + n + 1)))
                if n >= 2:
                    pe.wait_ge(*pt_ready.at(0, ub + n - 1))
                for k in range((T if s == CTX else TT) // P):
                    last = nc.tensor.transpose(ps[2 + n % 2][:, k * P:(k + 1) * P],
                                               prob[:, n % 2, k * P:(k + 1) * P], ident)
                last.then_inc(*pt_done.up())

            def attend(n):
                s, hd, t = us[n]
                pe.wait_ge(*pt_ready.at(0, ub + n + 1))
                pair = n // 4
                if n % 4 == 0 and pair >= 2:
                    pe.wait_ge(*av_out.at(0, ub // 4 + pair - 1))
                hi = slice((hd % 2) * HD, (hd % 2 + 1) * HD)
                nk = (T if s == CTX else TT) // P
                for k in range(nk):
                    kv = hd // (GQ // KVH)
                    v = vg[:, k, kv * HD:(kv + 1) * HD] if hd < GQ else vm[:, k, (hd - GQ) * HD:(hd - GQ + 1) * HD]
                    last = mm(ps[6 + pair % 2][hi, t * P:(t + 1) * P], v, probT[:, n % 2, k * P:(k + 1) * P],
                              start=(k == 0), stop=(k == nk - 1))
                last.then_inc(*av_done.up())

            for n in range(len(us) + 2):
                if n < len(us):
                    scores(n)
                if 1 <= n <= len(us):
                    turn(n - 1)
                if n >= 2:
                    attend(n - 2)
            pe.wait_ge(*av_out.at(0, (ub + len(us)) // 4))
            lo = 0 if i < DEPTH - 1 else T
            for j in range(LIN_TILES):
                r, used = loaded(("out", i, j))
                wt = r.rearrange("p (k n) -> p k n", k=KD)
                if j >= 2:
                    pe.wait_ge(*x_ready.at(i, 2 * len(streams(i)) * (j - 1)))
                for m in range(2):
                    for k in range(KD):
                        last = mm(ps[4 + 2 * (j % 2) + m][:, lo:TT], wt[:, k, m * P:(m + 1) * P], h[:, k, lo:TT],
                                  start=(k == 0), stop=(k == KD - 1))
                last.then_inc(used.sem, 1)
            norm(i, 1, streams(i))
            pe.wait_ge(*h_ready.at(i, 2 * KD + KD * len(streams(i))))
            for c in streams(i):
                mlp(i, c)
            layer_ends(i)
        pe.wait_ge(*x_ready.at(1, X_LAYER1))
        for t in range(2):
            for k in range(KD):
                last = nc.tensor.transpose(ps[4 + 2 * t + k // 4][:, (k % 4) * P:(k % 4 + 1) * P],
                                           xs[LAT][:, k, t * P:(t + 1) * P], ident)
            last.then_inc(*turned.up())

    def scalar_program(act):
        go = nc.scalar.activation

        def norm(i, n, which):
            for s in which:
                for q in range(4):
                    act.wait_ge(*x_ready.at(*x_needed(i, n, s, q)))
                    go(squares[s][:, 2 * q:2 * q + 2, :], xs[s][:, 2 * q:2 * q + 2, :], ACT.Square
                       ).then_inc(*sq_ready.up())
            for s in which:
                act.wait_ge(*ss_done.at(i, norm_at(i, n, s) + 1))
                go(std[:, s, :], ps[2 + s][:, 0:T], ACT.Sqrt, bias=eps[:, 0:1], scale=1.0 / D
                   ).then_inc(*std_ready.up())
            for s in which:
                for k in range(KD):
                    act.wait_ge(*scaled.at(i, 9 * norm_at(i, n, s) + k + 2))
                    shift = mod[:, s, n * 3 * KD + k:n * 3 * KD + k + 1]
                    go(h[:, k, cols(s)], h[:, k, cols(s)], ACT.Identity, bias=shift).then_inc(*h_ready.up())

        def mlp(i, c):
            n0, base = SECOND_AT[("mlp1", i, c, 0)], MLP_STEPS * streams(i).index(c)

            def relu(j, q, step):
                n = n0 + 2 * q
                act.wait_ge(w_used[n % RING2].sem, j + (n // RING2 + 1))
                if not isinstance(step, int) or step >= 1:
                    act.wait_ge(*act_ready.at(i, step + (base - 1)))
                go(prob[:, q % 2, :], ps[4 + q % 2], ACT.Relu).then_inc(relu_done.sem, 1)

            for q in range(4):
                relu(0, q, q)
            with act.Fori(1, MLP_STEPS // 4) as j:
                for q in range(4):
                    relu(j, q, j * 4 + q)
            relu_done.n += MLP_STEPS

        act.wait_ge(*placed.at(0, 1))
        for q in range(4):
            go(h[:, 2 * q:2 * q + 2, cols(LAT)], xs[LAT][:, 2 * q:2 * q + 2, :], ACT.Square
               ).then_inc(*placed_act.up())
        act.wait_ge(*turned.at(0, 2))
        go(std[:, LAT, :], ps[6][:, 0:T], ACT.Sqrt, bias=eps[:, 0:1], scale=1.0 / D).then_inc(*placed_act.up())
        act.wait_ge(*placed.at(0, 15))

        for i in range(DEPTH):
            ub = unit_base(i)
            norm(i, 0, (CTX, LAT))
            for n, (j, _, width) in enumerate(IN_TILES):
                s, use = place(("in", i, j))
                act.wait_ge(w_used[s].sem, use + 1)
                bank = 4 + 2 * (n % 2)
                if j == 2:
                    go(vg[:, :, :], ps[bank].rearrange("p (t n) -> p t n", t=4), ACT.Copy).then_inc(*in_evac.up())
                    go(cc[:, 0, :], ps[bank + 1], ACT.Copy).then_inc(*in_evac.up())
                elif j == 3:
                    for m in range(2):
                        go(cc[:, 1 + m, :], ps[bank + m], ACT.Copy).then_inc(*in_evac.up())
                    act.wait_ge(*in_evac.now(0))
                    go(sqc[:, :, :], cc[:, :, :], ACT.Square).then_inc(*nrm_act.up())
                elif j in (0, 1):
                    for m in range(2):
                        go(qk[:, 2 * j + m, :], ps[bank + m], ACT.Copy).then_inc(*in_evac.up())
                elif j == 4:
                    for hd in range(MH):
                        go(km[NOPE:MQK, hd, :], ps[bank][NOPE:MQK, :], ACT.Copy).then_inc(*in_evac.up())
                else:
                    for m in range(2):
                        go(pin[:, m, :], ps[bank + m], ACT.Copy).then_inc(*in_evac.up())
                if n == 3:
                    act.wait_ge(*nrm_sum.at(i, 1))
                    for m, width in ((0, 2 * P), (1, P)):
                        go(sqc[:, m, :], ps[m], ACT.Sqrt, bias=eps[:, 0:1], scale=1.0 / width
                           ).then_inc(*nrm_act.up())
            act.wait_ge(*in_evac.now(0))
            go(sqk[:, :, :], qk[:, :, :], ACT.Square).then_inc(*nrm_act.up())
            act.wait_ge(*nrm_sum.at(i, 2))
            go(sqk[:, :, :], psum[:, 0:4, :], ACT.Sqrt, bias=eps[:, 0:1], scale=1.0 / HD).then_inc(*nrm_act.up())

            def mla_ready(u):
                if u < MH - 1:
                    act.wait_ge(*mla_done.at(i, u + 1))
                elif u == MH - 1:
                    s, use = place(("uq", i))
                    act.wait_ge(w_used[s].sem, use + 1)
                else:
                    act.wait_ge(*mla_done.at(i, u))

            for u in range(2 * MH + 1):
                if u < 2 * MH:
                    b = u % 2
                    mla_ready(u)
                    dst, rows = (qm, MQK) if u < MH else (km, NOPE)
                    go(dst[0:rows, u % MH, :], ps[4 + u % 4][0:rows, :], ACT.Copy).then_inc(*mla_evac.up())
                    act.wait_ge(*mla_evac.now(0))
                    if u >= 2:
                        act.wait_ge(*mla_dve.at(i, MLA_NORMED(u - 2)))
                    go(sqm[0:MQK, b, :], dst[0:MQK, u % MH, :], ACT.Square).then_inc(*mla_sq.up())
                if u >= 1:
                    b = (u - 1) % 2
                    act.wait_ge(*nrm_sum.at(i, 2 + u))
                    go(sqm[0:MQK, b, :], ps[b][0:MQK, :], ACT.Sqrt, bias=eps[0:MQK, 0:1], scale=1.0 / MQK
                       ).then_inc(*mla_std.up())
            for t in range(4):
                if t < 3:
                    act.wait_ge(*mla_done.at(i, 2 * MH - 1 + t + 1))
                else:
                    s, use = place(("ukv", i))
                    act.wait_ge(w_used[s].sem, use + 1)
                go(vm[:, t, :], ps[4 + t][:, 0:MH * HD], ACT.Copy).then_inc(*mla_evac.up())

            us = units(i)
            for n in range(len(us) + 1):
                if n < len(us):
                    s, hd, t = us[n]
                    nk = T if s == CTX else TT
                    act.wait_ge(*sm_max.at(0, 2 * (ub + n + 1)))
                    if n >= 2:
                        act.wait_ge(*pt_done.at(0, ub + n - 1))
                    go(prob[:, n % 2, 0:nk], ps[n % 2][:, 0:nk], ACT.Exp, bias=smx[:, n % 2:n % 2 + 1],
                       scale=(HD if hd < GQ else MQK) ** -0.5, accum_out=ssum[:, n % 2:n % 2 + 1]
                       ).then_inc(*sm_act.up())
                if n >= 1:
                    nk = T if us[n - 1][0] == CTX else TT
                    b = (n - 1) % 2
                    act.wait_ge(*pt_done.at(0, ub + n))
                    if n >= 3:
                        act.wait_ge(*av_done.at(0, ub + n - 2))
                    go(probT[:, b, 0:nk], ps[2 + b][:, 0:nk], ACT.Copy).then_inc(*pt_ready.up())
            norm(i, 1, streams(i))
            for c in streams(i):
                mlp(i, c)
            layer_ends(i)

    def vector_program(dve):
        v = nc.vector

        def step(i, instruction, signal):
            instruction.then_inc(*signal.up())
            dve.wait_ge(*signal.now(0))

        def norm(i, n, which):
            for s in which:
                dve.wait_ge(*std_ready.at(i, norm_at(i, n, s) + 1))
                step(i, v.reciprocal(std[:, s, :], std[:, s, :]), scaled)
                for k in range(KD):
                    v.scalar_tensor_tensor(h[:, k, cols(s)], xs[s][:, k, :], scl[:, s, n, k:k + 1],
                                           std[:, s, :], ALU.mult, ALU.mult).then_inc(*scaled.up())

        v.memset(p_rows2[:, :], 0.0).then_inc(*placed.up())
        dve.wait_ge(*turned.at(0, 1))
        v.tensor_copy(par[:, :, :], ps[0][:, 0:DEPTH * P].rearrange("p (l c) -> p l c", l=DEPTH)[:, :, 0:NPAR2]
                      ).then_inc(*placed.up())
        for q in range(4):
            v.tensor_copy(xs[CTX][:, 2 * q:2 * q + 2, :], ps[2 + q].rearrange("p (m t) -> p m t", m=2)
                          ).then_inc(*placed.up())
        dve.wait_ge(*placed_act.at(0, 5))
        step(0, v.reciprocal(std[:, LAT, :], std[:, LAT, :]), placed)
        for k in range(KD):
            v.scalar_tensor_tensor(xs[LAT][:, k, :], xs[LAT][:, k, :], store["final_g"][:, k:k + 1],
                                   std[:, LAT, :], ALU.mult, ALU.mult).then_inc(*placed.up())
        dve.wait_ge(*placed.now(0))

        for i in range(DEPTH):
            ub = unit_base(i)
            s_, use = place(("mod", i, 1, MOD_THIRDS - 1))
            dve.wait_ge(w_used[s_].sem, use + 1)
            bias = PARAM2_AT["b_mod"]
            step(i, v.tensor_tensor(mod[:, :, :], ps[0][:, 0:2 * MODS].rearrange("p (s n) -> p s n", s=2),
                                    par[:, i, bias:bias + MODS].rearrange("p (o n) -> p o n", o=1
                                                                          ).to_broadcast([P, 2, MODS]),
                                    ALU.add), mod_ready)
            for n, gain in ((0, "g_norm1"), (1, "g_norm2")):
                g = PARAM2_AT[gain]
                step(i, v.scalar_tensor_tensor(
                    scl[:, :, n, :], mod[:, :, (3 * n + 1) * KD:(3 * n + 2) * KD], 1.0,
                    par[:, i, g:g + KD].rearrange("p (o n) -> p o n", o=1).to_broadcast([P, 2, KD]),
                    ALU.add, ALU.mult), mod_ready)
            norm(i, 0, (CTX, LAT))
            dve.wait_ge(*nrm_act.at(i, 3))
            step(i, v.reciprocal(sqc[:, 0:2, :], sqc[:, 0:2, :]), nrm_dve)
            for m, (name, at, r) in enumerate((("g_cq", 0, 0), ("g_cq", 1, 0), ("g_ckv", 0, 1))):
                step(i, v.scalar_tensor_tensor(cc[:, m, :], cc[:, m, :], pcol(i, name, at), sqc[:, r, :],
                                               ALU.mult, ALU.mult), nrm_dve)
            dve.wait_ge(*nrm_act.at(i, NRM_ACT_QK_STD))
            step(i, v.reciprocal(sqk[:, :, :], sqk[:, :, :]), nrm_dve)
            for m in range(4):
                step(i, v.scalar_tensor_tensor(qk[:, m, :], qk[:, m, :],
                                               pcol(i, "g_q_gqa" if m < 3 else "g_k_gqa"), sqk[:, m, :],
                                               ALU.mult, ALU.mult), nrm_dve)
            wide = lambda c: cst[c].rearrange("p (o t) -> p o t", o=1).to_broadcast([P, 4, T])
            rot4 = rot.rearrange("p (m t) -> p m t", m=4)
            dve.wait_ge(*rot_done.at(i, 1))
            step(i, v.tensor_tensor(rot4, psum[:, 2:4, :].rearrange("p b (m t) -> p (b m) t", m=2),
                                    wide("sin_g"), ALU.mult), nrm_dve)
            step(i, v.tensor_tensor(qk[:, :, cols(LAT)], qk[:, :, cols(LAT)], wide("cos_g"), ALU.mult), nrm_dve)
            step(i, v.tensor_tensor(qk[:, :, cols(LAT)], qk[:, :, cols(LAT)], rot4, ALU.add), nrm_dve)
            for e in range(2):
                step(i, v.tensor_copy(ksw[(1 - e) * HD:(2 - e) * HD, :], qk[e * HD:(e + 1) * HD, 3, :]), nrm_dve)
            dve.wait_ge(*in_evac.at(i, IN_EVACS))
            step(i, v.memset(csum, 0.0), pool_dve)
            first = EDGE + 1
            for m in range(2):
                for s in range(2):
                    g = 2 * m + s
                    step(i, v.tensor_tensor_scan(csum[:, g, first:first + T], ones_row, pin[:, m, cols(s)],
                                                 0.0, ALU.mult, ALU.add), pool_dve)
            step(i, v.tensor_copy(csum[:, :, first + T:], csum[:, :, first + T - 1:first + T].to_broadcast(
                [P, 4, EDGE])), pool_dve)
            for g, wd in enumerate(WINDOWS):
                hi, m = slice((g % 2) * HD, (g % 2 + 1) * HD), g // 2
                step(i, v.tensor_tensor(pooled[hi, m, :].rearrange("p (s t) -> p s t", s=2),
                                        csum[hi, 2 * m:2 * m + 2, EDGE + wd // 2:EDGE + wd // 2 + T],
                                        csum[hi, 2 * m:2 * m + 2, EDGE - wd // 2:EDGE - wd // 2 + T],
                                        ALU.subtract), pool_dve)
            for m in range(2):
                view = pooled[:, m, :].rearrange("p (s t) -> p s t", s=2)
                step(i, v.tensor_tensor(view, view, cst["pool"][:, m * T:(m + 1) * T].rearrange(
                    "p (o t) -> p o t", o=1).to_broadcast([P, 2, T]), ALU.mult), pool_dve)
            step(i, v.tensor_tensor(pooled, pooled, pin[:, :, :], ALU.subtract), pool_dve)
            for u in range(2 * MH + 1):
                if u < 2 * MH:
                    b, buf = u % 2, qm if u < MH else km
                    dve.wait_ge(*mla_std.at(i, u + 1))
                    step(i, v.reciprocal(sqm[0:MQK, b, :], sqm[0:MQK, b, :]), mla_dve)
                    step(i, v.scalar_tensor_tensor(buf[0:MQK, u % MH, :], buf[0:MQK, u % MH, :],
                                                   pcol(i, "g_q_mla" if u < MH else "g_k_mla", rows=MQK),
                                                   sqm[0:MQK, b, :], ALU.mult, ALU.mult), mla_dve)
                if u >= 1:
                    p_, buf = u - 1, qm if u - 1 < MH else km
                    b, lat = p_ % 2, buf[0:MQK, p_ % MH, cols(LAT)]
                    dve.wait_ge(*rot_done.at(i, 2 + p_))
                    step(i, v.tensor_tensor(rotm, ps[2 + b][0:MQK, 0:T], cst["sin_m"][0:MQK, :], ALU.mult),
                         mla_dve)
                    step(i, v.tensor_tensor(lat, lat, cst["cos_m"][0:MQK, :], ALU.mult), mla_dve)
                    step(i, v.tensor_tensor(lat, lat, rotm, ALU.add), mla_dve)
            dve.wait_ge(*pool_done.at(i, 1))
            for g in range(4):
                hi = slice((g % 2) * HD, (g % 2 + 1) * HD)
                step(i, v.tensor_scalar(h[hi, 6 + g // 2, :], ps[g][hi, :], pcol_part(i, "ls_pool", g // 2, hi),
                                        None, ALU.mult), pool_dve)

            us = units(i)
            for n in range(len(us) + 2):
                if n < len(us):
                    s, hd, t = us[n]
                    nk = T if s == CTX else TT
                    dve.wait_ge(*sc_done.at(0, ub + n + 1))
                    m1 = smx[:, n % 2:n % 2 + 1]
                    step(0, v.tensor_reduce(m1, ps[n % 2][:, 0:nk], AX_X, ALU.max), sm_max)
                    step(0, v.tensor_scalar(m1, m1, -((HD if hd < GQ else MQK) ** -0.5), None, ALU.mult), sm_max)
                if 1 <= n <= len(us):
                    b = (n - 1) % 2
                    nk = T if us[n - 1][0] == CTX else TT
                    dve.wait_ge(*sm_act.at(0, ub + n))
                    step(0, v.reciprocal(ssum[:, b:b + 1], ssum[:, b:b + 1]), sm_norm)
                    step(0, v.tensor_scalar(prob[:, b, 0:nk], prob[:, b, 0:nk], ssum[:, b:b + 1], None,
                                            ALU.mult), sm_norm)
                if n >= 2 and (n - 2) % 4 == 3:
                    s, hd, t = us[n - 2]
                    pair = (n - 2) // 4
                    dve.wait_ge(*av_done.at(0, ub + n - 1))
                    step(0, v.tensor_copy(h[:, hd // 2, cols(s)], ps[6 + pair % 2][:, 0:T]), av_out)
            for j in range(LIN_TILES):
                sl, use = place(("out", i, j))
                dve.wait_ge(w_used[sl].sem, use + 1)
                for m in range(2):
                    f = 2 * j + m
                    for s in streams(i):
                        v.scalar_tensor_tensor(xs[s][:, f, :], ps[4 + 2 * (j % 2) + m][:, cols(s)],
                                               mod[:, s, 2 * KD + f:2 * KD + f + 1], xs[s][:, f, :],
                                               ALU.mult, ALU.add).then_inc(*x_ready.up())
            dve.wait_ge(*x_ready.now(0))
            norm(i, 1, streams(i))
            for c in streams(i):
                n0, base = SECOND_AT[("mlp1", i, c, 0)], MLP_STEPS * streams(i).index(c)
                if i or streams(i).index(c):
                    dve.wait_ge(*x_ready.now(0))
                v.memset(psum[:, 0:4, :], 0.0).then_inc(*acc_zero.up())

                def square(j, q, sq_step):
                    n = n0 + 2 * q + 1
                    if not isinstance(sq_step, int) or sq_step >= 2:
                        back = n0 + 2 * ((q - 2) % 4) + 1
                        dve.wait_ge(w_used[back % RING2].sem, j + (back // RING2 + (1 if q >= 2 else 0)))
                    dve.wait_ge(*relu_done.at(i, sq_step + (base + 1)))
                    v.tensor_tensor(probT[:, q % 2, :], prob[:, q % 2, :], prob[:, q % 2, :], ALU.mult
                                    ).then_inc(act_ready.sem, 1)

                for q in range(4):
                    square(0, q, q)
                with dve.Fori(1, MLP_STEPS // 4) as j:
                    for q in range(4):
                        square(j, q, j * 4 + q)
                act_ready.n += MLP_STEPS
                sl, use = place(("mlp2", i, c, MLP_STEPS - 1))
                dve.wait_ge(w_used[sl].sem, use + 1)
                for f in range(KD):
                    v.scalar_tensor_tensor(xs[c][:, f, :], ps[f // 2][:, (f % 2) * T:(f % 2 + 1) * T],
                                           mod[:, c, 5 * KD + f:5 * KD + f + 1], xs[c][:, f, :],
                                           ALU.mult, ALU.add).then_inc(*x_ready.up())
                dve.wait_ge(*x_ready.now(0))
            layer_ends(i)
        for t in range(2):
            dve.wait_ge(*turned.at(0, 3 + t))
            v.tensor_copy(o_tok[:, t, :], psum[:, 4 + 2 * t:6 + 2 * t, :].rearrange("p b n -> p (b n)")
                          ).then_inc(*placed.up())

    NRM_ACT_QK_SQ, NRM_ACT_QK_STD = 4, 5
    NRM_DVE_C, NRM_DVE_QK, NRM_DVE_ROPE, NRM_DVE = 4, 9, 10, 14
    IN_EVACS = 2 + 2 + 2 + 2 + MH + 2
    POOL_DVE = 1 + 4 + 1 + 4 + 2 + 1
    MLA_DVE = 2 * MH * 5
    X_LAYER1 = 2 * KD
    N_PARAM2 = len(PARAMS2) + 6 + 2 * DEPTH

    def MLA_NORMED(u):
        return 2 * (u + 1) + 3 * max(u - 1, 0)

    def norm_at(i, n, s):
        return s if n == 0 else 2 + streams(i).index(s)

    def x_needed(i, n, s, q):
        if n == 1:
            return i, 2 * len(streams(i)) * (q + 1)
        return (0, 0) if i == 0 else (0, 2 * KD + s * KD + 2 * (q + 1))

    placed_act = sig("placed_act")
    mla_sq, mla_std, mla_dve = sig("mla_sq"), sig("mla_std"), sig("mla_dve")
    p_rows2 = qm[0:NPAR2, 0, :]
    c_tok = sqk[:, :, :].rearrange("p (h a) t -> p h (a t)", h=2)
    o_tok = sqk[:, :, :].rearrange("p (h a) t -> p h (a t)", h=2)
    rotm = probT[0:MQK, 0, 0:T]
    ones_row = sb("ones_row", [P, T])[:, :]

    def pcol_part(i, name, n, hi):
        c = PARAM2_AT[name] + n
        return par[hi, i, c:c + 1]

    block = ctx.enter_context(nc.Block())

    @block.sync
    def _(sp):
        sp.dma_start(cbuf[:, :], w["consts2"]).then_inc(in_loaded.sem, 16)
        sp.dma_start(c_tok, w["ctx_2"].rearrange("o (h p) n -> p (o h) n", p=P)).then_inc(in_loaded.sem, 16)
        sync_program(sp)
        for t in range(2):
            sp.wait_ge(*placed.at(0, 15 + t + 1))
            sp.dma_start(out[0, t * P:(t + 1) * P, :], o_tok[:, t, :]).then_inc(stored.sem, 16)
        sp.wait_ge(stored.sem, 32)

    @block.tensor
    def _(pe):
        tensor_program(pe)

    @block.scalar
    def _(act):
        act.wait_ge(*placed.at(0, 1))
        for name, n in PARAMS2:
            c = PARAM2_AT[name]
            act.dma_start(p_rows2[c:c + n, 0:DEPTH * P].rearrange("c (l p) -> c l p", l=DEPTH),
                          w[name + "_2"].rearrange("l (c p) -> c l p", p=P)).then_inc(par_loaded.sem, 16)
        for name, width, times in (("g_q_gqa", HD, 2), ("g_k_gqa", HD, 2), ("g_q_mla", MQK, 1), ("g_k_mla", MQK, 1)):
            c = PARAM2_AT[name]
            for r in range(times):
                act.dma_start(p_rows2[c:c + 1, 0:DEPTH * P].rearrange("c (l p) -> c l p", l=DEPTH)[
                    :, :, r * width:(r + 1) * width],
                    w[name + "_2"].rearrange("(o l) p -> o l p", o=1)).then_inc(par_loaded.sem, 16)
        for r in range(2):
            for l in range(DEPTH):
                act.dma_start(wp[r * HD:(r + 1) * HD, :, l, :],
                              w["w_pool_2"][l].rearrange("(g r) c d -> r c g d", r=2)[r]
                              ).then_inc(par_loaded.sem, 16)
        scalar_program(act)

    @block.vector
    def _(dve):
        nc.vector.memset(ones_row, 1.0)
        vector_program(dve)

    return signals


INPUTS = [
    "x", "mem", "rel_bias", "final_norm_g", "ffn1_norm_g", "ffn1_w_in", "ffn1_w_out", "mix_norm_g",
    "w_mix_in", "w_mix_out", "rwkv_mu", "rwkv_w0", "rwkv_w_up", "rwkv_a0", "rwkv_a_up",
    "rwkv_g_up", "rwkv_k_k", "rwkv_k_a", "rwkv_r_k", "rwkv_ln_g", "rwkv_ln_b", "xattn_norm_g",
    "mem_norm_g", "xattn_w_q", "xattn_w_kv", "xattn_w_o", "ffn2_norm_g", "ffn2_w_in", "ffn2_w_out",
    "c_2", "ctx_2", "c_ctx_2", "w_mod_2", "b_mod_2", "g_norm1_2", "g_norm2_2", "w_in_2",
    "g_q_gqa_2", "g_k_gqa_2", "g_cq_2", "g_ckv_2", "w_uq_2", "w_ukv_2", "g_q_mla_2", "g_k_mla_2",
    "w_pool_2", "ls_pool_2", "w_out_2", "w_mlp1_2", "w_mlp2_2"
]


def kernel(**inputs):
    import concourse.bacc as bacc
    from concourse.bass_utils import run_bass_kernel_spmd

    nc = bacc.Bacc("TRN2", target_bir_lowering=False, num_devices=1)
    arrays = {name: np.ascontiguousarray(inputs[name]) for name in INPUTS}
    arrays["consts"] = np.concatenate(list(constants().values()), axis=1)
    arrays["consts2"] = np.concatenate(list(constants2().values()), axis=1)
    arrays["onehot"] = rel_bucket_onehot()
    dram = {name: nc.dram_tensor(f"in_{name}", array.shape, F32, kind="ExternalInput").ap()
            for name, array in arrays.items()}
    out = nc.dram_tensor("out", (1, T, D), F32, kind="ExternalOutput").ap()
    program(nc, dram, out)
    result = run_bass_kernel_spmd(nc, [{f"in_{name}": array for name, array in arrays.items()}],
                                  core_ids=[0])
    return result.results[0]["out"]
```

```python
from contextlib import ExitStack

import numpy as np

import concourse.bass as bass
from concourse import mybir

ALU = mybir.AluOpType
ACT = mybir.ActivationFunctionType
F32 = mybir.dt.float32
AX_X = mybir.AxisListType.X

P = 128
T = 256
D = 1024
KD = D // P
DEPTH = 2
EPS = 1e-6

RING = 6
SLOT = 2048
BLK = 256

HD = 64
RW = 512
NPAIR = RW // P
NH = RW // HD
D_FF = 2816
FFN_STEPS = D_FF // BLK
CH = 64
SUB = 16
LNX_EPS = 64e-5
DECAY = float(np.exp(-0.5))
XH = 4
XD = D // XH

MIX_TILES = 13
MIX_ORDER = [6, 2, 3, 4, 5, 0, 1, 7, 8, 9, 10, 11, 12]
KV_TILES, LIN_TILES = 2 * D // BLK, D // BLK


def first_schedule():
    s = [(kind, i) for i in range(FFN_STEPS) for kind in ("ffn1_gate", "ffn1_up", "ffn1_down")]
    s += [("mix_in", j) for j in MIX_ORDER]
    s += [("kv", j) for j in range(KV_TILES)]
    s += [("mix_out", j) for j in range(LIN_TILES)]
    s += [("xq", j) for j in range(LIN_TILES)]
    s += [("xo", j) for j in range(LIN_TILES)]
    s += [(kind, i) for i in range(FFN_STEPS) for kind in ("ffn2_gate", "ffn2_up", "ffn2_down")]
    return s


FIRST = first_schedule()
FIRST_AT = {name: i for i, name in enumerate(FIRST)}
FIRST_USES = [len(range(s, len(FIRST), RING)) for s in range(RING)]

PARAMS = [("ffn1_norm_g", KD), ("mix_norm_g", KD), ("xattn_norm_g", KD), ("mem_norm_g", KD),
          ("ffn2_norm_g", KD), ("rwkv_mu", 14), ("rwkv_w0", NPAIR), ("rwkv_a0", NPAIR),
          ("rwkv_k_k", NPAIR), ("rwkv_k_a", NPAIR), ("rwkv_r_k", NPAIR), ("rwkv_ln_g", NPAIR),
          ("rwkv_ln_b", NPAIR)]
PARAM_AT = {}
NPAR = 0
for _name, _n in PARAMS:
    PARAM_AT[_name] = NPAR
    NPAR += _n


def constants():
    i = np.arange(P)
    r, c = i[:, None], i[None, :]
    f = lambda m: m.astype(np.float32)
    upper = (r < c) & (r // CH == c // CH)
    blocks = {
        "ident": f(r == c),
        "ones": np.ones((P, P), np.float32),
        "head_ones": f(r // HD == c // HD),
        "flip": f(r + c == P - 1),
        "upper": f(upper),
        "upper_incl": f((r <= c) & (r // CH == c // CH)),
        "upper_sub": f((r < c) & (r // SUB == c // SUB)),
        "lower_sub": f((r > c) & (r // SUB == c // SUB)),
        "lower_off": f((r > c) & (r // CH == c // CH) & (r // SUB != c // SUB)),
    }
    blocks["carry"] = np.tile(f(np.arange(T) % CH != 0), (P, 1))
    return blocks


def rel_bucket_onehot():
    n = np.maximum((T - 1) - np.arange(2 * T), 0)
    buckets, exact, top = 32, 16, 1024
    nf = np.maximum(n, 1).astype(np.float32)
    large = exact + (np.log(nf / np.float32(exact)) / np.float32(np.log(top / exact))
                     * (buckets - exact)).astype(np.int32)
    b = np.where(n < exact, n, np.minimum(large, buckets - 1))
    b = np.where(np.arange(2 * T) > T - 1, buckets, b)
    return (np.arange(buckets + 1)[:, None] == b[None, :]).astype(np.float32)


class Signal:

    def __init__(self, ctx, nc, name, per_layer=0, start=0):
        self.sem = ctx.enter_context(nc.semaphore(name))
        self.name, self.per_layer, self.start, self.n, self.layer0 = name, per_layer, start, 0, 0

    def up(self):
        self.n += 1
        return self.sem, 1

    def at(self, l, n):
        return self.sem, l * self.per_layer + (n + self.start)

    def now(self, l):
        return self.at(l, self.n)

SILU = ACT.Silu
SCORE_BANKS = (0, 1, 4, 5)
F32R = mybir.dt.float32r
FFN_TILES = 3 * FFN_STEPS
H_READY = (0, 13, 22, 31)
SEQ_PE = 7
SOLVE_PE, SOLVE_DVE = 38, 45
PAIR_FREE = ((2, 3), (4, 5), (7, 9))
DVE_CUM, DVE_KK, DVE_RKK, DVE_FEATURES, DVE_YC, DVE_LN = 5, 9, 24, 29, 31, 39
ACT_KK_SQ, ACT_KK_STD, ACT_LN_SQ, ACT_LN_STD = 4, 6, 7, 9
SOLVER_NEEDS = {"square": (10, 11), "fourth": (18, 20), "eighth": (23, 26), "d3": (28, 30),
                "apply": (31, 32), "turn_n": (33, 34), "y1": (35, 36), "y2": (37, 38), "y3": (39, 40),
                "turn_e": 44}


def SOLVER_GROUPS(lo, up, du, rhs):
    z = lambda s: rhs[:, s, 0:P]
    out = []
    for e in range(2):
        out += [("square", e, 6 + e, up, lo, P, False), ("square", e, 2 + e, lo, up, P, False)]
    for e in range(2):
        out += [("fourth", e, 4 + e, up, lo, P, False), ("fourth", e, 6 + e, lo, up, P, False),
                ("fourth", e, 2 + e, lo, du, P, False)]
    for e in range(2):
        out += [("eighth", e, 4 + e, up, lo, P, False), ("eighth", e, 6 + e, lo, du, P, False)]
    out += [("d3", e, 2 + e, lo, du, P, False) for e in range(2)]
    out += [("apply", e, 4 + 2 * e, du, lambda s: rhs[:, s, :], 2 * P, False) for e in range(2)]
    out += [("turn_n", e, e, lambda s: rhs[:, s, P:2 * P], None, P, True) for e in range(2)]
    out += [("y1", e, 2 + e, up, z, P, False) for e in range(2)]
    out += [("y2", e, e, up, du, P, False) for e in range(2)]
    out += [("y3", e, 2 + e, up, du, P, False) for e in range(2)]
    return out


N_MOD = 6
MODS = N_MOD * KD
FIRST_RISES = {
    "par_ready": 1, "x_ready": 16, "sq_ready": 16, "ss_done": 4, "std_ready": 4, "h_ready": 44,
    "w_high_ready": 66, "w_low_ready": 66, "acc_zero": 2, "silu_done": 22, "act_ready": 66,
    "mix_evac": 13, "mixed": 22, "lora_act": 2, "lora_done": 3, "gates": 10, "dve_step": 39,
    "act_step": 9, "hs_done": 4, "tok_done": 8, "tok_act": 6, "sol_done": 76, "sol_step": 90,
    "seq_done": 14, "seq_step": 17, "y_out": 4, "sc_done": 12, "sm_max": 36, "sm_norm": 36,
    "sm_act": 24, "pt_done": 12, "pt_ready": 12, "av_done": 12, "av_out": 8, "memh_ready": 8,
    "kv_evac": 8, "xq_evac": 4
}
N_MOD = 6
MODS = N_MOD * KD
BIG_NEGATIVE = -1e30
N_INPUTS = 3 + len(PARAMS) + 3


def load_second_params(nc, pool, a, store):
    rows, wp, loaded = store["rows2"], store["wp"], store["params2_loaded"].sem
    nc.gpsimd.memset(rows[:, :], 0.0).then_inc(*store["rows2_cleared"].up())
    pool.wait_ge(*store["rows2_cleared"].at(0, 1))

    def row(c, n):
        return rows[c:c + n, :].rearrange("c (l p) -> c l p", l=DEPTH)

    for name, n in PARAMS2:
        pool.dma_start(row(PARAM2_AT[name], n), a[name + "_2"].rearrange("l (c p) -> c l p", p=P)
                       ).then_inc(loaded, 16)
    for name, width, times in (("g_q_gqa", HD, 2), ("g_k_gqa", HD, 2), ("g_q_mla", MQK, 1), ("g_k_mla", MQK, 1)):
        for r in range(times):
            pool.dma_start(row(PARAM2_AT[name], 1)[:, :, r * width:(r + 1) * width],
                           a[name + "_2"].rearrange("(o l) p -> o l p", o=1)).then_inc(loaded, 16)
    for r in range(2):
        for l in range(DEPTH):
            pool.dma_start(wp[r * HD:(r + 1) * HD, :, l, :],
                           a["w_pool_2"][l].rearrange("(g r) c d -> r c g d", r=2)[r]).then_inc(loaded, 16)


def program(nc, a, out):
    with ExitStack() as ctx:
        store = {}
        sb = lambda n, s: ctx.enter_context(nc.sbuf_tensor(n, s, F32))
        store["x"] = sb("x_sb", [P, KD, T])
        store["par"] = sb("par", [P, DEPTH, NPAR])
        store["final_g"] = sb("final_g", [P, 3 * KD])[:, :]
        consts = sb("consts_sb", [P, sum(c.shape[1] for c in constants().values())])
        cst, at = {"all": consts[:, :]}, 0
        for name, c in constants().items():
            cst[name] = consts[:, at:at + c.shape[1]]
            at += c.shape[1]
        store["cst"] = cst
        store["eps"] = sb("eps", [P, 2])
        store["ps"] = ctx.enter_context(nc.psum_tensor("ps", [P, 8, 512], F32))
        store["rows2"] = sb("rows2", [P, DEPTH * P])
        store["wp"] = sb("wp", [P, 2, DEPTH, HD])
        store["rows2_cleared"] = Signal(ctx, nc, "rows2_cleared")
        store["params2_loaded"] = Signal(ctx, nc, "params2_loaded")
        store["w_loaded"] = [Signal(ctx, nc, f"w_loaded{s}") for s in range(RING)]
        store["w_used"] = [Signal(ctx, nc, f"w_used{s}") for s in range(RING)]
        scratch = {"bias": nc.dram_tensor("bias_scratch", (NH, 2 * T), F32).ap(),
                   "mod": nc.dram_tensor("mod_scratch", (DEPTH, P, 2, MODS * P), F32).ap()}
        with ExitStack() as first:
            signals = build_first(nc, first, a, scratch, store)
        with ExitStack() as second:
            signals += build_second(nc, second, a, scratch, store, out)
        for signal in signals:
            rises = signal.layer0 if signal.name in SECOND_RISES else signal.n
            table = SECOND_RISES if signal.name in SECOND_RISES else FIRST_RISES
            assert table.get(signal.name, 0) == rises, signal.name
        return signals


def build_first(nc, ctx, a, scratch, store):
    x_sb, par, cst, eps = store["x"], store["par"], store["cst"], store["eps"]
    PER = FIRST_RISES

    def sb(name, shape):
        return ctx.enter_context(nc.sbuf_tensor(name, shape, F32))

    def sig(name, start=0):
        s = Signal(ctx, nc, name, PER.get(name, 0), start)
        signals.append(s)
        return s

    signals = []
    with ExitStack() as under:
        part = lambda name, shape: under.enter_context(nc.sbuf_tensor(name, shape, F32R))
        w_low = part("w_low", [P, RING, SLOT])
        h_high = part("h_high", [P, KD, T])
        act_high = part("act_high", [P, 2, 512])
        w_high = [part(f"w_high{i}", [P, SLOT])[:, :] for i in range(2)]
        h_low = part("h_low", [P, KD, T])
        act_low = part("act_low", [P, 2, 512])
    ring = sb("ring", [P, RING, SLOT])
    h_sb = sb("h_sb", [P, KD, T])
    probT = sb("probT", [P, 2, 512])
    rk = sb("rk", [P, 2 * NPAIR, T])
    va = sb("va", [P, 2 * NPAIR, T])
    kt = sb("kt", [P, 2 * NPAIR, T])
    e1 = sb("e1", [P, NPAIR, T])
    h_whole = kt
    act_whole = e1[:, :, :].rearrange("p (b a) t -> p b (a t)", b=2)
    mem_sb = sb("mem_sb", [P, KD, T])
    prob = sb("prob", [P, 4, 512])
    hank = sb("hank", [P, NH, T])
    raw_buf = sb("raw_buf", [P, 2 * 2 * (T + 1)])
    dif = sb("dif", [P, 2, T])
    low = sb("low", [P, 2, T])
    sgt = sb("sgt", [P, NPAIR, T])
    cum = sb("cum", [P, NPAIR, T])
    gat = sb("gat", [P, NPAIR, T])
    e2 = sb("e2", [P, NPAIR, T])
    e3 = sb("e3", [P, NPAIR, T])
    cat = sb("cat", [P, KD, T])
    b_tok, k_tok, v_tok = (sb(n, [P, RW]) for n in ("b_tok", "k_tok", "v_tok"))
    state = sb("state", [P, NPAIR, HD])
    pend = sb("pend", [P, NPAIR, T // CH])
    mq, mk = sb("mq", [P, NPAIR, T]), sb("mk", [P, NPAIR, T])
    ecol, fcol = (mq[:, 2 * i:2 * i + 2, :].rearrange("p a t -> p (a t)") for i in range(2))
    mv = sb("mv", [P, 2, RW])
    lw = sb("lw", [P, 2 * RW])
    std = sb("std", [P, T])
    smx, ssum = sb("smx", [P, 4, 2]), sb("ssum", [P, 4, 2])

    r_t, k_t, v_t, a_t = rk[:, 0:NPAIR], rk[:, NPAIR:], va[:, 0:NPAIR], va[:, NPAIR:]
    kk_t, tmp = kt[:, 0:NPAIR], kt[:, NPAIR:]
    raw = raw_buf[:, :].rearrange("p (b m t) -> p b m t", b=2, m=2)
    mats = lambda ap: ap.rearrange("p a (b t) -> p (a b) t", b=2)
    m_up, l_lo, l_up = mats(sgt[:, :, :]), mats(kk_t), mats(tmp)
    nb_up, nk_up = mats(e2[:, :, :]), mats(e1[:, :, :])
    d_up = raw_buf[:, 0:2 * RW].rearrange("p (s t) -> p s t", s=NH)
    rhs = h_sb[:, :, :]
    e_row, u_tok = low[:, :, :].rearrange("p a (b t) -> p (a b) t", b=2), dif[:, :, :].rearrange("p a t -> p (a t)")
    xq, xk = rk[:, :, :], va[:, :, :]
    xv = kt[:, :, :].rearrange("p (h a) t -> p h (a t)", h=2)
    ps = [store["ps"][:, i, :] for i in range(8)]
    psum = store["ps"]

    ident, ones, head_ones = cst["ident"], cst["ones"], cst["head_ones"]

    def pcol(name, i=0):
        c = PARAM_AT[name] + i
        return par_cur[:, c:c + 1]

    par_cur = sb("par_cur", [P, NPAR])
    cond = sb("cond", [P, 2 * KD])
    wmod = sb("wmod", [P, KD, BLK])
    prod = sb("prod", [P, KD, BLK])
    mod_acc = prod[:, 2:4, :]
    junk = sb("junk", [P, 3 + RING])

    w_loaded, w_used = store["w_loaded"], store["w_used"]
    w_dram = a

    def slot(n):
        return ring[:, n % RING, :]

    def at_tile(n, l):
        return l * FIRST_USES[n % RING] + n // RING

    def freed(n, l):
        return at_tile(n, l) + 1

    class FfnTiles:

        def __init__(self, l, f):
            self.l, self.f, self.n0 = l, f, FIRST_AT[(f"ffn{f + 1}_gate", 0)]

        def slot(self, r, b):
            return (self.n0 + 3 * b + r) % RING

        def loaded(self, r, b, use):
            s = self.slot(r, b)
            return w_loaded[s].sem, (self.l * FIRST_USES[s] + self.n0 // RING + use + 1) * 16

        def used(self, r, b, use):
            s = self.slot(r, b)
            return w_used[s].sem, self.l * FIRST_USES[s] + (self.n0 // RING + 2) + use

        def split(self, t, signal):
            return signal.at(self.l, t + (FFN_TILES * self.f + 1))

        def act(self, i, part=3):
            return act_ready.at(self.l, 3 * i + (3 * FFN_STEPS * self.f + part))

    lora_loaded = sig("lora_loaded")
    par_ready = sig("par_ready")
    x_ready = sig("x_ready", 1)
    sq_ready = sig("sq_ready")
    ss_done = sig("ss_done")
    std_ready = sig("std_ready")
    h_ready = sig("h_ready")
    w_high_ready = sig("w_high_ready")
    w_low_ready = sig("w_low_ready")
    acc_zero = sig("acc_zero")
    silu_done = sig("silu_done")
    act_ready = sig("act_ready")
    mix_evac = sig("mix_evac")
    mixed = sig("mixed")
    lora_act = sig("lora_act")
    lora_done = sig("lora_done", 1)
    gates = sig("gates")
    dve_step = sig("dve_step")
    act_step = sig("act_step")
    hs_done = sig("hs_done")
    tok_done = sig("tok_done")
    tok_act = sig("tok_act")
    sol_done = sig("sol_done")
    sol_step = sig("sol_step")
    seq_done = sig("seq_done")
    seq_step = sig("seq_step")
    y_out = sig("y_out")
    sc_done = sig("sc_done")
    sm_max = sig("sm_max")
    sm_norm = sig("sm_norm")
    sm_act = sig("sm_act")
    pt_done = sig("pt_done")
    pt_ready = sig("pt_ready")
    av_done = sig("av_done")
    av_out = sig("av_out")
    memh_ready = sig("memh_ready")
    kv_evac = sig("kv_evac")
    wmod_loaded = sig("wmod_loaded")
    mod_stored = sig("mod_stored")
    mod_step = sig("mod_step")
    started = sig("started")
    xq_evac = sig("xq_evac")

    def wait_apart(engine, semaphore, value):
        engine.compute_val(value)
        engine.wait_ge(started.sem, 1)
        engine.wait_ge(semaphore, value)

    def sync_program(sp):
        def load(l, n, source, shape=None):
            s, free = n % RING, freed(n, l)
            wait_apart(sp, w_used[s].sem, free)
            dst = slot(n) if shape is None else slot(n).rearrange(*shape[0], **shape[1])
            sp.dma_start(dst, source).then_inc(w_loaded[s].sem, 16)

        cols = (("p (k n) -> p k n",), {"k": KD})
        rows = (("p (r n) -> p r n",), {"r": 2})

        def column_tile(w, l, c):
            return w[bass.ds(l, 1), :, bass.ds(c, BLK)].rearrange("o (k p) n -> p (o k) n", p=P)

        def row_tile(w, l, r):
            return w[bass.ds(l, 1), bass.ds(r, BLK), :].rearrange("o (k p) n -> p (o k) n", p=P)

        def ffn(l, f):
            w_in, w_out, tiles = w_dram[f"ffn{f + 1}_w_in"], w_dram[f"ffn{f + 1}_w_out"], FfnTiles(l, f)

            def step(i, b, use):
                for r, src in ((0, column_tile(w_in, l, i * BLK)),
                               (1, column_tile(w_in, l, i * BLK + D_FF)),
                               (2, row_tile(w_out, l, i * BLK))):
                    s = tiles.slot(r, b)
                    sp.wait_ge(*tiles.used(r, b, use - 1))
                    dst = ring[:, s, :].rearrange("p (k n) -> p k n", k=KD if r < 2 else 2)
                    sp.dma_start(dst, src).then_inc(w_loaded[s].sem, 16)

            with sp.Fori(0, FFN_STEPS // 2) as j:
                step(j * 2, 0, j)
                step(j * 2 + 1, 1, j)
            step(FFN_STEPS - 1, 0, FFN_STEPS // 2)

        with sp.Fori(0, DEPTH) as l:
            ffn(l, 0)
            for kind, w in (("mix_in", "w_mix_in"), ("kv", "xattn_w_kv"), ("mix_out", "w_mix_out"),
                            ("xq", "xattn_w_q"), ("xo", "xattn_w_o")):
                for name in [n for n in FIRST if n[0] == kind]:
                    load(l, FIRST_AT[name], column_tile(w_dram[w], l, name[1] * BLK), cols)
            ffn(l, 1)

    def tensor_program(pe):
        mm = nc.tensor.matmul

        def norm(l, n):
            squares = cat if n == 3 else h_sb
            for k in range(KD):
                if k % 2 == 0:
                    pe.wait_ge(*sq_ready.at(l, 4 * n + k // 2 + 1))
                last = mm(ps[4][:, 0:T], ones, squares[:, k, :], start=(k == 0), stop=(k == KD - 1))
            last.then_inc(*ss_done.up())

        def normed(l, n):
            def before(k):
                if n in (0, 3):
                    if k % 4 == 0:
                        pe.wait_ge(*h_ready.at(l, H_READY[n] + 1 + 6 * (k // 4 + 1)))
                else:
                    pe.wait_ge(*h_ready.at(l, H_READY[n] + 2 + k))
            return before

        def split_mm(dst, w_hi, w_lo, x_hi, x_lo, start, stop, **more):
            mm(dst, w_hi, x_hi, start=start, stop=False, **more)
            mm(dst, w_hi, x_lo, start=False, stop=False, **more)
            return mm(dst, w_lo, x_hi, start=False, stop=stop, **more)

        def ffn(l, f):
            tiles = FfnTiles(l, f)

            def parts(r, b, t, parity):
                pe.wait_ge(*tiles.split(t, w_low_ready))
                shape = {"k": KD if r < 2 else 2}
                return [ap.rearrange("p (k n) -> p k n", **shape)
                        for ap in (w_high[parity], w_low[:, tiles.slot(r, b), :])]

            def gate_up(i, b, t, parity, reuse, before=None):
                for r, bank in ((0, 4 + b), (1, 6 + b)):
                    hi, lo = parts(r, b, t + r, (parity + r) % 2)
                    if reuse:
                        pe.wait_ge(*(tiles.act(i - 2, 1) if r else
                                     silu_done.at(l, FFN_STEPS * f + i - 1)))
                    for m in range(2):
                        for k in range(KD):
                            if before and r == 0 and m == 0:
                                before(k)
                            cols = slice(m * P, (m + 1) * P)
                            last = split_mm(ps[bank][:, m * T:(m + 1) * T], hi[:, k, cols], lo[:, k, cols],
                                            h_high[:, k, :], h_low[:, k, :], k == 0, k == KD - 1)
                    last.then_inc(w_used[tiles.slot(r, b)].sem, 1)

            def down(i, b, t, parity):
                hi, lo = parts(2, b, t, parity)
                pe.wait_ge(*tiles.act(i))
                for k in range(2):
                    for m in range(KD):
                        cols, ks = slice(m * P, (m + 1) * P), slice(k * T, (k + 1) * T)
                        last = split_mm(ps[m // 2][:, (m % 2) * T:(m % 2 + 1) * T], hi[:, k, cols],
                                        lo[:, k, cols], act_high[:, b, ks], act_low[:, b, ks], False, False,
                                        skip_group_check=True)
                last.then_inc(w_used[tiles.slot(2, b)].sem, 1)

            gate_up(0, 0, 0, 0, False, normed(l, 3 * f))
            gate_up(1, 1, 2, 0, False)
            pe.wait_ge(*acc_zero.at(l, f + 1))
            down(0, 0, 4, 0)
            gate_up(2, 0, 5, 1, True)
            down(1, 1, 7, 1)
            with pe.Fori(1, FFN_STEPS // 2) as j:
                gate_up(j * 2 + 1, 1, j * 6 + 2, 0, True)
                down(j * 2, 0, j * 6 + 4, 0)
                gate_up(j * 2 + 2, 0, j * 6 + 5, 1, True)
                down(j * 2 + 1, 1, j * 6 + 7, 1)
            down(FFN_STEPS - 1, 0, FFN_TILES - 1, 0)

        def column_tile(l, name, bank, x, token_major=False, before=None):
            n = FIRST_AT[name]
            pe.wait_ge(w_loaded[n % RING].sem, (at_tile(n, l) + 1) * 16)
            w = slot(n).rearrange("p (k n) -> p k n", k=KD)
            for m in range(2):
                for k in range(KD):
                    if before and m == 0:
                        before(k)
                    lhs, right = w[:, k, m * P:(m + 1) * P], x[:, k, :]
                    if token_major:
                        lhs, right = x[:, k, m * P:(m + 1) * P], w[:, k, :]
                    last = mm(ps[bank][:, m * T:(m + 1) * T], lhs, right,
                              start=(k == 0), stop=(k == KD - 1))
            last.then_inc(w_used[n % RING].sem, 1)

        def head_sums(src, banks):
            for m in range(NPAIR):
                last = mm(ps[banks + m // 2][:, (m % 2) * T:(m % 2 + 1) * T], head_ones,
                          src[:, m, :], start=True, stop=True)
            last.then_inc(*hs_done.up())

        def moba(l):
            def scores(h):
                pair, hb, bank = h // 2, (h % 2) * HD, ps[SCORE_BANKS[h % 4]]
                if h >= 4:
                    pe.wait_ge(*sm_act.at(l, 2 * (h - 3)))
                hi = slice(hb, hb + HD)
                mm(bank[:, 0:T], cst["flip"], hank[:, h, :], start=True, stop=False,
                   skip_group_check=True)
                mm(bank[:, T:T + P], cst["flip"], hank[:, h, P:T], start=False, stop=False,
                   skip_group_check=True)
                mm(bank[:, 0:T], mq[hi, pair, P:T], mk[hi, pair, :], start=False, stop=False,
                   skip_group_check=True)
                mm(bank[:, T:T + P], mq[hi, pair, 0:P], mk[hi, pair, 0:P], start=False, stop=True,
                   skip_group_check=True).then_inc(*sc_done.up())

            def turn(h):
                e = h % 2
                pe.wait_ge(*sm_norm.at(l, 3 * (h + 1)))
                if h >= 2:
                    pe.wait_ge(*pt_ready.at(l, h - 1))
                for dst, src in ((P, 0), (2 * P, P), (0, 2 * P)):
                    last = nc.tensor.transpose(ps[2 + e][:, dst:dst + P], prob[:, h % 4, src:src + P], ident)
                last.then_inc(*pt_done.up())

            def out(h):
                pair, hb, e = h // 2, (h % 2) * HD, h % 2
                pe.wait_ge(*pt_ready.at(l, h + 1))
                if pair >= 2 and e == 0:
                    pe.wait_ge(*av_out.at(l, pair - 1))
                dst, cols = ps[6 + pair % 2][hb:hb + HD, 0:T], slice(h * HD, (h + 1) * HD)
                mm(dst, mv[:, 0, cols], probT[:, e, 0:T], start=True, stop=False, skip_group_check=True)
                last = mm(dst[:, P:T], mv[:, 1, cols], probT[:, e, T:T + P], start=False, stop=True,
                          skip_group_check=True)
                last.then_inc(*av_done.up())

            pe.wait_ge(*mix_evac.at(l, MIX_TILES))
            for h in range(NH + 3):
                if h < NH:
                    scores(h)
                if 2 <= h < NH + 2:
                    turn(h - 2)
                if h >= 3:
                    out(h - 3)

        def solver(l, c):
            ts = slice(c * P, (c + 1) * P)
            s0, d0 = SOLVE_PE * c, SOLVE_DVE * c
            if c:
                pe.wait_ge(*y_out.at(l, 2))
                pe.wait_ge(*seq_step.at(l, 9))
            for q, src in enumerate((e3, a_t, k_t, v_t)):
                for m in range(NPAIR):
                    last = nc.tensor.transpose(ps[q][:, m * P:(m + 1) * P], src[:, m, ts], ident)
                last.then_inc(*tok_done.up())
            for s, (left, right) in enumerate(((k_t, e3), (a_t, e3), (e3, a_t), (a_t, r_t), (k_t, r_t))):
                for e in range(2):
                    if s >= 2:
                        pe.wait_ge(*sol_step.at(l, d0 + PAIR_FREE[s - 2][e]))
                    hi = slice(e * HD, (e + 1) * HD)
                    for m in range(NPAIR):
                        last = mm(ps[4 + 2 * (s % 2) + e][:, m * P:(m + 1) * P], left[hi, m, ts],
                                  right[hi, m, ts], start=True, stop=True)
                    last.then_inc(*sol_done.up())
            pe.wait_ge(*tok_act.at(l, 3 * (c + 1)))
            pe.wait_ge(*sol_step.at(l, d0 + 1 + 2))
            for s in range(NH):
                h = 2 * (s % NPAIR) + s // NPAIR
                last = mm(ps[0][:, s * HD:(s + 1) * HD], m_up[:, s, :], v_tok[:, h * HD:(h + 1) * HD],
                          start=True, stop=True)
            last.then_inc(*sol_done.up())

            def group(bank, e, left, right, cols=P, turned=False):
                for m in range(NPAIR):
                    s = e * NPAIR + m
                    dst = ps[bank + m * cols // 512][:, (m * cols) % 512:(m * cols) % 512 + cols]
                    if turned:
                        last = nc.tensor.transpose(dst, left(s), ident)
                    else:
                        last = mm(dst, left(s), right(s), start=True, stop=True)
                last.then_inc(*sol_done.up())

            lo, up, du = (lambda s: l_lo[:, s, :]), (lambda s: l_up[:, s, :]), (lambda s: d_up[:, s, :])
            for name, e, bank, left, right, cols, turned in SOLVER_GROUPS(lo, up, du, rhs):
                pe.wait_ge(*sol_step.at(l, d0 + SOLVER_NEEDS[name][e]))
                group(bank, e, left, right, cols, turned)
            pe.wait_ge(*sol_step.at(l, d0 + SOLVER_NEEDS["turn_e"]))
            for m in range(NPAIR):
                last = nc.tensor.transpose(ps[4][:, m * P:(m + 1) * P], ecol[:, m * P:(m + 1) * P], ident)
            last.then_inc(*sol_done.up())

        def recurrence(l, c):
            for q in range(2):
                tb, chunk = slice(q * CH, (q + 1) * CH), 2 * c + q
                t0 = c * P + q * CH
                if q == 0:
                    wait_apart(pe, *sol_step.at(l, SOLVE_DVE * (c + 1)))
                wait_apart(pe, *seq_step.at(l, 1 + 4 * chunk))
                for e in range(2):
                    hi = slice(e * HD, (e + 1) * HD)
                    for m in range(NPAIR):
                        last = mm(ps[e][tb, m * HD:(m + 1) * HD], e_row[hi, m, tb], state[hi, m, :],
                                  start=True, stop=True)
                    last.then_inc(*seq_done.up())
                for e in range(2):
                    hi = slice(e * HD, (e + 1) * HD)
                    for m in range(NPAIR):
                        mm(ps[4 + e][hi, m * P + q * CH:m * P + (q + 1) * CH], state[hi, m, :],
                           r_t[hi, m, t0:t0 + CH], start=(q == 0 and m == 0), stop=False,
                           skip_group_check=True)
                wait_apart(pe, *seq_step.at(l, 1 + 4 * chunk + 2))
                for e in range(2):
                    hi = slice(e * HD, (e + 1) * HD)
                    for m in range(NPAIR):
                        h = 2 * m + e
                        hc = slice(h * HD, (h + 1) * HD)
                        dst = ps[2][hi, m * HD:(m + 1) * HD]
                        mm(dst, b_tok[tb, hc], u_tok[tb, hc], start=True, stop=False)
                        last = mm(dst, k_tok[tb, hc], v_tok[tb, hc], start=False, stop=True)
                last.then_inc(*seq_done.up())
            for e in range(2):
                hi = slice(e * HD, (e + 1) * HD)
                for m in range(NPAIR):
                    h, s = 2 * m + e, e * NPAIR + m
                    hc = slice(h * HD, (h + 1) * HD)
                    dst = ps[4 + e][hi, m * P:(m + 1) * P]
                    mm(dst, u_tok[:, hc], nb_up[:, s, :], start=False, stop=False, skip_group_check=True)
                    last = mm(dst, v_tok[:, hc], nk_up[:, s, :], start=False, stop=True,
                              skip_group_check=True)
            last.then_inc(*seq_done.up())

        def cross(l):
            def scores(h):
                for t in range(2):
                    for k in range(2):
                        last = mm(ps[SCORE_BANKS[h]][:, t * T:(t + 1) * T], xq[:, 2 * h + k, t * P:(t + 1) * P],
                                  xk[:, 2 * h + k, :], start=(k == 0), stop=(k == 1))
                last.then_inc(*sc_done.up())

            def turn(h):
                e = h % 2
                pe.wait_ge(*sm_norm.at(l, 3 * (NH + h + 1)))
                if h >= 2:
                    pe.wait_ge(*pt_ready.at(l, NH + h - 1))
                for t in range(2):
                    for k in range(2):
                        last = nc.tensor.transpose(ps[2 + e][:, k * T + t * P:k * T + (t + 1) * P],
                                                   prob[:, h, t * T + k * P:t * T + (k + 1) * P], ident)
                last.then_inc(*pt_done.up())

            def out(h):
                e = h % 2
                pe.wait_ge(*pt_ready.at(l, NH + h + 1))
                if h >= 2:
                    pe.wait_ge(*av_out.at(l, NPAIR + h - 1))
                for i in range(2):
                    f = (2 * h + i) * P
                    for k in range(2):
                        last = mm(ps[6 + e][:, i * T:(i + 1) * T], xv[:, k, f:f + P],
                                  probT[:, e, k * T:(k + 1) * T], start=(k == 0), stop=(k == 1))
                last.then_inc(*av_done.up())

            pe.wait_ge(*xq_evac.at(l, LIN_TILES))
            for h in range(XH + 3):
                if h < XH:
                    scores(h)
                if 2 <= h < XH + 2:
                    turn(h - 2)
                if h >= 3:
                    out(h - 3)

        with pe.Fori(0, DEPTH) as l:
            norm(l, 0)
            ffn(l, 0)
            norm(l, 1)
            for n, j in enumerate(MIX_ORDER):
                if n >= 4:
                    pe.wait_ge(*mix_evac.at(l, n - 3))
                column_tile(l, ("mix_in", j), 4 + n % 4, h_sb, token_major=(j >= 11),
                            before=normed(l, 1) if n == 0 else None)
                if n == 2:
                    pe.wait_ge(lora_loaded.sem, l * 48 + 48)
                    pe.wait_ge(*lora_act.at(l, 2))
                    for which, rows in ((0, slice(0, HD)), (1, slice(HD, P))):
                        for m in range(NPAIR):
                            last = mm(ps[2 * which + m // 2][:, (m % 2) * T:(m % 2 + 1) * T],
                                      lw[rows, m * P:(m + 1) * P], low[rows, 0, :],
                                      start=True, stop=True)
                        last.then_inc(*lora_done.up())
                if n == 4:
                    pe.wait_ge(*gates.at(l, 4))
                    for m in range(NPAIR):
                        last = mm(ps[m // 2][:, (m % 2) * T:(m % 2 + 1) * T],
                                  lw[:, RW + m * P:RW + (m + 1) * P], low[:, 1, :],
                                  start=True, stop=True)
                    last.then_inc(*lora_done.up())
                if n == 8:
                    pe.wait_ge(*gates.at(l, 8))
                    pe.wait_ge(*act_step.at(l, ACT_KK_SQ))
                    head_sums(sgt, 2)
                if n == 11:
                    pe.wait_ge(*gates.at(l, 10))
                    pe.wait_ge(*dve_step.at(l, DVE_RKK))
                    head_sums(tmp, 0)
            pe.wait_ge(*dve_step.at(l, DVE_FEATURES))
            moba(l)
            for c in range(2):
                if c == 0:
                    pe.wait_ge(*sm_act.at(l, 2 * NH))
                    pe.wait_ge(*pt_ready.at(l, NH))
                    pe.wait_ge(*av_out.at(l, NPAIR))
                solver(l, c)
                recurrence(l, c)
            pe.wait_ge(*y_out.at(l, 4))
            pe.wait_ge(*memh_ready.at(l, KD))
            for j in range(KV_TILES):
                if j >= 4:
                    pe.wait_ge(*kv_evac.at(l, j - 3))
                column_tile(l, ("kv", j), 4 + j % 4, h_sb, token_major=(j >= 4))
                if j == 0:
                    head_sums(cat, 0)
                if j == 2:
                    pe.wait_ge(*act_step.at(l, ACT_LN_SQ))
                    head_sums(sgt, 2)
            pe.wait_ge(*dve_step.at(l, DVE_LN))
            pe.wait_ge(*kv_evac.at(l, KV_TILES))
            for j in range(LIN_TILES):
                column_tile(l, ("mix_out", j), 4 + j % 4, cat)
            norm(l, 2)
            for j in range(LIN_TILES):
                column_tile(l, ("xq", j), 4 + j % 4, h_sb, before=None if j else normed(l, 2))
            cross(l)
            pe.wait_ge(*av_out.at(l, NPAIR + XH))
            for j in range(LIN_TILES):
                column_tile(l, ("xo", j), 4 + j % 4, h_sb)
            norm(l, 3)
            ffn(l, 1)

    def modulation_program(pool):
        g = nc.gpsimd
        n_tiles = MODS * P // BLK
        MOD_STAGES = 5

        with pool.Fori(0, DEPTH) as l:
            with pool.Fori(0, n_tiles) as t:
                done = l * n_tiles + t
                src = w_dram["w_mod_2"][bass.ds(l, 1), :, bass.ds(t * BLK, BLK)]
                pool.dma_start(wmod[:, :, :], src.rearrange("o (k p) n -> p (o k) n", p=P)
                               ).then_inc(wmod_loaded.sem, 16)
                pool.wait_ge(wmod_loaded.sem, done * 16 + 16)
                for c, dst in enumerate((prod[:, :, :], wmod[:, :, :])):
                    g.tensor_tensor(dst, wmod[:, :, :], cond[:, c * KD:(c + 1) * KD].rearrange(
                        "p (k o) -> p k o", o=1).to_broadcast([P, KD, BLK]), ALU.mult
                        ).then_inc(mod_step.sem, 1)
                    pool.wait_ge(mod_step.sem, done * MOD_STAGES + c + 1)
                for r, half in enumerate((4, 2, 1)):
                    for c, part in enumerate((prod, wmod)):
                        dst = part[:, 0:half, :] if half > 1 else mod_acc[:, c:c + 1, :]
                        last = g.tensor_tensor(dst, part[:, 0:half, :], part[:, half:2 * half, :],
                                               ALU.add)
                    last.then_inc(mod_step.sem, 1)
                    pool.wait_ge(mod_step.sem, done * MOD_STAGES + 3 + r)
                dst = scratch["mod"][bass.ds(l, 1), :, :, bass.ds(t * BLK, BLK)]
                pool.dma_start(dst.rearrange("o p c n -> p (o c) n"), mod_acc[:, :, :]
                               ).then_inc(mod_stored.sem, 16)
                pool.wait_ge(mod_stored.sem, done * 16 + 16)

    def scalar_program(act):
        go = nc.scalar.activation

        def norm(l, n):
            squares = cat if n == 3 else h_sb
            for q in range(4):
                act.wait_ge(*x_ready.at(l, 4 * (n - 1) + q + 1 if n else 0))
                go(squares[:, 2 * q:2 * q + 2, :], x_sb[:, 2 * q:2 * q + 2, :],
                   ACT.Square).then_inc(*sq_ready.up())
            if n in (0, 3):
                w_high_part(FfnTiles(l, n // 3), 0, 0, 0, 0)
            act.wait_ge(*ss_done.at(l, n + 1))
            go(std[:, :], ps[4][:, 0:T], ACT.Sqrt, bias=eps[:, 0:1], scale=1.0 / D).then_inc(*std_ready.up())

        def w_high_part(tiles, r, b, use, parity, before=None):
            act.wait_ge(*tiles.loaded(r, b, use))
            if before:
                act.wait_ge(*tiles.used(*before))
            go(w_high[parity], ring[:, tiles.slot(r, b), :], ACT.Copy).then_inc(w_high_ready.sem, 1)

        def ffn(l, f):
            tiles = FfnTiles(l, f)
            w_high_of = lambda *which: w_high_part(tiles, *which)

            def silu(i, b, use, reuse):
                act.wait_ge(*tiles.used(0, b, use))
                if reuse:
                    act.wait_ge(*tiles.act(i - 2, 1))
                go(prob[:, b, :], ps[4 + b], SILU).then_inc(silu_done.sem, 1)

            w_high_of(1, 0, 0, 1)
            w_high_of(0, 1, 0, 0, (0, 0, 0))
            silu(0, 0, 0, False)
            w_high_of(1, 1, 0, 1, (1, 0, 0))
            w_high_of(2, 0, 0, 0, (0, 1, 0))
            silu(1, 1, 0, False)
            w_high_of(0, 0, 1, 1, (1, 1, 0))
            w_high_of(1, 0, 1, 0, (2, 0, 0))
            w_high_of(2, 1, 0, 1, (0, 0, 1))
            with act.Fori(1, FFN_STEPS // 2) as j:
                silu(j * 2, 0, j, True)
                w_high_of(0, 1, j, 0, (1, 0, j))
                w_high_of(1, 1, j, 1, (2, 1, j - 1))
                w_high_of(2, 0, j, 0, (0, 1, j))
                silu(j * 2 + 1, 1, j, True)
                w_high_of(0, 0, j + 1, 1, (1, 1, j))
                w_high_of(1, 0, j + 1, 0, (2, 0, j))
                w_high_of(2, 1, j, 1, (0, 0, j + 1))
            silu(FFN_STEPS - 1, 0, FFN_STEPS // 2, True)
            w_high_of(2, 0, FFN_STEPS // 2, 0, (1, 0, FFN_STEPS // 2))
            w_high_ready.n += FFN_TILES
            silu_done.n += FFN_STEPS

        def take(l, name, bank, dst, signal, scale=1.0):
            n = FIRST_AT[name]
            act.wait_ge(w_used[n % RING].sem, freed(n, l) + 1)
            go(dst, ps[bank].rearrange("p (m t) -> p m t", m=2), ACT.Copy,
               scale=scale).then_inc(*signal.up())

        def softmax(l, heads, base, scale, widths):
            for h in range(heads + 2):
                if h < heads:
                    e, g, bank = h % 4, base + h, ps[SCORE_BANKS[h % 4]]
                    act.wait_ge(*sm_max.at(l, 3 * (g + 1)))
                    if h >= 4:
                        act.wait_ge(*pt_done.at(l, g - 3))
                    at = 0
                    for t, w in enumerate(widths):
                        go(prob[:, e, at:at + w], bank[:, at:at + w], ACT.Exp, bias=smx[:, e, t:t + 1],
                           scale=scale, accum_out=ssum[:, e, t:t + 1]).then_inc(*sm_act.up())
                        at += w
                if h >= 2:
                    e, g = (h - 2) % 2, base + h - 2
                    act.wait_ge(*pt_done.at(l, g + 1))
                    if h >= 4:
                        act.wait_ge(*av_done.at(l, g - 1))
                    w = sum(widths)
                    go(probT[:, e, 0:w], ps[2 + e][:, 0:w], ACT.Copy).then_inc(*pt_ready.up())

        with act.Fori(0, DEPTH) as l:
            act.wait_ge(*lora_done.at(l, 0))
            for dst, src in ((lw[0:HD, 0:RW], "rwkv_w_up"), (lw[HD:P, 0:RW], "rwkv_a_up"),
                             (lw[:, RW:], "rwkv_g_up")):
                act.dma_start(dst, w_dram[src][bass.ds(l, 1)].rearrange("o k n -> (o k) n")
                              ).then_inc(lora_loaded.sem, 16)
            norm(l, 0)
            ffn(l, 0)
            norm(l, 1)
            for n, j in enumerate(MIX_ORDER):
                if n < 7:
                    act.wait_ge(*mixed.at(l, 1 + 3 * max(n - 1, 0)))
                    take(l, ("mix_in", j), 4 + n % 4, raw[:, n % 2, :, 1:T + 1], mix_evac)
                elif j < 9:
                    take(l, ("mix_in", j), 4 + n % 4, mq[:, 2 * (j - 7):2 * (j - 7) + 2, :], mix_evac,
                         scale=HD ** -0.5)
                elif j < 11:
                    take(l, ("mix_in", j), 4 + n % 4, mk[:, 2 * (j - 9):2 * (j - 9) + 2, :], mix_evac)
                else:
                    take(l, ("mix_in", j), 4 + n % 4, mv[:, :, (j - 11) * BLK:(j - 10) * BLK], mix_evac)
                if n == 1:
                    act.wait_ge(*mixed.at(l, 4))
                    go(low[0:HD, 0, :], low[0:HD, 0, :], ACT.Tanh).then_inc(*lora_act.up())
                    go(low[:, 1, :], low[:, 1, :], ACT.Sigmoid).then_inc(*lora_act.up())
                if n == 3:
                    for dst, bank, bias, which in ((sgt, 0, "rwkv_w0", 1), (a_t, 2, "rwkv_a0", 2)):
                        act.wait_ge(*lora_done.at(l, which))
                        for m in range(NPAIR):
                            go(dst[:, m, :], ps[bank + m // 2][:, (m % 2) * T:(m % 2 + 1) * T],
                               ACT.Sigmoid, bias=pcol(bias, m)).then_inc(*gates.up())
                if n == 5:
                    act.wait_ge(*lora_done.at(l, 3))
                    for i in range(2):
                        go(gat[:, 2 * i:2 * i + 2, :], ps[i].rearrange("p (m t) -> p m t", m=2),
                           ACT.Copy).then_inc(*gates.up())
                    act.wait_ge(*dve_step.at(l, DVE_CUM))
                    go(e1[:, :, :], cum[:, :, :], ACT.Exp, scale=-DECAY).then_inc(*act_step.up())
                    go(e2[:, :, :], cum[:, :, :], ACT.Exp, scale=DECAY).then_inc(*act_step.up())
                    go(e3[:, :, :], e3[:, :, :], ACT.Exp, scale=-DECAY).then_inc(*act_step.up())
                if n == 6:
                    act.wait_ge(*dve_step.at(l, DVE_KK))
                    go(sgt[:, :, :], kk_t, ACT.Square).then_inc(*act_step.up())
                if n == 8:
                    act.wait_ge(*hs_done.at(l, 1))
                    for i in range(2):
                        go(sgt[:, 2 * i:2 * i + 2, :], ps[2 + i].rearrange("p (m t) -> p m t", m=2),
                           ACT.Sqrt).then_inc(*act_step.up())
            softmax(l, NH, 0, 1.0, (T, P))
            for c in range(2):
                for q, dst in enumerate((b_tok, k_tok, v_tok)):
                    act.wait_ge(*tok_done.at(l, 4 * c + q + 2))
                    go(dst[:, :], ps[q + 1], ACT.Copy).then_inc(*tok_act.up())
                act.wait_ge(*seq_done.at(l, SEQ_PE * (c + 1)))
                for e in range(2):
                    hi = slice(e * HD, (e + 1) * HD)
                    go(cat[hi, 0:NPAIR, c * P:(c + 1) * P],
                       ps[4 + e][hi, :].rearrange("p (m t) -> p m t", m=NPAIR),
                       ACT.Copy).then_inc(*y_out.up())
            for k in range(KD):
                go(h_sb[:, k, :], mem_sb[:, k, :], ACT.Copy, scale=pcol("mem_norm_g", k)
                   ).then_inc(*memh_ready.up())
            for j in range(KV_TILES):
                take(l, ("kv", j), 4 + j % 4, xk[:, 2 * j:2 * j + 2, :] if j < 4 else
                     xv[:, :, (j - 4) * BLK:(j - 3) * BLK], kv_evac)
                if j == 1:
                    act.wait_ge(*dve_step.at(l, DVE_YC))
                    go(sgt[:, :, :], cat[:, 0:NPAIR, :], ACT.Square).then_inc(*act_step.up())
                if j == 2:
                    act.wait_ge(*hs_done.at(l, 4))
                    for i in range(2):
                        go(sgt[:, 2 * i:2 * i + 2, :], ps[2 + i].rearrange("p (m t) -> p m t", m=2),
                           ACT.Sqrt, bias=eps[:, 1:2], scale=1.0 / HD).then_inc(*act_step.up())
            norm(l, 2)
            for j in range(LIN_TILES):
                take(l, ("xq", j), 4 + j % 4, xq[:, 2 * j:2 * j + 2, :], xq_evac)
            softmax(l, XH, NH, XD ** -0.5, (T, T))
            norm(l, 3)
            ffn(l, 1)

    def vector_program(dve):
        v = nc.vector

        def residual(l, n, names, scale):
            for q in range(4):
                bank, tile = (q, names[0]) if len(names) == 1 else (4 + q, names[q])
                s = tile % RING
                dve.wait_ge(w_used[s].sem, freed(tile, l) + 1)
                v.scalar_tensor_tensor(x_sb[:, 2 * q:2 * q + 2, :],
                                       ps[bank].rearrange("p (m t) -> p m t", m=2), scale,
                                       x_sb[:, 2 * q:2 * q + 2, :], ALU.mult, ALU.add
                                       ).then_inc(*x_ready.up())

        def norm(l, n, gain):
            if n in (0, 3):
                dve.wait_ge(*x_ready.at(l, 4 * n))
                v.memset(psum[:, 0:4, :], 0.0).then_inc(*acc_zero.up())
                w_low_part(FfnTiles(l, n // 3), 0, 0, 0, 0)
            dve.wait_ge(*std_ready.at(l, n + 1))
            step(l, v.reciprocal(std[:, :], std[:, :]), h_ready)
            if n in (0, 3):
                for half in (slice(0, KD // 2), slice(KD // 2, KD)):
                    for k in range(half.start, half.stop):
                        v.scalar_tensor_tensor(h_whole[:, k, :], x_sb[:, k, :], pcol(gain, k), std[:, :],
                                               ALU.mult, ALU.mult).then_inc(*h_ready.up())
                    dve.wait_ge(*h_ready.now(l))
                    step(l, v.tensor_copy(h_high[:, half, :], h_whole[:, half, :]), h_ready)
                    v.tensor_tensor(h_low[:, half, :], h_whole[:, half, :], h_high[:, half, :], ALU.subtract
                                    ).then_inc(*h_ready.up())
            else:
                for k in range(KD):
                    v.scalar_tensor_tensor(h_sb[:, k, :], x_sb[:, k, :], pcol(gain, k), std[:, :],
                                           ALU.mult, ALU.mult).then_inc(*h_ready.up())

        def w_low_part(tiles, r, b, t, parity):
            slot = tiles.slot(r, b)
            dve.wait_ge(*tiles.split(t, w_high_ready))
            v.tensor_tensor(w_low[:, slot, :], ring[:, slot, :], w_high[parity], ALU.subtract
                            ).then_inc(w_low_ready.sem, 1)

        def ffn(l, f):
            tiles = FfnTiles(l, f)
            w_low_of = lambda *which: w_low_part(tiles, *which)

            def times_up(i, b, use, reuse):
                dve.wait_ge(*silu_done.at(l, i + (FFN_STEPS * f + 1)))
                dve.wait_ge(*tiles.used(1, b, use))
                if reuse:
                    dve.wait_ge(*tiles.used(2, b, use - 1))
                v.tensor_tensor(act_whole[:, b, :], prob[:, b, :], ps[6 + b], ALU.mult
                                ).then_inc(act_ready.sem, 1)
                dve.wait_ge(*tiles.act(i, 1))
                v.tensor_copy(act_high[:, b, :], act_whole[:, b, :]).then_inc(act_ready.sem, 1)
                dve.wait_ge(*tiles.act(i, 2))
                v.tensor_tensor(act_low[:, b, :], act_whole[:, b, :], act_high[:, b, :], ALU.subtract
                                ).then_inc(act_ready.sem, 1)

            w_low_of(1, 0, 1, 1)
            w_low_of(0, 1, 2, 0)
            times_up(0, 0, 0, False)
            w_low_of(1, 1, 3, 1)
            w_low_of(2, 0, 4, 0)
            w_low_of(0, 0, 5, 1)
            times_up(1, 1, 0, False)
            w_low_of(1, 0, 6, 0)
            w_low_of(2, 1, 7, 1)
            with dve.Fori(1, FFN_STEPS // 2) as j:
                w_low_of(0, 1, j * 6 + 2, 0)
                times_up(j * 2, 0, j, True)
                w_low_of(1, 1, j * 6 + 3, 1)
                w_low_of(2, 0, j * 6 + 4, 0)
                w_low_of(0, 0, j * 6 + 5, 1)
                times_up(j * 2 + 1, 1, j, True)
                w_low_of(1, 0, j * 6 + 6, 0)
                w_low_of(2, 1, j * 6 + 7, 1)
            w_low_of(2, 0, FFN_TILES - 1, 0)
            times_up(FFN_STEPS - 1, 0, FFN_STEPS // 2, True)
            w_low_ready.n += FFN_TILES
            act_ready.n += 3 * FFN_STEPS
            residual(l, None, [tiles.n0 + FFN_TILES - 1], 0.5)

        def step(l, instruction, signal=None):
            signal = signal or dve_step
            instruction.then_inc(*signal.up())
            dve.wait_ge(*signal.now(l))

        def shift(l, n, j):
            dst, at = {6: (low, 0), 2: (k_t, 0), 3: (k_t, 2), 4: (v_t, 0), 5: (v_t, 2),
                       0: (r_t, 0), 1: (r_t, 2)}[j]
            dve.wait_ge(*mix_evac.at(l, n + 1))
            b = raw[:, n % 2]
            step(l, v.tensor_tensor(dif[:, :, :], b[:, :, 0:T], b[:, :, 1:T + 1], ALU.subtract), mixed)
            for m in range(2):
                step(l, v.scalar_tensor_tensor(dst[:, at + m, :], dif[:, m, :], pcol("rwkv_mu", 2 * j + m),
                                               b[:, m, 1:T + 1], ALU.mult, ALU.add), mixed)

        def softmax(l, heads, base, scale, widths, evac):
            for h in range(heads + 3):
                if h < heads:
                    e, g = h % 4, base + h
                    dve.wait_ge(*sc_done.at(l, g + 1))
                    at = 0
                    for t, w in enumerate(widths):
                        v.tensor_reduce(smx[:, e, t:t + 1], ps[SCORE_BANKS[e]][:, at:at + w], AX_X, ALU.max
                                        ).then_inc(*sm_max.up())
                        at += w
                    dve.wait_ge(*sm_max.now(l))
                    v.tensor_scalar(smx[:, e, :], smx[:, e, :], -scale, None, ALU.mult).then_inc(*sm_max.up())
                if 1 <= h <= heads:
                    e, g = (h - 1) % 4, base + h - 1
                    dve.wait_ge(*sm_act.at(l, 2 * (g + 1)))
                    step(l, v.reciprocal(ssum[:, e, :], ssum[:, e, :]), sm_norm)
                    at = 0
                    for t, w in enumerate(widths):
                        v.tensor_scalar(prob[:, e, at:at + w], prob[:, e, at:at + w],
                                        ssum[:, e, t:t + 1], None, ALU.mult).then_inc(*sm_norm.up())
                        at += w
                if h >= 3:
                    evac(h - 3)

        def moba_out(l):
            def evac(h):
                if h % 2:
                    dve.wait_ge(*av_done.at(l, h + 1))
                    step(l, v.tensor_copy(cat[:, NPAIR + h // 2, :], ps[6 + (h // 2) % 2][:, 0:T]), av_out)
            return evac

        def cross_out(l):
            def evac(h):
                dve.wait_ge(*av_done.at(l, NH + h + 1))
                step(l, v.tensor_copy(h_sb[:, 2 * h:2 * h + 2, :],
                                      ps[6 + h % 2].rearrange("p (m t) -> p m t", m=2)), av_out)
            return evac

        def by_slot(ap, e):
            return ap[:, e * NPAIR:(e + 1) * NPAIR, :]

        def bank4(b):
            return ps[b].rearrange("p (s t) -> p s t", s=NPAIR)

        def mask(name):
            return cst[name].rearrange("p (o t) -> p o t", o=1).to_broadcast([P, NPAIR, P])

        def solver(l, c):
            def need(n):
                dve.wait_ge(*sol_done.at(l, SOLVE_PE * c + n))

            def take(n, instruction):
                step(l, instruction(), sol_step)

            def masked(n, dst, e, bank, name):
                need(n)
                step(l, v.tensor_tensor(by_slot(dst, e), bank4(bank), mask(name), ALU.mult), sol_step)

            def copy(n, dst, bank):
                need(n)
                step(l, v.tensor_copy(dst, bank4(bank)), sol_step)

            def add(n, dst, bank, more):
                need(n)
                step(l, v.tensor_tensor(dst, bank4(bank), more, ALU.add), sol_step)

            dve.wait_ge(*tok_done.at(l, 4 * c + 1))
            step(l, v.tensor_copy(rhs[:, :, 0:HD].rearrange("p (e m) d -> p m e d", e=2),
                                  ps[0].rearrange("p (m e d) -> p m e d", m=NPAIR, e=2)), sol_step)
            for e in range(2):
                masked(1 + e, m_up, e, 4 + e, "upper")
            for e in range(2):
                masked(3 + e, l_up, e, 6 + e, "upper_sub")
            for e in range(2):
                masked(5 + e, l_lo, e, 4 + e, "lower_sub")
                masked(5 + e, rhs[:, :, P:2 * P], e, 4 + e, "lower_off")
            for e in range(2):
                masked(7 + e, nb_up, e, 6 + e, "upper_incl")
            for e in range(2):
                masked(9 + e, nk_up, e, 4 + e, "upper_incl")
            need(11)
            step(l, v.tensor_copy(rhs[:, :, HD:P], ps[0].rearrange("p (s d) -> p s d", s=NH)), sol_step)
            for e in range(2):
                step(l, v.tensor_tensor(by_slot(d_up, e), by_slot(l_up, e), mask("ident"), ALU.add),
                     sol_step)
            for e in range(2):
                copy(13 + 2 * e, by_slot(l_lo, e), 6 + e)
                copy(13 + 2 * e, by_slot(l_up, e), 2 + e)
            for e in range(2):
                add(18 + 3 * e, by_slot(d_up, e), 2 + e, by_slot(d_up, e))
                copy(18 + 3 * e, by_slot(l_lo, e), 4 + e)
                copy(18 + 3 * e, by_slot(l_up, e), 6 + e)
            for e in range(2):
                add(23 + 2 * e, by_slot(d_up, e), 6 + e, by_slot(d_up, e))
                copy(23 + 2 * e, by_slot(l_lo, e), 4 + e)
            for e in range(2):
                add(26 + e, by_slot(d_up, e), 2 + e, by_slot(d_up, e))
            for e in range(2):
                need(28 + e)
                step(l, v.tensor_copy(by_slot(rhs, e), psum[:, 4 + 2 * e:6 + 2 * e, :].rearrange(
                    "p b (s t) -> p (b s) t", s=2)), sol_step)
            for e in range(2):
                copy(30 + e, by_slot(l_up, e), 0 + e)
            for e in range(2):
                add(32 + e, by_slot(d_up, e), 2 + e, by_slot(rhs, e)[:, :, 0:P])
            for e in range(2):
                add(34 + e, by_slot(d_up, e), 0 + e, by_slot(rhs, e)[:, :, 0:P])
            for e in range(2):
                need(36 + e)
                for col, dst in ((0, ecol), (HD, fcol)):
                    step(l, v.tensor_tensor(
                        dst.rearrange("p (m e d) -> p m e d", m=NPAIR, e=2)[:, :, e, :],
                        bank4(2 + e)[:, :, col:col + HD], by_slot(rhs, e)[:, :, col:col + HD], ALU.add),
                        sol_step)
            copy(38, e_row, 4)

        def recurrence(l, c):
            for q in range(2):
                tb, base = slice(q * CH, (q + 1) * CH), SEQ_PE * c + 3 * q
                head = lambda ap, e: ap[tb, :].rearrange("p (m e d) -> p m e d", m=NPAIR, e=2)[:, :, e, :]
                for e in range(2):
                    dve.wait_ge(*seq_done.at(l, base + e + 1))
                    step(l, v.tensor_tensor(head(u_tok, e), ps[e][tb, 0:NPAIR * HD].rearrange(
                        "p (m d) -> p m d", m=NPAIR), head(fcol, e), ALU.add), seq_step)
                dve.wait_ge(*seq_done.at(l, base + 3))
                step(l, v.tensor_tensor(state[:, :, :], ps[2][:, 0:NPAIR * HD].rearrange(
                    "p (m d) -> p m d", m=NPAIR), state[:, :, :], ALU.add), seq_step)
                step(l, v.tensor_tensor(state[:, :, :], state[:, :, :],
                                        pend[:, :, 2 * c + q:2 * c + q + 1].to_broadcast([P, NPAIR, HD]),
                                        ALU.mult), seq_step)

        with dve.Fori(0, DEPTH) as l:
            step(l, v.tensor_copy(par_cur[:, :], par[:, bass.ds(l, 1), :].rearrange("p o n -> p (o n)")),
                 par_ready)
            norm(l, 0, "ffn1_norm_g")
            ffn(l, 0)
            norm(l, 1, "mix_norm_g")
            step(l, v.memset(raw_buf[:, :], 0.0), mixed)
            for n, j in enumerate(MIX_ORDER[:7]):
                shift(l, n, j)
                if n == 3:
                    dve.wait_ge(*gates.at(l, 4))
                    for m in range(NPAIR):
                        step(l, v.tensor_tensor_scan(cum[:, m, :], cst["carry"], sgt[:, m, :], 0.0,
                                                     ALU.mult, ALU.add))
                    step(l, v.tensor_tensor(e3[:, :, :], cum[:, :, :], sgt[:, :, :], ALU.subtract))
                if n == 4:
                    for m in range(NPAIR):
                        step(l, v.tensor_scalar(kk_t[:, m, :], k_t[:, m, :], pcol("rwkv_k_k", m), None,
                                                ALU.mult))
                    dve.wait_ge(*gates.at(l, 8))
                    for m in range(NPAIR):
                        step(l, v.tensor_scalar(tmp[:, m, :], a_t[:, m, :], 1.0, pcol("rwkv_k_a", m),
                                                ALU.subtract, ALU.mult))
                    step(l, v.scalar_tensor_tensor(k_t, tmp, 1.0, k_t, ALU.add, ALU.mult))
            dve.wait_ge(*act_step.at(l, ACT_KK_STD))
            step(l, v.tensor_scalar(sgt[:, :, :], sgt[:, :, :], 1e-12, None, ALU.max))
            step(l, v.reciprocal(sgt[:, :, :], sgt[:, :, :]))
            step(l, v.tensor_tensor(kk_t, kk_t, sgt[:, :, :], ALU.mult))
            step(l, v.tensor_tensor(a_t, kk_t, a_t, ALU.mult))
            step(l, v.tensor_tensor(a_t, a_t, e2[:, :, :], ALU.mult))
            step(l, v.scalar_tensor_tensor(e3[:, :, :], kk_t, -1.0, e3[:, :, :], ALU.mult, ALU.mult))
            for m in range(NPAIR):
                step(l, v.scalar_tensor_tensor(tmp[:, m, :], r_t[:, m, :], pcol("rwkv_r_k", m),
                                               k_t[:, m, :], ALU.mult, ALU.mult))
            step(l, v.tensor_tensor(k_t, k_t, e2[:, :, :], ALU.mult))
            step(l, v.tensor_tensor(r_t, r_t, e1[:, :, :], ALU.mult))
            dve.wait_ge(*hs_done.at(l, 2))
            for i in range(2):
                step(l, v.tensor_tensor(cum[:, 2 * i:2 * i + 2, :], ps[i].rearrange(
                    "p (m t) -> p m t", m=2), v_t[:, 2 * i:2 * i + 2, :], ALU.mult))
            step(l, v.tensor_copy(pend[:, :, :], e1[:, :, CH - 1::CH]))
            step(l, v.memset(state[:, :, :], 0.0), seq_step)
            softmax(l, NH, 0, 1.0, (T, P), moba_out(l))
            for c in range(2):
                solver(l, c)
                recurrence(l, c)
            dve.wait_ge(*y_out.at(l, 4))
            dve.wait_ge(*hs_done.at(l, 3))
            for i in range(2):
                y = cat[:, 2 * i:2 * i + 2, :]
                step(l, v.scalar_tensor_tensor(y, ps[i].rearrange("p (m t) -> p m t", m=2), -1.0 / HD, y,
                                               ALU.mult, ALU.add))
            y = cat[:, 0:NPAIR, :]
            dve.wait_ge(*act_step.at(l, ACT_LN_STD))
            step(l, v.reciprocal(sgt[:, :, :], sgt[:, :, :]))
            step(l, v.tensor_tensor(y, y, sgt[:, :, :], ALU.mult))
            for m in range(NPAIR):
                step(l, v.tensor_scalar(cat[:, m, :], cat[:, m, :], pcol("rwkv_ln_g", m),
                                        pcol("rwkv_ln_b", m), ALU.mult, ALU.add))
            step(l, v.tensor_tensor(y, y, cum[:, :, :], ALU.add))
            step(l, v.tensor_tensor(y, y, gat[:, :, :], ALU.mult))
            residual(l, 1, [FIRST_AT[("mix_out", j)] for j in range(LIN_TILES)], 1.0)
            norm(l, 2, "xattn_norm_g")
            softmax(l, XH, NH, XD ** -0.5, (T, T), cross_out(l))
            residual(l, 2, [FIRST_AT[("xo", j)] for j in range(LIN_TILES)], 1.0)
            norm(l, 3, "ffn2_norm_g")
            ffn(l, 1)


    with nc.Block() as block:
        loaded = Signal(ctx, nc, "inputs_loaded")
        const_loaded = Signal(ctx, nc, "const_loaded")
        relb_loaded = Signal(ctx, nc, "relb_loaded")
        turned = Signal(ctx, nc, "inputs_turned")
        placed = Signal(ctx, nc, "inputs_placed")
        mem_sq = Signal(ctx, nc, "mem_squares")
        mem_norm = Signal(ctx, nc, "mem_normalised")
        bias_row = Signal(ctx, nc, "bias_row")
        bias_stored = Signal(ctx, nc, "bias_stored")
        x_tok = h_sb[:, :, :].rearrange("p (h a) t -> p h (a t)", h=2)
        m_tok = cat[:, :, :].rearrange("p (h a) t -> p h (a t)", h=2)
        p_rows = rk[:, 0:2, :].rearrange("p a t -> p (a t)")
        onehot, relb, rows = va[:, 0:2, :].rearrange("p a t -> p (a t)"), std[0:33, 0:NH], kt[0:NH, 0:2, :].rearrange("p a t -> p (a t)")
        n_loads = 0

        @block.sync
        def _(sp):
            sp.dma_start(cst["all"], w_dram["consts"]).then_inc(const_loaded.sem, 16)
            sp.dma_start(x_tok, w_dram["x"].rearrange("o (h p) n -> p (o h) n", p=P)).then_inc(loaded.sem, 16)
            sp.dma_start(m_tok, w_dram["mem"].rearrange("o (h p) n -> p (o h) n", p=P)).then_inc(loaded.sem, 16)
            sp.dma_start(onehot[0:33, :], w_dram["onehot"]).then_inc(loaded.sem, 16)
            sp.wait_ge(*bias_row.at(0, 1))
            sp.dma_start(scratch["bias"], rows).then_inc(bias_stored.sem, 16)
            sp.wait_ge(bias_stored.sem, 16)
            src = scratch["bias"]
            sp.dma_start(hank[:, :, :], bass.AP(src.tensor, 0, [[1, P], [2 * T, NH], [1, T]])
                         ).then_inc(bias_stored.sem, 16)
            sp.wait_ge(bias_stored.sem, 32)

        @block.gpsimd
        def _(pool):
            for n, signal in enumerate([started, x_ready, lora_done] + w_used):
                nc.gpsimd.memset(junk[:, n:n + 1], 0.0).then_inc(signal.sem, 1)
            nc.gpsimd.memset(std[0:33, 0:NH], BIG_NEGATIVE).then_inc(*mem_norm.up())
            pool.wait_ge(*mem_norm.at(0, 1))
            pool.dma_start(relb[0:32, :], w_dram["rel_bias"].rearrange("h b -> b h"),
                           allow_slow_non_contiguous=True).then_inc(relb_loaded.sem, 16)

        @block.scalar
        def _(act):
            for name, n in PARAMS:
                r = w_dram[name]
                if len(r.shape) == 3:
                    r = r.rearrange("l h d -> l (h d)")
                c = PARAM_AT[name]
                act.dma_start(p_rows[c:c + n, 0:DEPTH * P].rearrange("c (l p) -> c l p", l=DEPTH),
                              r.rearrange("l (c p) -> c l p", p=P)).then_inc(loaded.sem, 16)
            act.dma_start(p_rows[NPAR:NPAR + KD, 0:P],
                          w_dram["final_norm_g"].rearrange("(c p) -> c p", p=P)).then_inc(loaded.sem, 16)
            for n, name in ((1, "c_ctx_2"), (2, "c_2")):
                src = w_dram[name] if len(w_dram[name].shape) == 1 else w_dram[name][0]
                act.dma_start(p_rows[NPAR + n * KD:NPAR + (n + 1) * KD, 0:P],
                              src.rearrange("(c p) -> c p", p=P)).then_inc(loaded.sem, 16)
            act.wait_ge(loaded.sem, 16 * N_INPUTS)
            act.wait_ge(*placed.at(0, 1))
            for h in range(2):
                nc.scalar.activation(probT[:, :, :].rearrange("p a n -> p (a n)"), m_tok[:, h, :],
                                     ACT.Square, accum_out=smx[:, h, 0:1]).then_inc(*mem_sq.up())
                act.wait_ge(*mem_sq.now(0))
            nc.scalar.activation(smx[:, 0:2, 1:2], smx[:, 0:2, 0:1], ACT.Sqrt, bias=eps[:, 0:1],
                                 scale=1.0 / D).then_inc(*mem_sq.up())
            act.wait_ge(*placed.at(0, 7))
            nc.scalar.activation(cond[:, :], store["final_g"][:, KD:3 * KD], SILU).then_inc(*mem_sq.up())

        @block.tensor
        def _(pe):
            pe.wait_ge(const_loaded.sem, 16)
            pe.wait_ge(loaded.sem, 16 * N_INPUTS)
            pe.wait_ge(relb_loaded.sem, 16)
            for l in range(DEPTH):
                nc.tensor.transpose(ps[0][:, l * P:l * P + NPAR], p_rows[0:NPAR, l * P:(l + 1) * P],
                                    ident[0:NPAR, 0:NPAR])
            nc.tensor.matmul(ps[1][0:NH, :], relb, onehot[0:33, :], start=True, stop=True)
            for h in range(2):
                for k in range(KD):
                    b, at = 2 + k // 2, (k % 2) * T + h * P
                    last = nc.tensor.transpose(ps[b][:, at:at + P], x_tok[:, h, k * P:(k + 1) * P], ident)
            last.then_inc(*turned.up())
            pe.wait_ge(*placed.at(0, 6))
            pe.wait_ge(*mem_norm.at(0, 4))
            for h in range(2):
                for k in range(KD):
                    b, at = 2 + k // 2, (k % 2) * T + h * P
                    last = nc.tensor.transpose(ps[b][:, at:at + P], m_tok[:, h, k * P:(k + 1) * P], ident)
            last.then_inc(*turned.up())
            nc.tensor.transpose(ps[0][:, 0:NPAR + 3 * KD], p_rows[0:NPAR + 3 * KD, 0:P],
                                ident[0:NPAR + 3 * KD, 0:NPAR + 3 * KD]).then_inc(*turned.up())

        @block.vector
        def _(dve):
            v = nc.vector
            v.memset(eps[:, 0:1], EPS)
            v.memset(eps[:, 1:2], LNX_EPS).then_inc(*placed.up())
            dve.wait_ge(*turned.at(0, 1))
            v.tensor_copy(par[:, 0:DEPTH, :], ps[0][:, 0:DEPTH * P].rearrange(
                "p (l c) -> p l c", l=DEPTH)[:, :, 0:NPAR]).then_inc(*placed.up())
            v.tensor_copy(rows, ps[1][0:NH, :]).then_inc(*bias_row.up())
            for q in range(4):
                v.tensor_copy(x_sb[:, 2 * q:2 * q + 2, :], ps[2 + q].rearrange("p (m t) -> p m t", m=2)
                              ).then_inc(*placed.up())
            dve.wait_ge(*mem_sq.at(0, 3))
            v.reciprocal(smx[:, 0:2, 1:2], smx[:, 0:2, 1:2]).then_inc(*mem_norm.up())
            dve.wait_ge(*mem_norm.at(0, 2))
            for h in range(2):
                v.tensor_scalar(m_tok[:, h, :], m_tok[:, h, :], smx[:, h, 1:2], None, ALU.mult
                                ).then_inc(*mem_norm.up())
            dve.wait_ge(*turned.at(0, 3))
            v.tensor_copy(store["final_g"], ps[0][:, NPAR:NPAR + 3 * KD]).then_inc(*placed.up())
            for q in range(4):
                v.tensor_copy(mem_sb[:, 2 * q:2 * q + 2, :], ps[2 + q].rearrange("p (m t) -> p m t", m=2)
                              ).then_inc(*placed.up())
            dve.wait_ge(*placed.now(0))
            dve.wait_ge(*mem_sq.at(0, 4))

    block = ctx.enter_context(nc.Block())

    @block.sync
    def _(sp):
        sync_program(sp)

    @block.gpsimd
    def _(pool):
        load_second_params(nc, pool, w_dram, store)
        modulation_program(pool)

    @block.tensor
    def _(pe):
        tensor_program(pe)

    @block.scalar
    def _(act):
        scalar_program(act)

    @block.vector
    def _(dve):
        vector_program(dve)

    return signals


RING2 = 8
CTX, LAT = 0, 1
TT = 2 * T
GQ, KVH = 6, 2
MH, NOPE, ROPE_D = 6, 64, 32
MQK = NOPE + ROPE_D
HID = 4 * D
MLP_STEPS = HID // BLK
MLP_TILES = 2 * MLP_STEPS
WINDOWS = (2, 4, 8, 16)
GRID_W = 64
EDGE = max(WINDOWS) // 2
IN_TILES = [(5, 1056, 256), (2, 512, 256), (3, 768, 256), (0, 0, 256), (1, 256, 256), (4, 1024, 32)]
MOD_THIRDS = 3
PIECE = 512
MOD_ROWS = 2 * MODS * P // PIECE

WHOLE = ((1, 1), (3, 1))

PARAMS2 = [("b_mod", MODS), ("g_norm1", KD), ("g_norm2", KD), ("g_cq", 2), ("g_ckv", 1), ("ls_pool", 2)]
PARAM2_AT = {}
NPAR2 = 0
for _name, _n in PARAMS2:
    PARAM2_AT[_name] = NPAR2
    NPAR2 += _n
for _name in ("g_q_gqa", "g_k_gqa", "g_q_mla", "g_k_mla"):
    PARAM2_AT[_name] = NPAR2
    NPAR2 += 1


def second_schedule():
    s = []
    for i in range(DEPTH):
        s += [("mod", i, c, t) for c in range(2) for t in range(MOD_THIRDS)]
        s += [("in", i, j) for j, _, _ in IN_TILES]
        s += [("uq", i), ("ukv", i)]
        s += [("out", i, j) for j in range(LIN_TILES)]
        for c in (CTX, LAT) if i < DEPTH - 1 else (LAT,):
            s += [(kind, i, c, n) for n in range(MLP_STEPS) for kind in ("mlp1", "mlp2")]
    return s


SECOND = second_schedule()
SECOND_AT = {name: n for n, name in enumerate(SECOND)}


def constants2():
    def rope(dim):
        n = dim // 4
        inv = (np.float32(10000.0) ** (-np.arange(n, dtype=np.float32) / np.float32(n))).astype(np.float32)
        row = np.repeat(np.arange(T // GRID_W, dtype=np.float32), GRID_W)
        col = np.tile(np.arange(GRID_W, dtype=np.float32), T // GRID_W)
        ang = np.concatenate([row[:, None] * inv, col[:, None] * inv], axis=-1)
        return np.cos(ang).T.astype(np.float32), np.sin(ang).T.astype(np.float32)

    def rotation(at, half):
        m = np.zeros((P, P), np.float32)
        for a in at:
            for i in range(half):
                m[a + half + i, a + i] = -1.0
                m[a + i, a + half + i] = 1.0
        return m

    cg, sg = rope(HD)
    cm, sm = rope(ROPE_D)
    cos_m, sin_m = np.ones((P, T), np.float32), np.zeros((P, T), np.float32)
    cos_m[NOPE:MQK], sin_m[NOPE:MQK] = np.tile(cm, (2, 1)), np.tile(sm, (2, 1))
    t = np.arange(T)
    count = [np.minimum(t + w // 2, T) - np.maximum(t - w // 2, 0) for w in WINDOWS]
    inv_count = (1.0 / np.array(count)).astype(np.float32)
    pool = np.concatenate([np.repeat(inv_count[2 * a:2 * a + 2], HD, axis=0) for a in range(2)], axis=1)
    heads = GQ + KVH
    to_rows, from_rows = np.zeros((P, 2 * heads - 2), np.float32), np.zeros((P, heads // 2 * P), np.float32)
    to_rows[:HD, heads - 2], to_rows[HD:, heads - 1] = 1.0, 1.0
    for n in range(heads):
        from_rows[n, n * HD:(n + 1) * HD] = 1.0
    return {"to_rows": to_rows, "from_rows": from_rows, "cos_g": np.tile(cg, (4, 1)), "sin_g": np.tile(sg, (4, 1)), "cos_m": cos_m, "sin_m": sin_m,
            "rot_g": rotation((0, HD), HD // 2), "rot_m": rotation((NOPE,), ROPE_D // 2),
            "pool": pool}


SECOND_RISES = {
    "second_turned": 2, "second_placed": 15, "mod_ready": 5, "x2_ready": 32, "sq2_ready": 16,
    "ss2_done": 4, "std2_ready": 4, "scaled": 36, "h2_ready": 32, "h2_low_ready": 16,
    "w2_high_ready": 64, "w2_low_ready": 64, "acc2_zero": 2, "relu_done": 32, "act2_ready": 96,
    "in_evac": 16, "nrm_act": 5, "nrm_sum": 14, "nrm_dve": 14, "rows_back": 1, "rot_done": 13,
    "mla_done": 14, "mla_evac": 16, "pool_dve": 17, "pool_done": 1, "sc2_done": 48, "sm2_max": 96,
    "sm2_norm": 96, "sm2_act": 48, "pt2_done": 48, "pt2_ready": 48, "av2_done": 48, "av2_out": 12,
    "placed_act": 5, "mla_sq": 12, "mla_std": 12, "mla_dve": 60, "one_row_ready": 2, "mod_turned":
    1
}


def build_second(nc, ctx, a, scratch, store, out):
    PER = SECOND_RISES
    signals = []

    def sb(name, shape):
        return ctx.enter_context(nc.sbuf_tensor(name, shape, F32))

    def sig(name, start=0):
        s = Signal(ctx, nc, name, PER.get(name, 0), start)
        signals.append(s)
        return s

    eps, psum = store["eps"], store["ps"]
    ps = [psum[:, i, :] for i in range(8)]
    ident, ones, head_ones = (store["cst"][n] for n in ("ident", "ones", "head_ones"))
    w = a
    wp, params_loaded = store["wp"], store["params2_loaded"]
    with ExitStack() as under:
        part = lambda name, shape: under.enter_context(nc.sbuf_tensor(name, shape, F32R))
        w_low = part("w2_low", [P, RING2, SLOT])
        h_low = part("h2_low", [P, KD, TT])
        h_high = [part(f"h2_high{s}", [P, KD, T]) for s in range(2)]
        w_high = [part(f"w2_high{b}", [P, MH * TT])[:, 0:SLOT] for b in range(2)]
        act_high = part("act2_high", [P, 2, 512])
        act_low = part("act2_low", [P, 3, TT])
    ring = sb("ring2", [P, RING2, SLOT])
    h = sb("h2_sb", [P, KD, TT])
    sqk = sb("sqk", [P, 4, TT])
    qk = sb("qk", [P, 4, TT])
    qm, km = sb("qm", [P, MH, TT]), sb("km", [P, MH, TT])
    probT = sb("probT2", [P, 2, 512])
    sqc = sb("sqc", [P, 3, TT])
    cc = sb("cc", [P, 3, TT])
    act_whole = cc
    xs = [sb("xc_sb", [P, KD, T]), store["x"]]
    n_const = sum(c.shape[1] for c in constants2().values())
    cbuf = sb("consts2_sb", [P, n_const])
    cst, _at = {}, 0
    for name, c in constants2().items():
        cst[name] = cbuf[:, _at:_at + c.shape[1]]
        _at += c.shape[1]
    par = sb("par2", [P, DEPTH, NPAR2])
    mod = sb("mod", [P, 2, MODS])
    scl = sb("scl", [P, 2, 2, KD])
    ksw = sb("ksw", [P, TT])
    vg = sb("vg", [P, 4, P])
    sqm = sb("sqm", [P, 2, TT])
    vm = sb("vm", [P, 4, MH * HD])
    pin = sb("pin", [P, 2, TT])
    std = sb("std2", [P, 2, T])
    prob = sb("prob2", [P, 4, 512])
    smx, ssum = sb("smx2", [P, 4]), sb("ssum2", [P, 4])
    csum = qm[:, :, :].rearrange("p a t -> p (a t)")[:, 0:4 * (T + 2 * EDGE + 1)].rearrange(
        "p (s t) -> p s t", s=4)
    pooled = vm[:, :, :].rearrange("p a t -> p (a t)")[:, 0:2 * TT].rearrange("p (m t) -> p m t", m=2)
    squares = [b[:, :, :].rearrange("p a (c t) -> p (a c) t", c=2) for b in (sqk, qk)]
    rot = sqc[:, 0:2, :].rearrange("p a t -> p (a t)")

    ctx_loaded, const_loaded = sig("ctx_loaded"), sig("const2_loaded")
    turned, placed = sig("second_turned"), sig("second_placed")
    w_loaded = [sig(f"v_loaded{s}") for s in range(RING2)]
    w_used = [sig(f"v_used{s}") for s in range(RING2)]
    mod_ready = sig("mod_ready")
    x_ready, sq_ready, ss_done = sig("x2_ready"), sig("sq2_ready"), sig("ss2_done")
    std_ready, scaled, h_ready = sig("std2_ready"), sig("scaled"), sig("h2_ready")
    h_low_ready = sig("h2_low_ready")
    w_high_ready, w_low_ready = sig("w2_high_ready"), sig("w2_low_ready")
    acc_zero, relu_done, act_ready = sig("acc2_zero"), sig("relu_done", 1), sig("act2_ready")
    in_evac = sig("in_evac")
    nrm_act = sig("nrm_act")
    nrm_sum = sig("nrm_sum")
    nrm_dve = sig("nrm_dve")
    rows_back = sig("rows_back")
    rot_done = sig("rot_done")
    mla_done = sig("mla_done")
    mla_evac = sig("mla_evac")
    pool_dve, pool_done = sig("pool_dve"), sig("pool_done")
    sc_done, sm_max, sm_norm, sm_act = sig("sc2_done"), sig("sm2_max"), sig("sm2_norm"), sig("sm2_act")
    pt_done, pt_ready, av_done, av_out = sig("pt2_done"), sig("pt2_ready"), sig("av2_done"), sig("av2_out")
    stored = sig("stored")

    def streams(i):
        return (CTX, LAT) if i < DEPTH - 1 else (LAT,)

    def asked(i):
        return slice(0 if i < DEPTH - 1 else T, TT)

    def cols(s, t=0, n=T):
        return slice(s * T + t, s * T + t + n)

    def pcol(i, name, n=0, rows=P):
        c = PARAM2_AT[name] + n
        return par[0:rows, i, c:c + 1]

    def place(name):
        n = SECOND_AT[name]
        return n % RING2, n // RING2

    def units(i):
        return [(s, hd, t) for s in streams(i) for hd in range(GQ + MH) for t in range(2)]

    def layer_ends(i):
        for x in signals:
            if i == 0 and not x.layer0:
                x.layer0 = x.n

    class MlpTiles:

        def __init__(self, i, c):
            self.i, self.n0, self.index = i, SECOND_AT[("mlp1", i, c, 0)], streams(i).index(c)
            self.c, self.base = c, MLP_STEPS * self.index

        def slot(self, r, q):
            return (self.n0 + 2 * q + r) % RING2

        def uses(self, r, q, j):
            return j + ((self.n0 + 2 * q + r) // RING2 + 1)

        def loaded(self, r, q, j):
            return w_loaded[self.slot(r, q)].sem, self.uses(r, q, j) * 16

        def used(self, r, q, j):
            return w_used[self.slot(r, q)].sem, self.uses(r, q, j)

        def split(self, t, signal):
            return signal.at(self.i, t + (MLP_TILES * self.index + 1))

        def act(self, step, part=3):
            return act_ready.at(self.i, 3 * step + (3 * self.base + part))

    def mlp_order(tiles, engine, tile, compute):
        groups = MLP_STEPS // 4

        def group(j, first=False, last=False):
            for q in range(4):
                here, back = (q, j), (q - 1, j) if q else (3, j - 1)
                ahead = ((q + 1) % 4, j + (q + 1) // 4)
                if not (last and q == 3):
                    tile(0, *ahead, j * 8 + (2 * q + 1), 1, (0, *here) if not (first and q == 0) else None)
                compute(j * 4 + q, j, q)
                if last and q == 3:
                    tile(1, *here, MLP_TILES - 1, 1, (0, *here))
                else:
                    tile(1, *here, j * 8 + (2 * q + 2), 0, (1, *back) if not (first and q == 0) else (0, 0, 0))

        group(0, first=True)
        with engine.Fori(1, groups - 1) as j:
            group(j)
        group(groups - 1, last=True)

    def unit_base(i):
        return len(units(0)) if i else 0

    def sync_program(sp):
        def load(name, view, src):
            s, use = place(name)
            if use:
                sp.wait_ge(w_used[s].sem, use)
            sp.dma_start(view(ring[:, s, :]), src).then_inc(w_loaded[s].sem, 16)

        def k_view(k, n):
            return lambda r: r[:, 0:k * n].rearrange("p (k n) -> p k n", k=k)

        def col_src(m, i, c, n):
            return m[i, :, c:c + n].rearrange("(k p) n -> p k n", p=P)

        for i in range(DEPTH):
            for c in range(2):
                for t in range(MOD_THIRDS):
                    load(("mod", i, c, t), lambda r: r,
                         scratch["mod"][i, :, c, t * SLOT:(t + 1) * SLOT])
            if i == 0:
                sp.dma_start(cbuf[:, :], w["consts2"]).then_inc(const_loaded.sem, 16)
            for j, c, n in IN_TILES:
                load(("in", i, j), k_view(KD, n), col_src(w["w_in_2"], i, c, n))
            load(("uq", i), k_view(2, MH * MQK), col_src(w["w_uq_2"], i, 0, MH * MQK))
            load(("ukv", i), lambda r: r[:, 0:MH * P], w["w_ukv_2"][i])
            for j in range(LIN_TILES):
                load(("out", i, j), k_view(KD, BLK), col_src(w["w_out_2"], i, j * BLK, BLK))
            for c in streams(i):
                n0 = SECOND_AT[("mlp1", i, c, 0)]
                with sp.Fori(0, MLP_STEPS // 4) as j:
                    for q in range(4):
                        for r in range(2):
                            n, at = n0 + 2 * q + r, j * (4 * BLK) + q * BLK
                            s = n % RING2
                            sp.wait_ge(w_used[s].sem, j + n // RING2)
                            if r == 0:
                                src = w["w_mlp1_2"][i, :, bass.ds(at, BLK)].rearrange("(k p) n -> p k n", p=P)
                            else:
                                src = w["w_mlp2_2"][i, bass.ds(at, BLK), :].rearrange("(k p) n -> p k n", p=P)
                            sp.dma_start(k_view(KD if r == 0 else 2, BLK if r == 0 else D)(ring[:, s, :]),
                                         src).then_inc(w_loaded[s].sem, 16)

    def tensor_program(pe):
        mm = nc.tensor.matmul

        def loaded(name):
            s, use = place(name)
            pe.wait_ge(w_loaded[s].sem, 16 * (use + 1))
            return ring[:, s, :], w_used[s]

        def norm(i, n, which):
            for s in which:
                for k in range(KD):
                    if k % 2 == 0:
                        pe.wait_ge(*sq_ready.at(i, norm_at(i, n, s) * 4 + k // 2 + 1))
                    last = mm(ps[2 + s][:, 0:T], ones, squares[s][:, k, :], start=(k == 0), stop=(k == KD - 1))
                last.then_inc(*ss_done.up())

        def split_mm(dst, w_hi, w_lo, x_hi, x_lo, start, stop, **more):
            mm(dst, w_hi, x_hi, start=start, stop=False, **more)
            mm(dst, w_hi, x_lo, start=False, stop=False, **more)
            return mm(dst, w_lo, x_hi, start=False, stop=stop, **more)

        def mlp(i, c):
            tiles = MlpTiles(i, c)

            def tile(r, q, j, t, parity, before=None):
                pe.wait_ge(*tiles.split(t, w_low_ready))
                hi, lo = (ap.rearrange("p (k n) -> p k n", k=2 if r else KD)
                          for ap in (w_high[parity], w_low[:, tiles.slot(r, q), :]))
                step = j * 4 + q
                if r == 0:
                    if not (isinstance(step, int) and step == 0):
                        pe.wait_ge(*relu_done.at(i, step + (tiles.base - 1)))
                    for m in range(2):
                        for k in range(KD):
                            if m == 0 and isinstance(step, int) and step == 0:
                                pe.wait_ge(*h_low_ready.at(i, KD * tiles.index + k + 1))
                            ms = slice(m * P, (m + 1) * P)
                            last = split_mm(ps[4 + q % 2][:, m * T:(m + 1) * T], hi[:, k, ms], lo[:, k, ms],
                                            h_high[c][:, k, :], h_low[:, k, cols(c)], k == 0, k == KD - 1)
                else:
                    if isinstance(step, int) and step == 0:
                        pe.wait_ge(*acc_zero.at(i, tiles.index + 1))
                    pe.wait_ge(*tiles.act(step))
                    for k in range(2):
                        for m in range(KD):
                            ms, ks = slice(m * P, (m + 1) * P), slice(k * T, (k + 1) * T)
                            last = split_mm(ps[m // 2][:, (m % 2) * T:(m % 2 + 1) * T], hi[:, k, ms],
                                            lo[:, k, ms], act_high[:, q % 2, ks], act_low[:, q % 2, ks],
                                            False, False, skip_group_check=True)
                last.then_inc(w_used[tiles.slot(r, q)].sem, 1)

            tile(0, 0, 0, 0, 0)
            mlp_order(tiles, pe, tile, lambda step, j, q: None)

        for k in range(KD):
            if k % 2 == 0:
                pe.wait_ge(*placed_act.at(0, k // 2 + 1))
            last = mm(ps[6][:, 0:T], ones, h[:, k, cols(LAT)], start=(k == 0), stop=(k == KD - 1))
        last.then_inc(*turned.up())
        pe.wait_ge(params_loaded.sem, 16 * N_PARAM2)
        for i in range(DEPTH):
            nc.tensor.transpose(ps[0][:, i * P:i * P + NPAR2], p_rows2[:, i * P:(i + 1) * P],
                                ident[0:NPAR2, 0:NPAR2])
        pe.wait_ge(ctx_loaded.sem, 16)
        for t in range(2):
            for k in range(KD):
                b, at = 2 + k // 2, (k % 2) * T + t * P
                last = nc.tensor.transpose(ps[b][:, at:at + P], c_tok[:, t, k * P:(k + 1) * P], ident)
        last.then_inc(*turned.up())
        pe.wait_ge(*placed.at(0, 15))

        for i in range(DEPTH):
            ub, ask = unit_base(i), asked(i)
            if i == 0:
                pe.wait_ge(*one_row_ready.at(0, 2))
            else:
                pe.wait_ge(*x_ready.at(i, 0))
            for c in range(2):
                for t in range(MOD_THIRDS):
                    r, used = loaded(("mod", i, c, t))
                    for n in range(SLOT // PIECE):
                        row = (c * MOD_THIRDS + t) * (SLOT // PIECE) + n
                        last = mm(ps[0][0:MOD_ROWS, :], one_row[:, MOD_ROWS - 1 - row:2 * MOD_ROWS - 1 - row],
                                  r[:, n * PIECE:(n + 1) * PIECE], start=(row == 0), stop=(row == MOD_ROWS - 1))
                    last.then_inc(used.sem, 1)
            pe.wait_ge(*mod_ready.at(i, 1))
            for r in range(PIECE // P):
                last = nc.tensor.transpose(ps[1][:, r * MOD_ROWS:(r + 1) * MOD_ROWS],
                                           mod_rows[:, r * P:(r + 1) * P], ident[0:MOD_ROWS, 0:MOD_ROWS])
            last.then_inc(*mod_turned.up())
            norm(i, 0, (CTX, LAT))
            pe.wait_ge(*h_ready.at(i, 2 * KD))
            if i == 0:
                pe.wait_ge(const_loaded.sem, 16)
            for n, (j, _, width) in enumerate(IN_TILES):
                r, used = loaded(("in", i, j))
                wt = r[:, 0:KD * width].rearrange("p (k n) -> p k n", k=KD)
                if n >= 2:
                    pe.wait_ge(*in_evac.at(i, 2 * (n - 1)))
                bank = 4 + 2 * (n % 2)
                if j == 2:
                    for t in range(4):
                        for k in range(KD):
                            mm(ps[bank][:, t * P:(t + 1) * P], h[:, k, t * P:(t + 1) * P], wt[:, k, 0:P],
                               start=(k == 0), stop=(k == KD - 1))
                    for k in range(KD):
                        last = mm(ps[bank + 1][:, ask], wt[:, k, P:2 * P], h[:, k, ask],
                                  start=(k == 0), stop=(k == KD - 1))
                elif j == 4:
                    for k in range(KD):
                        last = mm(ps[bank][NOPE:MQK, :], wt[:, k, :], h[:, k, :], start=(k == 0), stop=(k == KD - 1))
                else:
                    for m in range(2):
                        c = slice(0, TT) if (j, m) in WHOLE else ask
                        for k in range(KD):
                            last = mm(ps[bank + m][:, c], wt[:, k, m * P:(m + 1) * P], h[:, k, c],
                                      start=(k == 0), stop=(k == KD - 1))
                last.then_inc(used.sem, 1)
                if n == 2:
                    pe.wait_ge(*pool_dve.at(i, POOL_DVE))
                    pe.wait_ge(*mod_ready.at(i, 3))
                    for g in range(4):
                        hi = slice((g % 2) * HD, (g % 2 + 1) * HD)
                        last = mm(ps[g][hi, ask], wp[hi, g // 2, i, :], pooled[hi, g // 2, ask], start=True,
                                  stop=True)
                    last.then_inc(*pool_done.up())
                if n == 3:
                    pe.wait_ge(*nrm_act.at(i, 1))
                    pe.wait_ge(*pool_dve.at(i, POOL_DVE + 4))
                    for k in range(2):
                        mm(ps[0], ones, sqc[:, k, :], start=(k == 0), stop=(k == 1))
                    mm(ps[1], ones, sqc[:, 2, :], start=True, stop=True).then_inc(*nrm_sum.up())
            pe.wait_ge(*nrm_act.at(i, NRM_ACT_QK_SQ))
            heads = GQ + KVH
            for m in range(4):
                last = mm(ps[0][0:heads, :], cst["to_rows"][:, heads - 2 - 2 * m:2 * heads - 2 - 2 * m],
                          sqk[:, m, :], start=(m == 0), stop=(m == 3))
            last.then_inc(*nrm_sum.up())
            pe.wait_ge(*in_evac.at(i, IN_EVACS))
            pe.wait_ge(*nrm_dve.at(i, NRM_DVE_C))
            ruq, used_q = loaded(("uq", i))
            wq = ruq[:, 0:2 * MH * MQK].rearrange("p (k n) -> p k n", k=2)
            rkv, used_kv = loaded(("ukv", i))
            wkv = rkv[:, 0:MH * P].rearrange("p (m n) -> p m n", m=MH)
            for u in range(2 * MH + 2):
                if u < 2 * MH:
                    if u >= 4:
                        pe.wait_ge(*mla_evac.at(i, u - 3))
                    bank = 4 + u % 4
                    if u < MH:
                        for k in range(2):
                            last = mm(ps[bank][0:MQK, ask], wq[:, k, u * MQK:(u + 1) * MQK], cc[:, k, ask],
                                      start=(k == 0), stop=(k == 1))
                    else:
                        last = mm(ps[bank][0:NOPE, :], wkv[:, u - MH, 0:NOPE], cc[:, 2, :],
                                  start=True, stop=True)
                    last.then_inc(*((used_q.sem, 1) if u == MH - 1 else mla_done.up()))
                if u == 1:
                    pe.wait_ge(*nrm_dve.at(i, NRM_DVE_C + 1))
                    for m in range(4):
                        c = ask if m < 3 else slice(0, TT)
                        last = mm(ps[m][:, c], cst["from_rows"][0:heads, m * P:(m + 1) * P],
                                  sqk[0:heads, 0, c], start=True, stop=True)
                    last.then_inc(*rows_back.up())
                    pe.wait_ge(*nrm_dve.at(i, NRM_DVE_C + 3))
                if u == 2:
                    pe.wait_ge(*nrm_dve.at(i, NRM_DVE_QK))
                    for m in range(4):
                        last = mm(ps[2 + m // 2][:, (m % 2) * T:(m % 2 + 1) * T], cst["rot_g"],
                                  qk[:, m, cols(LAT)], start=True, stop=True)
                    last.then_inc(*rot_done.up())
                if 1 <= u <= 2 * MH:
                    b = (u - 1) % 2
                    pe.wait_ge(*mla_sq.at(i, u))
                    if u >= 3:
                        pe.wait_ge(*mla_std.at(i, u - 2))
                    c = ask if u - 1 < MH else slice(0, TT)
                    mm(ps[b][0:MQK, c], ones[0:MQK, 0:MQK], sqm[0:MQK, b, c], start=True, stop=True
                       ).then_inc(*nrm_sum.up())
                if u >= 2:
                    b = (u - 2) % 2
                    src = (qm if u - 2 < MH else km)[0:MQK, (u - 2) % MH, cols(LAT)]
                    pe.wait_ge(*nrm_dve.at(i, NRM_DVE_ROPE))
                    pe.wait_ge(*mla_dve.at(i, MLA_NORMED(u - 2)))
                    mm(ps[2 + b][0:MQK, 0:T], cst["rot_m"][0:MQK, 0:MQK], src, start=True, stop=True
                       ).then_inc(*rot_done.up())
            for t in range(4):
                pe.wait_ge(*mla_evac.at(i, 2 * MH - 3 + t))
                last = mm(ps[4 + t][:, 0:MH * HD], cc[:, 2, t * P:(t + 1) * P], wkv[:, :, NOPE:P],
                          start=True, stop=True)
                last.then_inc(*((used_kv.sem, 1) if t == 3 else mla_done.up()))
            pe.wait_ge(*mla_dve.at(i, MLA_DVE))
            pe.wait_ge(*nrm_dve.at(i, NRM_DVE))
            pe.wait_ge(*mla_evac.at(i, 2 * MH + 4))

            us = units(i)

            def scores(n):
                s, hd, t = us[n]
                nk = T if s == CTX else TT
                if n >= 4:
                    pe.wait_ge(*sm_act.at(0, ub + n - 3))
                bank = ps[SCORE_BANKS[n % 4]]
                q = cols(s, t * P, P)
                if hd < GQ:
                    hi = slice((hd % 2) * HD, (hd % 2 + 1) * HD)
                    same = hd % 2 == hd // (GQ // KVH)
                    key = qk[hi, 3, 0:nk] if same else ksw[hi, 0:nk]
                    last = mm(bank[:, 0:nk], qk[hi, hd // 2, q], key, start=True, stop=True)
                else:
                    last = mm(bank[:, 0:nk], qm[0:MQK, hd - GQ, q], km[0:MQK, hd - GQ, 0:nk],
                              start=True, stop=True)
                last.then_inc(*sc_done.up())

            def turn(n):
                s, hd, t = us[n]
                pe.wait_ge(*sm_norm.at(0, 2 * (ub + n + 1)))
                if n >= 2:
                    pe.wait_ge(*pt_ready.at(0, ub + n - 1))
                for k in range((T if s == CTX else TT) // P):
                    last = nc.tensor.transpose(ps[2 + n % 2][:, k * P:(k + 1) * P],
                                               prob[:, n % 4, k * P:(k + 1) * P], ident)
                last.then_inc(*pt_done.up())

            def attend(n):
                s, hd, t = us[n]
                pe.wait_ge(*pt_ready.at(0, ub + n + 1))
                pair = n // 4
                if n % 4 == 0 and pair >= 2:
                    pe.wait_ge(*av_out.at(0, ub // 4 + pair - 1))
                hi = slice((hd % 2) * HD, (hd % 2 + 1) * HD)
                nk = (T if s == CTX else TT) // P
                for k in range(nk):
                    kv = hd // (GQ // KVH)
                    v = vg[:, k, kv * HD:(kv + 1) * HD] if hd < GQ else vm[:, k, (hd - GQ) * HD:(hd - GQ + 1) * HD]
                    last = mm(ps[6 + pair % 2][hi, t * P:(t + 1) * P], v, probT[:, n % 2, k * P:(k + 1) * P],
                              start=(k == 0), stop=(k == nk - 1))
                last.then_inc(*av_done.up())

            for n in range(len(us) + 3):
                if n < len(us):
                    scores(n)
                if 2 <= n < len(us) + 2:
                    turn(n - 2)
                if n >= 3:
                    attend(n - 3)
            pe.wait_ge(*av_out.at(0, (ub + len(us)) // 4))
            lo = 0 if i < DEPTH - 1 else T
            mixed_out = [h[:, k, :] for k in range(KD - 2)] + [pin[:, m, :] for m in range(2)]
            for j in range(LIN_TILES):
                r, used = loaded(("out", i, j))
                wt = r.rearrange("p (k n) -> p k n", k=KD)
                if j >= 2:
                    pe.wait_ge(*x_ready.at(i, 2 * len(streams(i)) * (j - 1)))
                for m in range(2):
                    for k in range(KD):
                        last = mm(ps[4 + 2 * (j % 2) + m][:, lo:TT], wt[:, k, m * P:(m + 1) * P], mixed_out[k][:, lo:TT],
                                  start=(k == 0), stop=(k == KD - 1))
                last.then_inc(used.sem, 1)
            norm(i, 1, streams(i))
            for c in streams(i):
                mlp(i, c)
            layer_ends(i)
        pe.wait_ge(*x_ready.at(1, X_LAYER1))
        for t in range(2):
            for k in range(KD):
                last = nc.tensor.transpose(ps[4 + 2 * t + k // 4][:, (k % 4) * P:(k % 4 + 1) * P],
                                           xs[LAT][:, k, t * P:(t + 1) * P], ident)
            last.then_inc(*turned.up())

    def scalar_program(act):
        go = nc.scalar.activation

        def norm(i, n, which):
            for s in which:
                for q in range(4):
                    act.wait_ge(*x_ready.at(*x_needed(i, n, s, q)))
                    go(squares[s][:, 2 * q:2 * q + 2, :], xs[s][:, 2 * q:2 * q + 2, :], ACT.Square
                       ).then_inc(*sq_ready.up())
            if n:
                w_high_part(MlpTiles(i, which[0]), 0, 0, 0, 0)
            for s in which:
                act.wait_ge(*ss_done.at(i, norm_at(i, n, s) + 1))
                go(std[:, s, :], ps[2 + s][:, 0:T], ACT.Sqrt, bias=eps[:, 0:1], scale=1.0 / D
                   ).then_inc(*std_ready.up())
            for s in which:
                for k in range(KD):
                    act.wait_ge(*scaled.at(i, 9 * norm_at(i, n, s) + k + 2))
                    shift = mod[:, s, n * 3 * KD + k:n * 3 * KD + k + 1]
                    dst = h_high[s][:, k, :] if n else h[:, k, cols(s)]
                    go(dst, h[:, k, cols(s)], ACT.Identity, bias=shift).then_inc(*h_ready.up())
                if n and s == which[0]:
                    w_high_part(MlpTiles(i, s), 0, 1, 0, 1)

        def w_high_part(tiles, r, q, j, parity, before=None):
            act.wait_ge(*tiles.loaded(r, q, j))
            if before:
                act.wait_ge(*before)
            go(w_high[parity], ring[:, tiles.slot(r, q), :], ACT.Copy).then_inc(w_high_ready.sem, 1)

        def mlp(i, c):
            tiles = MlpTiles(i, c)

            def tile(r, q, j, t, parity, before):
                if tiles.index == 0 and isinstance(j, int) and (r, q, j) == (0, 1, 0):
                    return
                if before:
                    before = tiles.used(*before)
                elif tiles.index:
                    s, use = place(("mlp2", i, streams(i)[tiles.index - 1], MLP_STEPS - 1))
                    before = (w_used[s].sem, use + 1)
                w_high_part(tiles, r, q, j, parity, before)

            def relu(step, j, q):
                act.wait_ge(*tiles.used(0, q, j))
                if tiles.index or not isinstance(step, int) or step >= 2:
                    act.wait_ge(*tiles.act(step - 2, 1))
                go(prob[:, q % 2, :], ps[4 + q % 2], ACT.Relu).then_inc(relu_done.sem, 1)

            if tiles.index:
                s, use = place(("mlp2", i, streams(i)[tiles.index - 1], MLP_STEPS - 2))
                w_high_part(tiles, 0, 0, 0, 0, (w_used[s].sem, use + 1))
            mlp_order(tiles, act, tile, relu)
            relu_done.n += MLP_STEPS
            w_high_ready.n += MLP_TILES

        act.wait_ge(*placed.at(0, 1))
        for q in range(4):
            go(h[:, 2 * q:2 * q + 2, cols(LAT)], xs[LAT][:, 2 * q:2 * q + 2, :], ACT.Square
               ).then_inc(*placed_act.up())
        act.wait_ge(*turned.at(0, 1))
        go(std[:, LAT, :], ps[6][:, 0:T], ACT.Sqrt, bias=eps[:, 0:1], scale=1.0 / D).then_inc(*placed_act.up())
        act.wait_ge(*placed.at(0, 15))

        for i in range(DEPTH):
            ub, ask = unit_base(i), asked(i)
            norm(i, 0, (CTX, LAT))
            for n, (j, _, width) in enumerate(IN_TILES):
                s, use = place(("in", i, j))
                act.wait_ge(w_used[s].sem, use + 1)
                bank = 4 + 2 * (n % 2)
                if j == 2:
                    go(vg[:, :, :], ps[bank].rearrange("p (t n) -> p t n", t=4), ACT.Copy).then_inc(*in_evac.up())
                    go(cc[:, 0, ask], ps[bank + 1][:, ask], ACT.Copy).then_inc(*in_evac.up())
                elif j == 3:
                    for m, c in enumerate((ask, slice(0, TT))):
                        go(cc[:, 1 + m, c], ps[bank + m][:, c], ACT.Copy).then_inc(*in_evac.up())
                    act.wait_ge(*in_evac.now(0))
                    go(sqc[:, :, :], cc[:, :, :], ACT.Square).then_inc(*nrm_act.up())
                elif j in (0, 1):
                    for m in range(2):
                        c = slice(0, TT) if (j, m) in WHOLE else ask
                        go(qk[:, 2 * j + m, c], ps[bank + m][:, c], ACT.Copy).then_inc(*in_evac.up())
                elif j == 4:
                    for hd in range(MH):
                        go(km[NOPE:MQK, hd, :], ps[bank][NOPE:MQK, :], ACT.Copy).then_inc(*in_evac.up())
                else:
                    for m in range(2):
                        go(pin[:, m, ask], ps[bank + m][:, ask], ACT.Copy).then_inc(*in_evac.up())
                if n == 4:
                    act.wait_ge(*nrm_sum.at(i, 1))
                    for m, width in ((0, 2 * P), (1, P)):
                        go(sqc[:, m, :], ps[m], ACT.Sqrt, bias=eps[:, 0:1], scale=1.0 / width
                           ).then_inc(*nrm_act.up())
            act.wait_ge(*in_evac.now(0))
            go(sqk[:, :, :], qk[:, :, :], ACT.Square).then_inc(*nrm_act.up())
            act.wait_ge(*nrm_sum.at(i, 2))
            heads = GQ + KVH
            go(sqk[0:heads, 0, :], ps[0][0:heads, :], ACT.Sqrt, bias=eps[0:heads, 0:1], scale=1.0 / HD
               ).then_inc(*nrm_act.up())

            def mla_ready(u):
                if u < MH - 1:
                    act.wait_ge(*mla_done.at(i, u + 1))
                elif u == MH - 1:
                    s, use = place(("uq", i))
                    act.wait_ge(w_used[s].sem, use + 1)
                else:
                    act.wait_ge(*mla_done.at(i, u))

            for u in range(2 * MH + 1):
                if u < 2 * MH:
                    b = u % 2
                    mla_ready(u)
                    dst, rows = (qm, MQK) if u < MH else (km, NOPE)
                    c = ask if u < MH else slice(0, TT)
                    go(dst[0:rows, u % MH, c], ps[4 + u % 4][0:rows, c], ACT.Copy).then_inc(*mla_evac.up())
                    act.wait_ge(*mla_evac.now(0))
                    if u >= 2:
                        act.wait_ge(*mla_dve.at(i, MLA_NORMED(u - 2)))
                    go(sqm[0:MQK, b, c], dst[0:MQK, u % MH, c], ACT.Square).then_inc(*mla_sq.up())
                if u >= 1:
                    b = (u - 1) % 2
                    act.wait_ge(*nrm_sum.at(i, 2 + u))
                    c = ask if u - 1 < MH else slice(0, TT)
                    go(sqm[0:MQK, b, c], ps[b][0:MQK, c], ACT.Sqrt, bias=eps[0:MQK, 0:1], scale=1.0 / MQK
                       ).then_inc(*mla_std.up())
            for t in range(4):
                if t < 3:
                    act.wait_ge(*mla_done.at(i, 2 * MH - 1 + t + 1))
                else:
                    s, use = place(("ukv", i))
                    act.wait_ge(w_used[s].sem, use + 1)
                go(vm[:, t, :], ps[4 + t][:, 0:MH * HD], ACT.Copy).then_inc(*mla_evac.up())

            us = units(i)
            for n in range(len(us) + 2):
                if n < len(us):
                    s, hd, t = us[n]
                    b, nk = n % 4, T if s == CTX else TT
                    act.wait_ge(*sm_max.at(0, 2 * (ub + n + 1)))
                    if n >= 4:
                        act.wait_ge(*pt_done.at(0, ub + n - 3))
                    go(prob[:, b, 0:nk], ps[SCORE_BANKS[b]][:, 0:nk], ACT.Exp, bias=smx[:, b:b + 1],
                       scale=(HD if hd < GQ else MQK) ** -0.5, accum_out=ssum[:, b:b + 1]
                       ).then_inc(*sm_act.up())
                if n >= 2:
                    nk = T if us[n - 2][0] == CTX else TT
                    b = n % 2
                    act.wait_ge(*pt_done.at(0, ub + n - 1))
                    if n >= 4:
                        act.wait_ge(*av_done.at(0, ub + n - 3))
                    go(probT[:, b, 0:nk], ps[2 + b][:, 0:nk], ACT.Copy).then_inc(*pt_ready.up())
            norm(i, 1, streams(i))
            for c in streams(i):
                mlp(i, c)
            layer_ends(i)

    def vector_program(dve):
        v = nc.vector

        def step(i, instruction, signal):
            instruction.then_inc(*signal.up())
            dve.wait_ge(*signal.now(0))

        def norm(i, n, which):
            if n:
                w_low_part(MlpTiles(i, which[0]), 0, 0, 0, 0)
            for s in which:
                dve.wait_ge(*std_ready.at(i, norm_at(i, n, s) + 1))
                step(i, v.reciprocal(std[:, s, :], std[:, s, :]), scaled)
                for k in range(KD):
                    v.scalar_tensor_tensor(h[:, k, cols(s)], xs[s][:, k, :], scl[:, s, n, k:k + 1],
                                           std[:, s, :], ALU.mult, ALU.mult).then_inc(*scaled.up())
                if n:
                    for k in range(KD):
                        dve.wait_ge(*h_ready.at(i, 2 * KD + KD * streams(i).index(s) + k + 1))
                        v.scalar_tensor_tensor(h_low[:, k, cols(s)], h[:, k, cols(s)],
                                               mod[:, s, n * 3 * KD + k:n * 3 * KD + k + 1],
                                               h_high[s][:, k, :], ALU.add, ALU.subtract
                                               ).then_inc(*h_low_ready.up())
                    if s == which[0]:
                        w_low_part(MlpTiles(i, s), 0, 1, 1, 1)

        def w_low_part(tiles, r, q, t, parity):
            slot = tiles.slot(r, q)
            dve.wait_ge(*tiles.split(t, w_high_ready))
            v.tensor_tensor(w_low[:, slot, :], ring[:, slot, :], w_high[parity], ALU.subtract
                            ).then_inc(w_low_ready.sem, 1)

        def mlp(i, c):
            tiles = MlpTiles(i, c)

            def tile(r, q, j, t, parity, before):
                if not (tiles.index == 0 and isinstance(t, int) and t == 1):
                    w_low_part(tiles, r, q, t, parity)

            def square(step, j, q):
                if not isinstance(step, int) or step >= 2:
                    dve.wait_ge(*(tiles.used(1, q - 2, j) if q >= 2 else tiles.used(1, q + 2, j - 1)))
                dve.wait_ge(*relu_done.at(i, step + (tiles.base + 1)))
                b = q % 2
                v.tensor_tensor(act_whole[:, b, :], prob[:, b, :], prob[:, b, :], ALU.mult
                                ).then_inc(act_ready.sem, 1)
                dve.wait_ge(*tiles.act(step, 1))
                v.tensor_copy(act_high[:, b, :], act_whole[:, b, :]).then_inc(act_ready.sem, 1)
                dve.wait_ge(*tiles.act(step, 2))
                v.tensor_tensor(act_low[:, b, :], act_whole[:, b, :], act_high[:, b, :], ALU.subtract
                                ).then_inc(act_ready.sem, 1)

            if tiles.index:
                w_low_part(tiles, 0, 0, 0, 0)
            mlp_order(tiles, dve, tile, square)
            act_ready.n += 3 * MLP_STEPS
            w_low_ready.n += MLP_TILES

        step(0, v.memset(one_row[:, :], 0.0), one_row_ready)
        v.memset(one_row[:, MOD_ROWS - 1:MOD_ROWS], 1.0).then_inc(*one_row_ready.up())
        dve.wait_ge(*placed_act.at(0, 5))
        step(0, v.reciprocal(std[:, LAT, :], std[:, LAT, :]), placed)
        for k in range(KD):
            v.scalar_tensor_tensor(xs[LAT][:, k, :], xs[LAT][:, k, :], store["final_g"][:, k:k + 1],
                                   std[:, LAT, :], ALU.mult, ALU.mult).then_inc(*placed.up())
        dve.wait_ge(*turned.at(0, 2))
        v.tensor_copy(par[:, :, :], ps[0][:, 0:DEPTH * P].rearrange("p (l c) -> p l c", l=DEPTH)[:, :, 0:NPAR2]
                      ).then_inc(*placed.up())
        for q in range(4):
            v.tensor_copy(xs[CTX][:, 2 * q:2 * q + 2, :], ps[2 + q].rearrange("p (m t) -> p m t", m=2)
                          ).then_inc(*placed.up())
        dve.wait_ge(const_loaded.sem, 16)
        dve.wait_ge(*placed.now(0))

        for i in range(DEPTH):
            ub, ask = unit_base(i), asked(i)
            s_, use = place(("mod", i, 1, MOD_THIRDS - 1))
            dve.wait_ge(w_used[s_].sem, use + 1)
            bias = PARAM2_AT["b_mod"]
            step(i, v.tensor_copy(mod_rows, ps[0][0:MOD_ROWS, :]), mod_ready)
            dve.wait_ge(*mod_turned.at(i, 1))
            for c in range(2):
                v.tensor_tensor(mod[:, c, :].rearrange("p (q r) -> p q r", r=PIECE // P),
                                ps[1][:, 0:2 * MODS].rearrange("p (r c q) -> p c q r", c=2, r=PIECE // P)[:, c],
                                par[:, i, bias:bias + MODS].rearrange("p (q r) -> p q r", r=PIECE // P),
                                ALU.add).then_inc(*mod_ready.up())
            dve.wait_ge(*mod_ready.now(0))
            for n, gain in ((0, "g_norm1"), (1, "g_norm2")):
                g = PARAM2_AT[gain]
                step(i, v.scalar_tensor_tensor(
                    scl[:, :, n, :], mod[:, :, (3 * n + 1) * KD:(3 * n + 2) * KD], 1.0,
                    par[:, i, g:g + KD].rearrange("p (o n) -> p o n", o=1).to_broadcast([P, 2, KD]),
                    ALU.add, ALU.mult), mod_ready)
            norm(i, 0, (CTX, LAT))
            dve.wait_ge(*in_evac.at(i, 2))
            step(i, v.memset(csum, 0.0), pool_dve)
            first = EDGE + 1
            for m in range(2):
                for s in range(2):
                    g = 2 * m + s
                    step(i, v.tensor_tensor_scan(csum[:, g, first:first + T], ones_row, pin[:, m, cols(s)],
                                                 0.0, ALU.mult, ALU.add), pool_dve)
            step(i, v.tensor_copy(csum[:, :, first + T:], csum[:, :, first + T - 1:first + T].to_broadcast(
                [P, 4, EDGE])), pool_dve)
            for g, wd in enumerate(WINDOWS):
                hi, m = slice((g % 2) * HD, (g % 2 + 1) * HD), g // 2
                step(i, v.tensor_tensor(pooled[hi, m, :].rearrange("p (s t) -> p s t", s=2),
                                        csum[hi, 2 * m:2 * m + 2, EDGE + wd // 2:EDGE + wd // 2 + T],
                                        csum[hi, 2 * m:2 * m + 2, EDGE - wd // 2:EDGE - wd // 2 + T],
                                        ALU.subtract), pool_dve)
            for m in range(2):
                view = pooled[:, m, :].rearrange("p (s t) -> p s t", s=2)
                step(i, v.tensor_tensor(view, view, cst["pool"][:, m * T:(m + 1) * T].rearrange(
                    "p (o t) -> p o t", o=1).to_broadcast([P, 2, T]), ALU.mult), pool_dve)
            step(i, v.tensor_tensor(pooled, pooled, pin[:, :, :], ALU.subtract), pool_dve)
            dve.wait_ge(*pool_done.at(i, 1))
            for g in range(4):
                hi = slice((g % 2) * HD, (g % 2 + 1) * HD)
                step(i, v.tensor_scalar(pin[hi, g // 2, ask], ps[g][hi, ask], pcol_part(i, "ls_pool", g // 2, hi),
                                        None, ALU.mult), pool_dve)
            dve.wait_ge(*nrm_act.at(i, 3))
            step(i, v.reciprocal(sqc[:, 0:2, :], sqc[:, 0:2, :]), nrm_dve)
            for m, (name, at, r) in enumerate((("g_cq", 0, 0), ("g_cq", 1, 0), ("g_ckv", 0, 1))):
                step(i, v.scalar_tensor_tensor(cc[:, m, :], cc[:, m, :], pcol(i, name, at), sqc[:, r, :],
                                               ALU.mult, ALU.mult), nrm_dve)
            dve.wait_ge(*nrm_act.at(i, NRM_ACT_QK_STD))
            heads = GQ + KVH
            step(i, v.reciprocal(sqk[0:heads, 0, :], sqk[0:heads, 0, :]), nrm_dve)
            dve.wait_ge(*rows_back.at(i, 1))
            for m in range(4):
                c = ask if m < 3 else slice(0, TT)
                step(i, v.scalar_tensor_tensor(qk[:, m, c], qk[:, m, c],
                                               pcol(i, "g_q_gqa" if m < 3 else "g_k_gqa"), ps[m][:, c],
                                               ALU.mult, ALU.mult), nrm_dve)
            wide = lambda c: cst[c].rearrange("p (o t) -> p o t", o=1).to_broadcast([P, 4, T])
            rot4 = rot.rearrange("p (m t) -> p m t", m=4)
            dve.wait_ge(*rot_done.at(i, 1))
            step(i, v.tensor_tensor(rot4, psum[:, 2:4, :].rearrange("p b (m t) -> p (b m) t", m=2),
                                    wide("sin_g"), ALU.mult), nrm_dve)
            step(i, v.tensor_tensor(qk[:, :, cols(LAT)], qk[:, :, cols(LAT)], wide("cos_g"), ALU.mult), nrm_dve)
            step(i, v.tensor_tensor(qk[:, :, cols(LAT)], qk[:, :, cols(LAT)], rot4, ALU.add), nrm_dve)
            for e in range(2):
                step(i, v.tensor_copy(ksw[(1 - e) * HD:(2 - e) * HD, :], qk[e * HD:(e + 1) * HD, 3, :]), nrm_dve)
            for u in range(2 * MH + 1):
                if u < 2 * MH:
                    b, buf = u % 2, qm if u < MH else km
                    dve.wait_ge(*mla_std.at(i, u + 1))
                    c = ask if u < MH else slice(0, TT)
                    step(i, v.reciprocal(sqm[0:MQK, b, c], sqm[0:MQK, b, c]), mla_dve)
                    step(i, v.scalar_tensor_tensor(buf[0:MQK, u % MH, c], buf[0:MQK, u % MH, c],
                                                   pcol(i, "g_q_mla" if u < MH else "g_k_mla", rows=MQK),
                                                   sqm[0:MQK, b, c], ALU.mult, ALU.mult), mla_dve)
                if u >= 1:
                    p_, buf = u - 1, qm if u - 1 < MH else km
                    b, lat = p_ % 2, buf[0:MQK, p_ % MH, cols(LAT)]
                    dve.wait_ge(*rot_done.at(i, 2 + p_))
                    step(i, v.tensor_tensor(rotm, ps[2 + b][0:MQK, 0:T], cst["sin_m"][0:MQK, :], ALU.mult),
                         mla_dve)
                    step(i, v.tensor_tensor(lat, lat, cst["cos_m"][0:MQK, :], ALU.mult), mla_dve)
                    step(i, v.tensor_tensor(lat, lat, rotm, ALU.add), mla_dve)

            us = units(i)
            for n in range(len(us) + 3):
                if n < len(us):
                    s, hd, t = us[n]
                    nk = T if s == CTX else TT
                    dve.wait_ge(*sc_done.at(0, ub + n + 1))
                    m1 = smx[:, n % 4:n % 4 + 1]
                    step(0, v.tensor_reduce(m1, ps[SCORE_BANKS[n % 4]][:, 0:nk], AX_X, ALU.max), sm_max)
                    v.tensor_scalar(m1, m1, -((HD if hd < GQ else MQK) ** -0.5), None, ALU.mult
                                    ).then_inc(*sm_max.up())
                if 1 <= n <= len(us):
                    b = (n - 1) % 4
                    nk = T if us[n - 1][0] == CTX else TT
                    dve.wait_ge(*sm_act.at(0, ub + n))
                    step(0, v.reciprocal(ssum[:, b:b + 1], ssum[:, b:b + 1]), sm_norm)
                    v.tensor_scalar(prob[:, b, 0:nk], prob[:, b, 0:nk], ssum[:, b:b + 1], None,
                                    ALU.mult).then_inc(*sm_norm.up())
                if n >= 3 and (n - 3) % 4 == 3:
                    s, hd, t = us[n - 3]
                    pair = (n - 3) // 4
                    dve.wait_ge(*av_done.at(0, ub + n - 2))
                    v.tensor_copy(h[:, hd // 2, cols(s)], ps[6 + pair % 2][:, 0:T]).then_inc(*av_out.up())
            for j in range(LIN_TILES):
                sl, use = place(("out", i, j))
                dve.wait_ge(w_used[sl].sem, use + 1)
                for m in range(2):
                    f = 2 * j + m
                    for s in streams(i):
                        v.scalar_tensor_tensor(xs[s][:, f, :], ps[4 + 2 * (j % 2) + m][:, cols(s)],
                                               mod[:, s, 2 * KD + f:2 * KD + f + 1], xs[s][:, f, :],
                                               ALU.mult, ALU.add).then_inc(*x_ready.up())
            dve.wait_ge(*x_ready.now(0))
            norm(i, 1, streams(i))
            for c in streams(i):
                if i or streams(i).index(c):
                    dve.wait_ge(*x_ready.now(0))
                v.memset(psum[:, 0:4, :], 0.0).then_inc(*acc_zero.up())

                mlp(i, c)
                sl, use = place(("mlp2", i, c, MLP_STEPS - 1))
                dve.wait_ge(w_used[sl].sem, use + 1)
                for f in range(KD):
                    v.scalar_tensor_tensor(xs[c][:, f, :], ps[f // 2][:, (f % 2) * T:(f % 2 + 1) * T],
                                           mod[:, c, 5 * KD + f:5 * KD + f + 1], xs[c][:, f, :],
                                           ALU.mult, ALU.add).then_inc(*x_ready.up())
                dve.wait_ge(*x_ready.now(0))
            layer_ends(i)
        for t in range(2):
            dve.wait_ge(*turned.at(0, 3 + t))
            v.tensor_copy(o_tok[:, t, :], psum[:, 4 + 2 * t:6 + 2 * t, :].rearrange("p b n -> p (b n)")
                          ).then_inc(*placed.up())

    NRM_ACT_QK_SQ, NRM_ACT_QK_STD = 4, 5
    NRM_DVE_C, NRM_DVE_QK, NRM_DVE_ROPE, NRM_DVE = 4, 9, 10, 14
    IN_EVACS = 2 + 2 + 2 + 2 + MH + 2
    POOL_DVE = 1 + 4 + 1 + 4 + 2 + 1
    MLA_DVE = 2 * MH * 5
    X_LAYER1 = 2 * KD
    N_PARAM2 = len(PARAMS2) + 6 + 2 * DEPTH

    def MLA_NORMED(u):
        return 2 * (u + 1) + 3 * max(u - 1, 0)

    def norm_at(i, n, s):
        return s if n == 0 else 2 + streams(i).index(s)

    def x_needed(i, n, s, q):
        if n == 1:
            return i, 2 * len(streams(i)) * (q + 1)
        return (0, 0) if i == 0 else (0, 2 * KD + s * KD + 2 * (q + 1))

    placed_act = sig("placed_act")
    mla_sq, mla_std, mla_dve = sig("mla_sq"), sig("mla_std"), sig("mla_dve")
    p_rows2 = store["rows2"][0:NPAR2, :]
    c_tok = sqk[:, :, :].rearrange("p (h a) t -> p h (a t)", h=2)
    o_tok = sqk[:, :, :].rearrange("p (h a) t -> p h (a t)", h=2)
    mod_rows = sqm[0:MOD_ROWS, 0, :]
    one_row = sb("one_row", [P, 2 * MOD_ROWS - 1])
    one_row_ready, mod_turned = sig("one_row_ready"), sig("mod_turned")
    rotm = probT[0:MQK, 0, 0:T]
    ones_row = sb("ones_row", [P, T])[:, :]

    def pcol_part(i, name, n, hi):
        c = PARAM2_AT[name] + n
        return par[hi, i, c:c + 1]

    block = ctx.enter_context(nc.Block())

    @block.sync
    def _(sp):
        sp.dma_start(c_tok, w["ctx_2"].rearrange("o (h p) n -> p (o h) n", p=P)).then_inc(ctx_loaded.sem, 16)
        sync_program(sp)
        for t in range(2):
            sp.wait_ge(*placed.at(0, 15 + t + 1))
            sp.dma_start(out[0, t * P:(t + 1) * P, :], o_tok[:, t, :]).then_inc(stored.sem, 16)
        sp.wait_ge(stored.sem, 32)

    @block.tensor
    def _(pe):
        tensor_program(pe)

    @block.scalar
    def _(act):
        scalar_program(act)

    @block.vector
    def _(dve):
        nc.vector.memset(ones_row[:, 0:P], 1.0).then_inc(*placed.up())
        nc.vector.memset(ones_row[:, P:], 1.0).then_inc(relu_done.sem, 1)
        vector_program(dve)

    return signals


INPUTS = [
    "x", "mem", "rel_bias", "final_norm_g", "ffn1_norm_g", "ffn1_w_in", "ffn1_w_out", "mix_norm_g",
    "w_mix_in", "w_mix_out", "rwkv_mu", "rwkv_w0", "rwkv_w_up", "rwkv_a0", "rwkv_a_up",
    "rwkv_g_up", "rwkv_k_k", "rwkv_k_a", "rwkv_r_k", "rwkv_ln_g", "rwkv_ln_b", "xattn_norm_g",
    "mem_norm_g", "xattn_w_q", "xattn_w_kv", "xattn_w_o", "ffn2_norm_g", "ffn2_w_in", "ffn2_w_out",
    "c_2", "ctx_2", "c_ctx_2", "w_mod_2", "b_mod_2", "g_norm1_2", "g_norm2_2", "w_in_2",
    "g_q_gqa_2", "g_k_gqa_2", "g_cq_2", "g_ckv_2", "w_uq_2", "w_ukv_2", "g_q_mla_2", "g_k_mla_2",
    "w_pool_2", "ls_pool_2", "w_out_2", "w_mlp1_2", "w_mlp2_2"
]


def kernel(**inputs):
    import concourse.bacc as bacc
    from concourse.bass_utils import run_bass_kernel_spmd

    nc = bacc.Bacc("TRN2", target_bir_lowering=False, num_devices=1)
    arrays = {name: np.ascontiguousarray(inputs[name]) for name in INPUTS}
    arrays["consts"] = np.concatenate(list(constants().values()), axis=1)
    arrays["consts2"] = np.concatenate(list(constants2().values()), axis=1)
    arrays["onehot"] = rel_bucket_onehot()
    dram = {name: nc.dram_tensor(f"in_{name}", array.shape, F32, kind="ExternalInput").ap()
            for name, array in arrays.items()}
    out = nc.dram_tensor("out", (1, T, D), F32, kind="ExternalOutput").ap()
    program(nc, dram, out)
    result = run_bass_kernel_spmd(nc, [{f"in_{name}": array for name, array in arrays.items()}],
                                  core_ids=[0])
    return result.results[0]["out"]
```
